# Optimizing a Trainium2 kernel written in Bass

```python
import math
import jax, jax.numpy as jnp
from jax import lax
import numpy as np

D_MODEL = 1024
BATCH = 1
SEQ = 2048
DEPTH = 1
DEC_BATCH = 8
DEC_SEQ = 8
PAST_LEN = 16384
PAGE_SIZE = 128

MIX_WIDTH = D_MODEL
POOL_WIDTH = MIX_WIDTH // 2
SSM_WIDTH = MIX_WIDTH - POOL_WIDTH
POOL_WINDOWS = (2, 4, 8, 16)
N_POOL_GROUPS = len(POOL_WINDOWS)
POOL_GROUP = POOL_WIDTH // N_POOL_GROUPS
POOL_BUF = max(POOL_WINDOWS) - 1
SSM_GROUP = 16
N_SSM_GROUPS = SSM_WIDTH // SSM_GROUP
SSM_STATE = 64
DT_MIN = 1e-3
DT_MAX = 1e-1
N_EXPERT_GROUPS = 4
EXPERTS_PER_GROUP = 4
N_EXPERTS = N_EXPERT_GROUPS * EXPERTS_PER_GROUP
EXPERT_TOP_K = 2
EXPERT_HIDDEN = 256
N_MOD = 6
EPS = 1e-6

kernel_name = 'hybrid_pool_s5_hmoe_adaln_step'

def rmsnorm(x, g):
    xf = x.astype(jnp.float32)
    y = xf * lax.rsqrt(jnp.mean(xf * xf, axis=-1, keepdims=True) + EPS)
    return (y * g.astype(jnp.float32)).astype(x.dtype)

def modulate(h, shift, scale):
    return h * (1 + scale[:, None, :]) + shift[:, None, :]

def pool_mixer(u, buf, start_pos, pool_w, pool_scale):
    n, L, _ = u.shape
    uf = u.astype(jnp.float32)
    z = jnp.concatenate([buf.astype(jnp.float32), uf], axis=1)
    cs = jnp.concatenate([jnp.zeros((n, 1, POOL_WIDTH), jnp.float32), jnp.cumsum(z, axis=1)], axis=1)
    end = cs[:, POOL_BUF + 1:]
    pos = start_pos + jnp.arange(L)
    outs = []
    for k, w in enumerate(POOL_WINDOWS):
        sl = slice(k * POOL_GROUP, (k + 1) * POOL_GROUP)
        start = cs[:, POOL_BUF + 1 - w:POOL_BUF + 1 - w + L, sl]
        cnt = jnp.minimum(w, pos + 1).astype(jnp.float32)[None, :, None]
        outs.append((end[..., sl] - start) / cnt - uf[..., sl])
    pooled = jnp.stack(outs, axis=2)
    mixed = jnp.einsum('nlgc,gcd->nlgd', pooled, pool_w.astype(jnp.float32)).reshape(n, L, POOL_WIDTH)
    return mixed * pool_scale.astype(jnp.float32), z[:, -POOL_BUF:]

def complex_affine_combine(e1, e2):
    a1r, a1i, b1r, b1i = e1
    a2r, a2i, b2r, b2i = e2
    return (a2r * a1r - a2i * a1i,
            a2r * a1i + a2i * a1r,
            a2r * b1r - a2i * b1i + b2r,
            a2r * b1i + a2i * b1r + b2i)

def ssm_mixer(u, h0_re, h0_im, a_re, a_im, log_dt, b_re, b_im, c_re, c_im, d, glu_w, glu_b):
    f32 = jnp.float32
    n, L, _ = u.shape
    uf = u.astype(f32).reshape(n, L, N_SSM_GROUPS, SSM_GROUP)
    a_re = a_re.astype(f32)
    a_im = a_im.astype(f32)
    dt = jnp.exp(log_dt.astype(f32))[:, None]
    mag = jnp.exp(a_re * dt)
    lb_re = mag * jnp.cos(a_im * dt)
    lb_im = mag * jnp.sin(a_im * dt)
    den = a_re * a_re + a_im * a_im
    nr = lb_re - 1.0
    ni = lb_im
    k_re = (nr * a_re + ni * a_im) / den
    k_im = (ni * a_re - nr * a_im) / den
    b_re = b_re.astype(f32)
    b_im = b_im.astype(f32)
    bb_re = k_re[..., None] * b_re - k_im[..., None] * b_im
    bb_im = k_re[..., None] * b_im + k_im[..., None] * b_re
    bu_re = jnp.einsum('nlgh,gph->nlgp', uf, bb_re)
    bu_im = jnp.einsum('nlgh,gph->nlgp', uf, bb_im)
    h0_re = h0_re.astype(f32)
    h0_im = h0_im.astype(f32)
    bu_re = bu_re.at[:, 0].add(lb_re * h0_re - lb_im * h0_im)
    bu_im = bu_im.at[:, 0].add(lb_re * h0_im + lb_im * h0_re)
    ar = jnp.broadcast_to(lb_re, bu_re.shape)
    ai = jnp.broadcast_to(lb_im, bu_im.shape)
    _, _, h_re, h_im = lax.associative_scan(complex_affine_combine, (ar, ai, bu_re, bu_im), axis=1)
    y = (jnp.einsum('nlgp,ghp->nlgh', h_re, c_re.astype(f32))
         - jnp.einsum('nlgp,ghp->nlgh', h_im, c_im.astype(f32))
         + d.astype(f32) * uf).reshape(n, L, SSM_WIDTH)
    g = jax.nn.gelu(y)
    out = g * jax.nn.sigmoid(g @ glu_w.astype(f32) + glu_b.astype(f32))
    return out, h_re[:, -1], h_im[:, -1]

def hier_moe(h, rw1, rb1, rw2, rb2, w_gate, w_up, w_down):
    n, L, D = h.shape
    t = h.reshape(n * L, D)
    lg1 = (t @ rw1 + rb1).astype(jnp.float32)
    p1 = jax.nn.softmax(lg1, axis=-1)
    p_top, g_idx = lax.top_k(p1, 1)
    lg2 = (jnp.einsum('td,gde->tge', t, rw2) + rb2).astype(jnp.float32)
    lg2_sel = jnp.einsum('tge,tg->te', lg2, jax.nn.one_hot(g_idx[:, 0], N_EXPERT_GROUPS, dtype=jnp.float32))
    v2, e_idx = lax.top_k(lg2_sel, EXPERT_TOP_K)
    w2 = jax.nn.softmax(v2, axis=-1) * p_top
    flat = g_idx * EXPERTS_PER_GROUP + e_idx
    gates = jnp.sum(jax.nn.one_hot(flat, N_EXPERTS, dtype=jnp.float32) * w2[..., None], axis=1)
    a = jnp.einsum('td,edf->tef', t, w_gate)
    b = jnp.einsum('td,edf->tef', t, w_up)
    hid = (jax.nn.silu(a) * b * gates[:, :, None].astype(a.dtype)).astype(t.dtype)
    out = jnp.einsum('tef,efd->td', hid, w_down)
    return out.reshape(n, L, D)

def run_layer(x, c, pool_buf, h0_re, h0_im, start_pos, prm):
    mod = jax.nn.silu(c) @ prm['w_ada'] + prm['b_ada']
    sh1, sc1, g1, sh2, sc2, g2 = jnp.split(mod, N_MOD, axis=-1)
    h = modulate(rmsnorm(x, prm['norm1_g']), sh1, sc1)
    u = h @ prm['w_in']
    pool_out, new_buf = pool_mixer(u[..., :POOL_WIDTH], pool_buf, start_pos, prm['pool_w'], prm['pool_scale'])
    ssm_out, nh_re, nh_im = ssm_mixer(u[..., POOL_WIDTH:], h0_re, h0_im, prm['ssm_a_re'], prm['ssm_a_im'],
                                      prm['ssm_log_dt'], prm['ssm_b_re'], prm['ssm_b_im'], prm['ssm_c_re'],
                                      prm['ssm_c_im'], prm['ssm_d'], prm['glu_w'], prm['glu_b'])
    mix = jnp.concatenate([pool_out, ssm_out], axis=-1).astype(x.dtype) @ prm['w_out']
    x = x + g1[:, None, :] * mix
    h2 = modulate(rmsnorm(x, prm['norm2_g']), sh2, sc2)
    x = x + g2[:, None, :] * hier_moe(h2, prm['router_w1'], prm['router_b1'], prm['router_w2'], prm['router_b2'],
                                      prm['exp_w_gate'], prm['exp_w_up'], prm['exp_w_down'])
    return x, new_buf, nh_re, nh_im

def setup_inputs(seed: int = 0) -> dict:
    key = jax.random.key(seed)
    ks = iter(jax.random.split(key, 40))
    f32 = jnp.float32

    def nrm(shape, std):
        return jax.random.normal(next(ks), shape, f32) * std

    inp = {}
    inp['x_prompt'] = nrm((BATCH, SEQ, D_MODEL), 1.0)
    inp['x_sample'] = nrm((DEC_BATCH, DEC_SEQ, D_MODEL), 1.0)
    inp['c_prompt'] = nrm((BATCH, D_MODEL), 1.0)
    inp['c_sample'] = nrm((DEC_BATCH, D_MODEL), 1.0)
    inp['state_pool'] = nrm((DEPTH, DEC_BATCH, POOL_BUF, POOL_WIDTH), 1.0)
    inp['state_ssm_re'] = nrm((DEPTH, DEC_BATCH, N_SSM_GROUPS, SSM_STATE), 0.1)
    inp['state_ssm_im'] = nrm((DEPTH, DEC_BATCH, N_SSM_GROUPS, SSM_STATE), 0.1)
    inp['w_ada'] = nrm((DEPTH, D_MODEL, N_MOD * D_MODEL), 0.5 * D_MODEL ** -0.5)
    inp['b_ada'] = nrm((DEPTH, N_MOD * D_MODEL), 0.02)
    inp['norm1_g'] = 1.0 + nrm((DEPTH, D_MODEL), 0.05)
    inp['w_in'] = nrm((DEPTH, D_MODEL, MIX_WIDTH), D_MODEL ** -0.5)
    inp['pool_w'] = nrm((DEPTH, N_POOL_GROUPS, POOL_GROUP, POOL_GROUP), POOL_GROUP ** -0.5)
    inp['pool_scale'] = 1.0 + nrm((DEPTH, POOL_WIDTH), 0.1)
    inp['ssm_a_re'] = -0.5 + nrm((DEPTH, N_SSM_GROUPS, SSM_STATE), 0.01)
    inp['ssm_a_im'] = math.pi * jnp.arange(SSM_STATE, dtype=f32) + nrm((DEPTH, N_SSM_GROUPS, SSM_STATE), 0.01)
    inp['ssm_log_dt'] = jax.random.uniform(next(ks), (DEPTH, N_SSM_GROUPS), f32, math.log(DT_MIN), math.log(DT_MAX))
    inp['ssm_b_re'] = nrm((DEPTH, N_SSM_GROUPS, SSM_STATE, SSM_GROUP), (2 * SSM_GROUP) ** -0.5)
    inp['ssm_b_im'] = nrm((DEPTH, N_SSM_GROUPS, SSM_STATE, SSM_GROUP), (2 * SSM_GROUP) ** -0.5)
    inp['ssm_c_re'] = nrm((DEPTH, N_SSM_GROUPS, SSM_GROUP, SSM_STATE), 2.0 * SSM_STATE ** -0.5)
    inp['ssm_c_im'] = nrm((DEPTH, N_SSM_GROUPS, SSM_GROUP, SSM_STATE), 2.0 * SSM_STATE ** -0.5)
    inp['ssm_d'] = nrm((DEPTH, N_SSM_GROUPS, SSM_GROUP), 1.0)
    inp['glu_w'] = nrm((DEPTH, SSM_WIDTH, SSM_WIDTH), SSM_WIDTH ** -0.5)
    inp['glu_b'] = nrm((DEPTH, SSM_WIDTH), 0.02)
    inp['w_out'] = nrm((DEPTH, MIX_WIDTH, D_MODEL), MIX_WIDTH ** -0.5)
    inp['norm2_g'] = 1.0 + nrm((DEPTH, D_MODEL), 0.05)
    inp['router_w1'] = nrm((DEPTH, D_MODEL, N_EXPERT_GROUPS), D_MODEL ** -0.5)
    inp['router_b1'] = nrm((DEPTH, N_EXPERT_GROUPS), 0.01)
    inp['router_w2'] = nrm((DEPTH, N_EXPERT_GROUPS, D_MODEL, EXPERTS_PER_GROUP), D_MODEL ** -0.5)
    inp['router_b2'] = nrm((DEPTH, N_EXPERT_GROUPS, EXPERTS_PER_GROUP), 0.01)
    inp['exp_w_gate'] = nrm((DEPTH, N_EXPERTS, D_MODEL, EXPERT_HIDDEN), D_MODEL ** -0.5)
    inp['exp_w_up'] = nrm((DEPTH, N_EXPERTS, D_MODEL, EXPERT_HIDDEN), D_MODEL ** -0.5)
    inp['exp_w_down'] = nrm((DEPTH, N_EXPERTS, EXPERT_HIDDEN, D_MODEL), EXPERT_HIDDEN ** -0.5)
    inp['final_norm_g'] = 1.0 + nrm((D_MODEL,), 0.05)
    return inp

def reference(x_prompt, x_sample, c_prompt, c_sample, state_pool, state_ssm_re, state_ssm_im,
              w_ada, b_ada, norm1_g, w_in, pool_w, pool_scale, ssm_a_re, ssm_a_im, ssm_log_dt,
              ssm_b_re, ssm_b_im, ssm_c_re, ssm_c_im, ssm_d, glu_w, glu_b, w_out, norm2_g,
              router_w1, router_b1, router_w2, router_b2, exp_w_gate, exp_w_up, exp_w_down, final_norm_g):
    nb = x_prompt.shape[0]
    xp = x_prompt
    xs = x_sample
    pool_p, pool_s, re_p, im_p, re_s, im_s = [], [], [], [], [], []
    for l in range(DEPTH):
        prm = dict(w_ada=w_ada[l], b_ada=b_ada[l], norm1_g=norm1_g[l], w_in=w_in[l], pool_w=pool_w[l],
                   pool_scale=pool_scale[l], ssm_a_re=ssm_a_re[l], ssm_a_im=ssm_a_im[l], ssm_log_dt=ssm_log_dt[l],
                   ssm_b_re=ssm_b_re[l], ssm_b_im=ssm_b_im[l], ssm_c_re=ssm_c_re[l], ssm_c_im=ssm_c_im[l],
                   ssm_d=ssm_d[l], glu_w=glu_w[l], glu_b=glu_b[l], w_out=w_out[l], norm2_g=norm2_g[l],
                   router_w1=router_w1[l], router_b1=router_b1[l], router_w2=router_w2[l], router_b2=router_b2[l],
                   exp_w_gate=exp_w_gate[l], exp_w_up=exp_w_up[l], exp_w_down=exp_w_down[l])
        zbuf = jnp.zeros((nb, POOL_BUF, POOL_WIDTH), x_prompt.dtype)
        zh = jnp.zeros((nb, N_SSM_GROUPS, SSM_STATE), jnp.float32)
        xp, bp, hrp, hip = run_layer(xp, c_prompt, zbuf, zh, zh, 0, prm)
        xs, bs, hrs, his = run_layer(xs, c_sample, state_pool[l], state_ssm_re[l], state_ssm_im[l], PAST_LEN, prm)
        pool_p.append(bp.astype(x_prompt.dtype))
        pool_s.append(bs.astype(state_pool.dtype))
        re_p.append(hrp.astype(state_ssm_re.dtype))
        im_p.append(hip.astype(state_ssm_im.dtype))
        re_s.append(hrs.astype(state_ssm_re.dtype))
        im_s.append(his.astype(state_ssm_im.dtype))
    y_prompt = rmsnorm(xp, final_norm_g)
    y_sample = rmsnorm(xs, final_norm_g)
    new_pool_prompt = jnp.stack(pool_p, axis=0)
    new_pool_sample = jnp.stack(pool_s, axis=0)
    new_ssm_re_prompt = jnp.stack(re_p, axis=0)
    new_ssm_im_prompt = jnp.stack(im_p, axis=0)
    new_ssm_re_sample = jnp.stack(re_s, axis=0)
    new_ssm_im_sample = jnp.stack(im_s, axis=0)
    return (y_prompt, y_sample, new_pool_prompt, new_pool_sample, new_ssm_re_prompt, new_ssm_im_prompt, new_ssm_re_sample, new_ssm_im_sample)


_drawn_inputs = setup_inputs


def setup_inputs(seed=0):
    import zlib

    import numpy as np

    out = dict(_drawn_inputs(seed))
    spreads = {}
    factors = {'ssm_a_re': 3.448,
     'ssm_c_re': 3.701,
     'ssm_c_im': 3.527,
     'glu_b': 8.0,
     'norm2_g': 3.169,
     'router_b1': 8.0,
     'router_b2': 8.0}
    for name, (base, spread) in spreads.items():
        noise = np.random.default_rng([zlib.crc32(name.encode()), seed]).standard_normal(out[name].shape)
        drawn = base * np.exp(spread * noise) if base else spread * noise
        out[name] = __import__('jax').numpy.asarray(drawn.astype(out[name].dtype))
    for name, factor in factors.items():
        out[name] = (out[name] * factor).astype(out[name].dtype)
    return out
```

```python
from contextlib import ExitStack

import numpy as np

import concourse.bass as bass
from concourse import mybir

F32 = mybir.dt.float32
F32R = mybir.dt.float32r
I32 = mybir.dt.int32
ALU = mybir.AluOpType
ACT = mybir.ActivationFunctionType
AX_X = mybir.AxisListType.X

P = 128
D = 1024
KD = D // P
HALF = D // 2
QH = HALF // P
TP = 2048
NSEQ = 8
LSEQ = 8
TS = NSEQ * LSEQ
TOK = TP + TS
ROWS = NSEQ + 1
BLK = 512
NBLK = TP // BLK
TPB = BLK // P
STEP = 8
NCH = TOK // STEP
PCH = TP // STEP
G = 32
GH = 16
NS = 64
PAIRS = G // 2
BUF = 15
WINDOWS = (2, 4, 8, 16)
NE = 16
EPG = 4
FH = 256
NT = (TOK + P - 1) // P
EPS = 1e-6
MAXT = (2 * TOK + NE * (P - 1)) // P // 2 * 2


class Chain:

    def __init__(self, eng, sem):
        self.eng, self.sem, self.base, self.n = eng, sem, 0, 0

    def link(self, ins):
        self.n += 1
        ins.then_inc(self.sem, 1)
        self.eng.wait_ge(self.sem, self.base + self.n)


class Core:

    def __init__(self, nc, stack):
        self.nc, self.stack, self.stage = nc, stack, "all"
        self.own = []

    def sb(self, stack, name, shape, dt=F32):
        return stack.enter_context(self.nc.sbuf_tensor(f"{self.stage}_{name}", shape, dt))

    def ps(self, stack, name, shape):
        return stack.enter_context(self.nc.psum_tensor(f"{self.stage}_{name}", shape, F32))

    def sem(self, name):
        self.own.append(self.nc.alloc_semaphore(name=name))
        return self.own[-1]

    def clear_semaphores(self):
        self.nc.clear_and_free_semaphores(self.own)
        self.nc.all_engine_barrier()
        self.own = []

    def dram(self, name, shape, dt=F32):
        return self.nc.dram_tensor(name, shape, dt).ap()


def matmul3(pe, out, l_hi, l_lo, r_hi, r_lo, start, stop):
    pe.matmul(out, l_hi, r_hi, start=start, stop=False)
    pe.matmul(out, l_lo, r_hi, start=False, stop=False)
    return pe.matmul(out, l_hi, r_lo, start=False, stop=stop)


def adaln_first(k, a, s1, w_hi, w_lo, xraw, A1, B1):
    nc = k.nc
    k.stage = "adaln_first"
    with ExitStack() as st:
        c_sb = k.sb(st, "c_sb", [ROWS, D])
        cs = k.sb(st, "cs", [ROWS, D])
        brow = k.sb(st, "brow1", [ROWS, 2 * D])
        modA = k.sb(st, "modA", [ROWS, 2 * D])
        n1col = k.sb(st, "n1col", [P, KD])
        raw = k.sb(st, "raw1", [P, 2, KD, BLK])
        psT = k.ps(st, "psT1", [P, KD * ROWS])
        psB = k.ps(st, "psB1", [P, 2, BLK])
        psC = k.ps(st, "psC1", [P, 2 * KD * ROWS])
        c_in, small_in, silu_done, ct_ps, ada_mm, ada_row, modt_ps, modt_sb, w1_hi, w1_lo, ident_ok = [
            k.sem(n) for n in ("c_in", "small_in1", "silu_done", "ct_ps", "ada_mm", "ada_row", "modt_ps",
                               "modt_sb", "w1_hi", "w1_lo", "ident_ok")]
        raw_in = [k.sem(f"raw1_in{i}") for i in range(2)]
        NA = 2 * D // BLK
        with nc.Block() as block:

            @block.sync
            def _(sp):
                sp.dma_start(c_sb[0:1, :], a["c_prompt"]).then_inc(c_in, 16)
                sp.dma_start(c_sb[1:ROWS, :], a["c_sample"]).then_inc(c_in, 16)
                sp.dma_start(brow[:], a["b_ada"][:, 0:2 * D].broadcast_to([ROWS, 2 * D])).then_inc(small_in, 16)
                sp.dma_start(n1col[:], a["norm1_g"][0].rearrange("(k p) -> p k", p=P),
                             allow_slow_non_contiguous=True).then_inc(small_in, 16)
                ada = a["w_ada"][0].rearrange("(k p) n -> p k n", p=P)
                w_in = a["w_in"][0].rearrange("(k p) n -> p k n", p=P)
                for j in range(NA + 2):
                    if 2 <= j < NA + 2:
                        sp.wait_ge(ada_mm, j - 1)
                    src = ada[:, :, j * BLK:(j + 1) * BLK] if j < NA else w_in[:, :, (j - NA) * BLK:(j - NA + 1) * BLK]
                    sp.dma_start(raw[:, j % 2], src).then_inc(raw_in[j % 2], 16)
                sp.dma_start(xraw[:], a["x_prompt"][0, 0:BLK, :].rearrange("(j p) d -> p j d", p=P)
                             ).then_inc(s1["x_in"], 16)

            @block.gpsimd
            def _(pool):
                pool.memset(k.ident[:], 0.0).then_inc(ident_ok, 1)
                pool.wait_ge(ident_ok, 1)
                pool.affine_select(out=k.ident[:], in_=k.ident[:], compare_op=ALU.not_equal, fill=1.0, base=0,
                                   pattern=[[-1, P]], channel_multiplier=1).then_inc(ident_ok, 1)

            @block.scalar
            def _(act):
                act.wait_ge(c_in, 32)
                act.activation(cs[:], c_sb[:], ACT.Silu).then_inc(silu_done, 1)
                for h in range(2):
                    act.wait_ge(raw_in[(NA + h) % 2], 16 * ((NA + h) // 2 + 1))
                    act.copy(w_hi[:, :, h * BLK:(h + 1) * BLK], raw[:, (NA + h) % 2]).then_inc(w1_hi, 1)

            @block.tensor
            def _(pe):
                pe.wait_ge(ident_ok, 2)
                pe.wait_ge(silu_done, 1)
                for t in range(KD):
                    mm = pe.transpose(psT[:, t * ROWS:(t + 1) * ROWS], cs[:, t * P:(t + 1) * P],
                                      k.ident[0:ROWS, 0:ROWS])
                mm.then_inc(ct_ps, 1)
                pe.wait_ge(s1["ct_sb"], 1)
                for j in range(NA):
                    pe.wait_ge(raw_in[j % 2], 16 * (j // 2 + 1))
                    if j >= 2:
                        pe.wait_ge(ada_row, j - 1)
                    for t in range(KD):
                        mm = pe.matmul(psB[0:ROWS, j % 2, :], k.cT[:, t, :], raw[:, j % 2, t, :],
                                       start=t == 0, stop=t == KD - 1)
                    mm.then_inc(ada_mm, 1)
                pe.wait_ge(ada_row, NA)
                for t in range(2 * KD):
                    mm = pe.transpose(psC[:, t * ROWS:(t + 1) * ROWS], modA[:, t * P:(t + 1) * P],
                                      k.ident[0:ROWS, 0:ROWS])
                mm.then_inc(modt_ps, 1)

            @block.vector
            def _(dve):
                dve.wait_ge(ct_ps, 1)
                dve.tensor_copy(k.cT[:].rearrange("p k r -> p (k r)"), psT[:]).then_inc(s1["ct_sb"], 1)
                dve.wait_ge(small_in, 32)
                for j in range(NA):
                    dve.wait_ge(ada_mm, j + 1)
                    dve.tensor_tensor(modA[:, j * BLK:(j + 1) * BLK], psB[0:ROWS, j % 2, :],
                                      brow[:, j * BLK:(j + 1) * BLK], ALU.add).then_inc(ada_row, 1)
                dve.wait_ge(modt_ps, 1)
                dve.tensor_copy(B1[:].rearrange("p k r -> p (k r)"), psC[:, 0:KD * ROWS]).then_inc(modt_sb, 1)
                dve.scalar_tensor_tensor(out=A1[:], in0=psC[:, KD * ROWS:].rearrange("p (k r) -> p k r", r=ROWS),
                                         scalar=1.0, in1=n1col[:].unsqueeze(2).broadcast_to([P, KD, ROWS]),
                                         op0=ALU.add, op1=ALU.mult).then_inc(modt_sb, 1)
                for h in range(2):
                    dve.wait_ge(w1_hi, h + 1)
                    dve.tensor_tensor(w_lo[:, :, h * BLK:(h + 1) * BLK], raw[:, (NA + h) % 2],
                                      w_hi[:, :, h * BLK:(h + 1) * BLK].bitcast(F32), ALU.subtract).then_inc(w1_lo, 1)


def in_projection(k, a, s1, w_hi, w_lo, xraw, A1, B1, u_pool, u_ssm):
    nc = k.nc
    k.stage = "in_projection"
    with ExitStack() as st:
        xn = k.sb(st, "xn", [P, TPB, D])
        junk = k.sb(st, "junk2", [P, TPB, D])
        ss = k.sb(st, "ss2", [P, 4 * TPB])
        hf = k.sb(st, "hf", [P, 2, BLK])
        hT_hi = k.sb(st, "hT_hi", [P, 2, KD, BLK], F32R)
        hT_lo = k.sb(st, "hT_lo", [P, 2, KD, BLK], F32R)
        ust = k.sb(st, "ust", [P, 2, BLK])
        psT = k.ps(st, "psT2", [P, 2, BLK])
        psM = k.ps(st, "psM2", [P, 2, BLK])
        sq_done, ms_done, rt_done, rstd_done, xn_done, t_done, hf_done, hi_done, lo_done, mm_done, u_evac = [
            k.sem(n) for n in ("sq_done", "ms_done", "rt_done", "rstd_done", "xn_done", "t_done", "hf_done",
                               "hi_done", "lo_done", "mm_done", "u_evac")]
        ust_out = [k.sem(f"ust_out{i}") for i in range(2)]
        x_in = s1["x_in"]
        MM0, UE0 = 1, 2
        x_s = a["x_sample"].rearrange("b t d -> (b t) d")

        def t_steps(m):
            return (2 * (m - 3), 2 * (m - 3) + 1) if 3 <= m <= 6 else ()

        with nc.Block() as block:

            @block.sync
            def _(sp):
                for u in range(2):
                    sp.sem_inc(ust_out[u], 16)

                def stores(b, w):
                    for m in range(KD):
                        sp.wait_ge(u_evac, UE0 + 8 * b + m + 1)
                        sp.sem_inc(s1["store_go"], 1)
                        if m < QH:
                            dst = u_pool[m * P:(m + 1) * P, bass.ds(b * BLK, w)]
                            sp.dma_start(dst, ust[:, m % 2, 0:w]).then_inc(ust_out[m % 2], 16)
                        else:
                            c0 = NSEQ + b * (BLK // STEP) if w == BLK else 0
                            dst = u_ssm[(m - QH) * P:(m - QH + 1) * P, :, bass.ds(c0, w // STEP)]
                            sp.dma_start(dst, ust[:, m % 2, 0:w].rearrange("p (s c) -> p s c", s=STEP)
                                         ).then_inc(ust_out[m % 2], 16)

                with sp.Fori(0, NBLK - 1) as b:
                    row = sp.snap(b * BLK + BLK)
                    sp.wait_ge(xn_done, b + 1)
                    sp.dma_start(xraw[:], a["x_prompt"][0, bass.ds(row, BLK), :]
                                 .rearrange("(j p) d -> p j d", p=P)).then_inc(x_in, 16)
                    stores(b, BLK)
                sp.wait_ge(xn_done, NBLK)
                sp.dma_start(xraw[0:TS, 0, :], x_s).then_inc(x_in, 16)
                stores(NBLK - 1, BLK)
                stores(NBLK, TS)
                for u in range(2):
                    sp.wait_ge(ust_out[u], 16 * (1 + 4 * (NBLK + 1)))

            @block.scalar
            def _(act):
                act.sem_inc(u_evac, UE0)

                def norm(b, rows, tiles):
                    act.wait_ge(x_in, 16 * b + 16)
                    for j in range(tiles):
                        ins = act.activation(junk[0:rows, j, :], xraw[0:rows, j, :], ACT.Square,
                                             accum_out=ss[0:rows, j:j + 1])
                    ins.then_inc(sq_done, 1)
                    act.wait_ge(ms_done, b + 1)
                    act.activation(ss[0:rows, 2 * TPB:2 * TPB + tiles], ss[0:rows, TPB:TPB + tiles],
                                   ACT.Sqrt).then_inc(rt_done, 1)

                def modulate(b, t, first=False):
                    act.wait_ge(t_done, 8 * b + t + 1)
                    if not (first and t < 2):
                        act.wait_ge(lo_done, 8 * b + t - 1)
                    act.activation(hf[:, t % 2, :], psT[:, t % 2, :], ACT.Identity, bias=B1[:, t, 0:1],
                                   scale=A1[:, t, 0:1]).then_inc(hf_done, 1)

                def evac(b, m, w):
                    act.wait_ge(mm_done, MM0 + 8 * b + m + 1)
                    act.wait_ge(ust_out[m % 2], 16 * (4 * b + m // 2) + 16)
                    if m < QH:
                        act.copy(ust[:, m % 2, 0:w], psM[:, m % 2, 0:w]).then_inc(u_evac, 1)
                    else:
                        act.copy(ust[:, m % 2, 0:w].rearrange("p (s c) -> p c s", s=STEP),
                                 psM[:, m % 2, 0:w].rearrange("p (c s) -> p c s", s=STEP)).then_inc(u_evac, 1)

                norm(0, P, TPB)
                for t in range(KD):
                    modulate(0, t, first=True)
                with act.Fori(0, NBLK - 1) as b:
                    for m in range(KD):
                        evac(b, m, BLK)
                        if m == 1:
                            norm(b + 1, P, TPB)
                        for t in t_steps(m):
                            modulate(b + 1, t)
                for m in range(KD):
                    evac(NBLK - 1, m, BLK)
                    if m == 1:
                        norm(NBLK, TS, 1)
                for m in range(KD):
                    evac(NBLK, m, TS)

            @block.vector
            def _(dve):
                def norm(b, rows, tiles, first=False):
                    dve.wait_ge(sq_done, b + 1)
                    dve.tensor_scalar(ss[0:rows, TPB:TPB + tiles], ss[0:rows, 0:tiles], 1.0 / D, EPS,
                                      ALU.mult, ALU.add).then_inc(ms_done, 1)
                    dve.wait_ge(rt_done, b + 1)
                    dve.reciprocal(ss[0:rows, 3 * TPB:3 * TPB + tiles],
                                   ss[0:rows, 2 * TPB:2 * TPB + tiles]).then_inc(rstd_done, 1)
                    dve.wait_ge(rstd_done, b + 1)
                    if not first:
                        dve.wait_ge(t_done, 8 * b)
                    for j in range(tiles):
                        ins = dve.tensor_scalar(xn[0:rows, j, :], xraw[0:rows, j, :],
                                                ss[0:rows, 3 * TPB + j:3 * TPB + j + 1], None, ALU.mult)
                    ins.then_inc(xn_done, 1)

                def split(b, t, w, par):
                    dve.wait_ge(hf_done, 8 * b + t + 1)
                    hi = hT_hi[:, par, t, 0:w] if isinstance(par, int) else \
                        hT_hi[:, bass.ds(par, 1), t, 0:w].rearrange("p a n -> p (a n)")
                    lo = hT_lo[:, par, t, 0:w] if isinstance(par, int) else \
                        hT_lo[:, bass.ds(par, 1), t, 0:w].rearrange("p a n -> p (a n)")
                    dve.tensor_copy(hi, hf[:, t % 2, 0:w]).then_inc(hi_done, 1)
                    dve.wait_ge(hi_done, 8 * b + t + 1)
                    dve.tensor_tensor(lo, hf[:, t % 2, 0:w], hi.bitcast(F32), ALU.subtract).then_inc(lo_done, 1)

                norm(0, P, TPB, first=True)
                for t in range(KD):
                    split(0, t, BLK, 0)
                with dve.Fori(0, NBLK - 1) as b:
                    norm(b + 1, P, TPB)
                    dve.wait_ge(mm_done, MM0 + 8 * b)
                    for t in range(KD):
                        split(b + 1, t, BLK, (b + 1) & 1)
                norm(NBLK, TS, 1)
                dve.wait_ge(mm_done, MM0 + 8 * (NBLK - 1))
                for t in range(KD):
                    dve.wait_ge(t_done, 8 * NBLK + t + 1)
                    ps = psT[:, t % 2, 0:TS].rearrange("p (q s) -> p q s", s=LSEQ)
                    h = hf[:, t % 2, 0:TS].rearrange("p (q s) -> p q s", s=LSEQ)
                    dve.tensor_tensor(h, ps, A1[:, t, 1:ROWS].unsqueeze(2).broadcast_to([P, NSEQ, LSEQ]),
                                      ALU.mult).then_inc(s1["hs"], 1)
                    dve.wait_ge(s1["hs"], t + 1)
                    dve.tensor_tensor(h, h, B1[:, t, 1:ROWS].unsqueeze(2).broadcast_to([P, NSEQ, LSEQ]),
                                      ALU.add).then_inc(hf_done, 1)
                    split(NBLK, t, TS, NBLK % 2)

            @block.tensor
            def _(pe):
                pe.sem_inc(mm_done, MM0)

                def turn(b, t, rows, tiles, first=False):
                    if t == 0:
                        pe.wait_ge(xn_done, b + 1)
                    if not (first and t < 2):
                        pe.wait_ge(hf_done, 8 * b + t - 1)
                    for j in range(tiles):
                        mm = pe.transpose(psT[:, t % 2, j * P:j * P + rows], xn[0:rows, j, t * P:(t + 1) * P],
                                          k.ident[0:rows, 0:rows])
                    mm.then_inc(t_done, 1)

                def product(b, m, w, par):
                    if m == 0:
                        pe.wait_ge(lo_done, 8 * b + 8)
                    pe.wait_ge(u_evac, UE0 + 8 * b + m - 1)
                    for t in range(KD):
                        r = [x[:, par, t, 0:w] if isinstance(par, int) else
                             x[:, bass.ds(par, 1), t, 0:w].rearrange("p a n -> p (a n)") for x in (hT_hi, hT_lo)]
                        mm = matmul3(pe, psM[:, m % 2, 0:w], w_hi[:, t, m * P:(m + 1) * P],
                                     w_lo[:, t, m * P:(m + 1) * P], r[0], r[1], t == 0, t == KD - 1)
                    mm.then_inc(mm_done, 1)

                for t in range(KD):
                    turn(0, t, P, TPB, first=True)
                with pe.Fori(0, NBLK - 1) as b:
                    for m in range(KD):
                        product(b, m, BLK, b & 1)
                        for t in t_steps(m):
                            turn(b + 1, t, P, TPB)
                for m in range(KD):
                    product(NBLK - 1, m, BLK, (NBLK - 1) % 2)
                    for t in t_steps(m):
                        turn(NBLK, t, TS, 1)
                for m in range(KD):
                    product(NBLK, m, TS, NBLK % 2)


TWO_PI = 6.283185307179586
TWO_PI_HI = 6.28125
TWO_PI_MID = float(np.float32(TWO_PI - TWO_PI_HI))
TWO_PI_LO = TWO_PI - TWO_PI_HI - TWO_PI_MID
LN2 = 0.6931471805599453
LN2_HI = 0.693359375
LN2_LO = LN2 - LN2_HI
EXP_C = [1 / 5040, 1 / 720, 1 / 120, 1 / 24, 1 / 6, 1 / 2, 1.0]
ROUND = 12582912.0
ADA_W = 128
ADA_FIRST = 2 * D
ADA_N = (6 * D - ADA_FIRST) // ADA_W
ZP = BUF + TP
ZS = BUF + LSEQ


def mixers(k, a, o, mod_d, u_pool, u_ssm, mix_d, g_d):
    nc = k.nc
    k.stage = "mixers"
    with ExitStack() as st:
        U = k.sb(st, "U", [P, G, NCH])
        H = k.sb(st, "H", [P, 2, PAIRS, NCH + 1])
        scratch = k.sb(st, "scratch", [P, 2, 2, PAIRS * P])
        T = k.sb(st, "T", [P, G, P])
        VB = k.sb(st, "VB", [P, 2, PAIRS, P])
        CL = k.sb(st, "CL", [P, 2, PAIRS, (STEP + 1) * GH])
        raw = k.sb(st, "raw3", [P, 2, KD, ADA_W])
        brow = k.sb(st, "brow3", [1, 2, ADA_W])
        ones = k.sb(st, "ones3", [1, ROWS])
        modrow = k.sb(st, "modrow", [ROWS, 2, ADA_W])
        z = k.sb(st, "z", [P, 3, ZP])
        zs = k.sb(st, "zs", [P, QH, NSEQ, ZS])
        ws = k.sb(st, "ws", [P, 2, NSEQ, ZS])
        pooled_s = k.sb(st, "pooled_s", [P, TS])
        yst = k.sb(st, "yst", [P, 2, NCH])
        pst = k.sb(st, "pst", [P, 2, BLK])
        pw = k.sb(st, "pw", [P, QH, P])
        pscale = k.sb(st, "pscale", [P, QH])
        cnt_i = k.sb(st, "cnt_i", [P, 16], I32)
        cnt = k.sb(st, "cnt", [P, QH + 1, 16])
        B = k.sb(st, "B", [P, 2, PAIRS, GH])
        Bb = k.sb(st, "Bb", [P, 2, PAIRS, GH])
        C = k.sb(st, "C", [P, 2, PAIRS, GH])
        h0 = k.sb(st, "h0", [P, 2, NSEQ, PAIRS])
        fin_s = k.sb(st, "fin_s", [P, 2, NSEQ, PAIRS])
        PW = k.sb(st, "PW", [P, 2, STEP + 1, PAIRS])
        sm = k.sb(st, "sm", [P, 24, PAIRS])
        dskip = k.sb(st, "dskip", [GH, G])
        dd = yst[:].rearrange("p a c -> p (a c)")[0:GH, 0:G * GH].rearrange("h (g e) -> h g e", g=G)
        Hf = H[:].rearrange("p a b c -> p (a b c)")
        crow = Hf[0:GH, 0:2 * G * NS].rearrange("h (a n) -> h a n", a=2)
        o1 = 2 * G * NS
        arow = Hf[0:PAIRS, o1:o1 + 3 * P].rearrange("k (a n) -> k a n", a=3)
        dtrow = Hf[0:PAIRS, o1 + 3 * P:o1 + 3 * P + 4]
        o2 = o1 + 3 * P + 4
        h0row = Hf[:, o2:o2 + 2 * P].rearrange("p (a n) -> p a n", a=2)
        o3 = o2 + 2 * P
        sprow = Hf[0:NSEQ * BUF, o3:o3 + HALF]
        o4 = o3 + HALF
        nprow = Hf[0:TS, o4:o4 + 2 * HALF].rearrange("p (a n) -> p a n", a=2)
        o5 = o4 + 2 * HALF
        ztail = Hf[:, o5:o5 + QH * BUF].rearrange("p (q j) -> p q j", q=QH)
        o6 = o5 + QH * BUF
        zsrow = Hf[:, o6:o6 + QH * TS].rearrange("p (q j) -> p q j", q=QH)
        WB = scratch[:, 0].rearrange("p a (k n) -> p a k n", k=PAIRS)
        tmp = scratch[:, 1]
        KK = scratch[0:GH, 1].rearrange("h a n -> h (a n)").rearrange("h (g n) -> h g n", g=G)
        E = scratch[:].rearrange("p a b n -> p (a b n)").rearrange("p (a k c) -> p a k c", a=2, k=PAIRS)
        rt = VB[:].rearrange("p a k n -> p (a k n)").rearrange("p (t k c) -> p t k c", t=8, k=2)
        finrow = rt[:, 6].rearrange("p k (a n) -> p (k a) n", n=P)

        psA = k.ps(st, "psA3", [P, 2, BLK])
        psX = k.ps(st, "psX3", [P, 4, BLK])
        psP = k.ps(st, "psP3", [P, 2, BLK])
        names = ("tab_in", "c3_in", "h0_in", "sp_in", "pw_in", "u3_in", "zs_in", "z_in", "dt_row",
                 "x_fill", "x_evac", "ada2_mm", "a_evac", "arg", "sins", "wb_ready", "cl_ready",
                 "kk_diag", "t_zero", "t_in", "dve3", "pool3", "cnt_i_ok", "cnt_ok", "pooled", "p_mm", "p_evac",
                 "h_ready", "h_fix", "np_out", "fin_out", "b3_in", "d3_in", "ones_ok", "z_head", "zt_in")
        s = {n: k.sem(n) for n in names}
        raw_in = [k.sem(f"raw3_in{i}") for i in range(2)]
        mod_out = [k.sem(f"mod_out{i}") for i in range(2)]
        y_out = [k.sem(f"y_out{i}") for i in range(2)]
        p_out = [k.sem(f"p_out{i}") for i in range(2)]
        order = ["hist", "C", "h0", "np_s", "np_p", "tab"] + [f"VB{i}" for i in range(8)] + \
            [f"KK{i}" for i in range(8)] + [f"V{i}" for i in range(2 * PAIRS)] + [f"Y{i}" for i in range(G)] + \
            ["fin_p", "fin_s"]
        at = {n: i for i, n in enumerate(order)}
        PB = [(j * BLK, BLK) for j in range(NBLK)] + [(TP, TS)]

        with nc.Block() as block:

            @block.sync
            def _(sp):
                for i, n in enumerate(("ssm_a_re", "ssm_a_im")):
                    sp.dma_start(arow[:, i, :], a[n][0].rearrange("(k g) p -> k (g p)", g=2)).then_inc(s["tab_in"], 16)
                sp.dma_start(dtrow[:, 0:2], a["ssm_log_dt"][0].rearrange("(k g) -> k g", g=2)).then_inc(s["tab_in"], 16)
                for i, n in enumerate(("ssm_c_re", "ssm_c_im")):
                    sp.dma_start(crow[:, i, :].rearrange("h (g p) -> h g p", g=G),
                                 a[n][0].rearrange("g h p -> h g p")).then_inc(s["c3_in"], 16)
                for i, n in enumerate(("ssm_b_re", "ssm_b_im")):
                    sp.dma_start(B[:, i], a[n][0].rearrange("(k g) p h -> (g p) k h", g=2)).then_inc(s["b3_in"], 16)
                sp.dma_start(sprow, a["state_pool"][0].rearrange("b j c -> (b j) c")).then_inc(s["sp_in"], 16)
                for i, n in enumerate(("state_ssm_re", "state_ssm_im")):
                    sp.dma_start(h0row[:, i, :], a[n][0].rearrange("b (k g) p -> (b k) (g p)", g=2)
                                 ).then_inc(s["h0_in"], 16)
                for q in range(QH):
                    sp.dma_start(zs[:, q, :, BUF:ZS], u_pool[q * P:(q + 1) * P, TP:TOK]
                                 .rearrange("p (b j) -> p b j", b=NSEQ)).then_inc(s["zs_in"], 16)
                sp.dma_start(zsrow, u_pool[:, TP:TOK].rearrange("(q p) j -> p q j", p=P)).then_inc(s["zt_in"], 16)
                sp.dma_start(ztail, u_pool[:, TP - BUF:TP].rearrange("(q p) j -> p q j", p=P)).then_inc(s["zt_in"], 16)
                sp.dma_start(dskip[:], a["ssm_d"][0].rearrange("g h -> h g"),
                             allow_slow_non_contiguous=True).then_inc(s["d3_in"], 16)
                sp.dma_start(pw[:], a["pool_w"][0].rearrange("q c d -> c q d")).then_inc(s["pw_in"], 16)
                sp.dma_start(pscale[:], a["pool_scale"][0].rearrange("(q p) -> p q", p=P),
                             allow_slow_non_contiguous=True).then_inc(s["pw_in"], 16)
                sp.dma_start(o["pool_s"][0, :, 0:BUF - LSEQ, :], a["state_pool"][0, :, LSEQ:BUF, :]).then_inc(s["np_out"], 16)
                ada = a["w_ada"][0].rearrange("(k p) n -> p k n", p=P)

                def ada_load(j, u):
                    c0 = sp.snap((j + u) * ADA_W + ADA_FIRST) if not isinstance(j, int) else (j + u) * ADA_W + ADA_FIRST
                    sp.wait_ge(s["ada2_mm"], j + u + 1)
                    sp.dma_start(raw[:, u], ada[:, :, bass.ds(c0, ADA_W)]).then_inc(raw_in[u], 16)
                    sp.dma_start(brow[:, u, :], a["b_ada"][:, bass.ds(c0, ADA_W)]).then_inc(raw_in[u], 16)

                for u in range(2):
                    ada_load(0, u)
                for i in range(STEP):
                    sp.dma_start(U[i * GH:(i + 1) * GH, :, :],
                                 u_ssm[:, STEP - 1 - i, :].rearrange("(g h) c -> h g c", h=GH)).then_inc(s["u3_in"], 16)
                with sp.Fori(2, ADA_N - 1, 2) as j:
                    for u in range(2):
                        ada_load(j, u)

            @block.gpsimd
            def _(pool):
                ch = Chain(pool, s["pool3"])
                pool.memset(ones[:], 1.0).then_inc(s["ones_ok"], 1)
                pool.memset(T[:], 0.0).then_inc(s["t_zero"], 1)
                pool.iota(cnt_i[:], [[1, 16]], base=1, channel_multiplier=0).then_inc(s["cnt_i_ok"], 1)
                pool.memset(z[:, 0, 0:BUF], 0.0).then_inc(s["z_head"], 1)
                pool.wait_ge(s["zs_in"], 16 * QH)
                pool.wait_ge(s["x_evac"], at["hist"] + 1)
                for q, w in enumerate(WINDOWS):
                    if q:
                        pool.wait_ge(s["p_mm"], 5 * q)
                    pool.dma_start(z[:, 0, BUF:ZP], u_pool[q * P:(q + 1) * P, 0:TP]).then_inc(s["z_in"], 16)
                    pool.wait_ge(s["z_in"], 16 * (q + 1))
                    pool.wait_ge(s["z_head"], 1)
                    zc, sc = z[:, 0], zs[:, q]
                    lag, slot = 1, 0
                    while lag < w:
                        zn, sn = z[:, 1 + slot % 2], ws[:, slot % 2]
                        b0 = 2 * lag - 1
                        pool.tensor_tensor(zn[:, b0:ZP], zc[:, b0:ZP], zc[:, b0 - lag:ZP - lag], ALU.add
                                           ).then_inc(s["pool3"], 1)
                        pool.tensor_tensor(sn[:, :, b0:ZS], sc[:, :, b0:ZS], sc[:, :, b0 - lag:ZS - lag], ALU.add
                                           ).then_inc(s["pool3"], 1)
                        ch.n += 2
                        pool.wait_ge(s["pool3"], ch.n)
                        zc, sc, lag, slot = zn, sn, 2 * lag, slot + 1
                    pool.wait_ge(s["cnt_ok"], 1)
                    pool.tensor_tensor(zc[:, BUF:BUF + 16], zc[:, BUF:BUF + 16], cnt[:, q, :], ALU.mult).then_inc(s["pool3"], 1)
                    pool.tensor_scalar(zc[:, BUF + 16:ZP], zc[:, BUF + 16:ZP], 1.0 / w, None, ALU.mult).then_inc(s["pool3"], 1)
                    pool.tensor_scalar(sc[:, :, BUF:ZS], sc[:, :, BUF:ZS], 1.0 / w, None, ALU.mult).then_inc(s["pool3"], 1)
                    ch.n += 3
                    pool.wait_ge(s["pool3"], ch.n)
                    pool.tensor_tensor(zc[:, BUF:ZP], zc[:, BUF:ZP], z[:, 0, BUF:ZP], ALU.subtract).then_inc(s["pooled"], 1)
                    pool.tensor_tensor(pooled_s[:].rearrange("p (b j) -> p b j", b=NSEQ), sc[:, :, BUF:ZS],
                                       zs[:, q, :, BUF:ZS], ALU.subtract).then_inc(s["pooled"], 1)

            @block.tensor
            def _(pe):
                pe.sem_inc(s["ada2_mm"], 2)
                pe.wait_ge(s["ones_ok"], 1)
                idt = k.ident

                def slot(n):
                    i = at[n]
                    if i >= 4:
                        pe.wait_ge(s["x_evac"], i - 3)
                    return psX[:, i % 4, :]

                def ada(j0, j1):
                    with pe.Fori(j0, j1 - 1, 2) as j:
                        for u in range(2):
                            pe.wait_ge(raw_in[u], 16 * j + 32)
                            pe.wait_ge(s["a_evac"], j + u + 1)
                            out = psA[0:ROWS, u, 0:ADA_W]
                            for t in range(KD):
                                pe.matmul(out, k.cT[:, t, :], raw[:, u, t, :], start=t == 0, stop=False)
                            pe.matmul(out, ones[0:1, :], brow[0:1, u, :], start=False, stop=True
                                      ).then_inc(s["ada2_mm"], 1)

                def pooled_product(q):
                    pe.wait_ge(s["pw_in"], 32)
                    pe.wait_ge(s["pooled"], 2 * q + 2)
                    src = z[:, 1 + q % 2]
                    for j, (c0, w) in enumerate(PB):
                        n = 5 * q + j
                        if n >= 2:
                            pe.wait_ge(s["p_evac"], n - 1)
                        rhs = src[:, BUF + c0:BUF + c0 + w] if w == BLK else pooled_s[:]
                        pe.matmul(psP[:, n % 2, 0:w], pw[:, q, :], rhs, start=True, stop=True).then_inc(s["p_mm"], 1)

                pe.wait_ge(s["sp_in"], 16)
                x = slot("hist")
                nh = NSEQ * BUF
                for q in range(QH):
                    mm = pe.transpose(x[:, q * nh:(q + 1) * nh], sprow[:, q * P:(q + 1) * P], idt[0:nh, 0:nh])
                mm.then_inc(s["x_fill"], 1)
                pe.wait_ge(s["c3_in"], 32)
                x = slot("C")
                for i in range(2):
                    for p in range(PAIRS):
                        c0 = (i * PAIRS + p) * GH
                        mm = pe.transpose(x[:, c0:c0 + GH], crow[:, i, p * P:(p + 1) * P], idt[0:GH, 0:GH])
                mm.then_inc(s["x_fill"], 1)
                pe.wait_ge(s["h0_in"], 32)
                x = slot("h0")
                for i in range(2):
                    mm = pe.transpose(x[:, i * P:(i + 1) * P], h0row[:, i, :], idt[:])
                mm.then_inc(s["x_fill"], 1)
                pe.wait_ge(s["zt_in"], 32)
                x = slot("np_s")
                for q in range(QH):
                    mm = pe.transpose(x[0:TS, q * P:(q + 1) * P], zsrow[:, q, :], idt[:])
                mm.then_inc(s["x_fill"], 1)
                x = slot("np_p")
                for q in range(QH):
                    mm = pe.transpose(x[0:BUF, q * P:(q + 1) * P], ztail[:, q, :], idt[:])
                mm.then_inc(s["x_fill"], 1)
                pe.wait_ge(s["dt_row"], 1)
                x = slot("tab")
                for i in range(3):
                    mm = pe.transpose(x[:, i * PAIRS:(i + 1) * PAIRS], arow[:, i, :], idt[0:PAIRS, 0:PAIRS])
                mm.then_inc(s["x_fill"], 1)
                ada(0, 8)
                ada(8, 16)
                pooled_product(0)
                pe.wait_ge(s["wb_ready"], 1)
                for f in range(8):
                    x = slot(f"VB{f}")
                    for j in range(4):
                        i, p = divmod(4 * f + j, PAIRS)
                        mm = pe.transpose(x[:, j * P:(j + 1) * P], WB[:, i, p, :], idt[:])
                    mm.then_inc(s["x_fill"], 1)
                pe.wait_ge(s["cl_ready"], 1)
                for f in range(8):
                    x = slot(f"KK{f}")
                    for j in range(4):
                        p, g2 = 4 * (f // 2) + j, f % 2
                        r = slice(NS * g2, NS * g2 + NS)
                        for i in range(2):
                            mm = pe.matmul(x[0:GH, j * P:(j + 1) * P], Bb[r, i, p, :], CL[r, i, p, 0:P],
                                           start=i == 0, stop=i == 1)
                    mm.then_inc(s["x_fill"], 1)
                pooled_product(1)
                pe.wait_ge(s["u3_in"], 16 * STEP)
                for p in range(PAIRS):
                    for i in range(2):
                        x = slot(f"V{2 * p + i}")
                        for g2 in range(2):
                            mm = pe.matmul(x[NS * g2:NS * g2 + NS, 0:NCH], VB[:, i, p, NS * g2:NS * g2 + NS],
                                           U[:, 2 * p + g2, :], start=True, stop=True)
                        mm.then_inc(s["x_fill"], 1)
                pooled_product(2)
                pooled_product(3)
                ada(16, 32)
                pe.wait_ge(s["t_in"], 16 * STEP)
                for g in range(G):
                    p, g2 = divmod(g, 2)
                    pe.wait_ge(s["h_ready"], g // 4 + 1)
                    x = slot(f"Y{g}")[:, 0:NCH]
                    r = slice(NS * g2, NS * g2 + NS)
                    pe.matmul(x, T[:, g, :], U[:, g, :], start=True, stop=False)
                    for i in range(2):
                        mm = pe.matmul(x, CL[r, i, p, GH:], H[r, i, p, 0:NCH], start=False, stop=i == 1)
                    mm.then_inc(s["x_fill"], 1)
                x = slot("fin_p")
                for i in range(2):
                    mm = pe.transpose(x[0:PAIRS, i * P:(i + 1) * P], H[:, i, :, NCH], idt[:])
                mm.then_inc(s["x_fill"], 1)
                x = slot("fin_s")
                for i in range(2):
                    mm = pe.transpose(x[:, i * P:(i + 1) * P], fin_s[:, i].rearrange("p b k -> p (b k)"), idt[:])
                mm.then_inc(s["x_fill"], 1)

            @block.scalar
            def _(act):
                act.sem_inc(s["a_evac"], 2)
                for u in range(2):
                    act.sem_inc(mod_out[u], 16)
                def evac(n, out, rows=P, w=BLK, func=None, f=None):
                    i = at[n]
                    act.wait_ge(s["x_fill"], i + 1)
                    x = psX[0:rows, i % 4, 0:w]
                    if f:
                        x = f(x)
                    (act.activation(out, x, func) if func else act.copy(out, x)).then_inc(s["x_evac"], 1)

                def ada(j0, j1):
                    with act.Fori(j0, j1 - 1, 2) as j:
                        for u in range(2):
                            c0 = act.snap((j + u) * ADA_W + ADA_FIRST)
                            act.wait_ge(mod_out[u], 8 * j + 16)
                            act.wait_ge(s["ada2_mm"], j + u + 3)
                            act.copy(modrow[:, u, :], psA[0:ROWS, u, 0:ADA_W]).then_inc(s["a_evac"], 1)
                            act.wait_ge(s["a_evac"], j + u + 3)
                            act.dma_start(mod_d[:, bass.ds(c0, ADA_W)], modrow[:, u, :]).then_inc(mod_out[u], 16)

                def pooled_out(q):
                    for j, (c0, w) in enumerate(PB):
                        n = 5 * q + j
                        act.wait_ge(s["p_mm"], n + 1)
                        if n >= 2:
                            act.wait_ge(p_out[n % 2], 16 * (n // 2))
                        act.activation(pst[:, n % 2, 0:w], psP[:, n % 2, 0:w], ACT.Copy,
                                       scale=pscale[:, q:q + 1]).then_inc(s["p_evac"], 1)
                        act.wait_ge(s["p_evac"], n + 1)
                        act.dma_start(mix_d[q * P:(q + 1) * P, c0:c0 + w], pst[:, n % 2, 0:w]).then_inc(p_out[n % 2], 16)

                evac("hist", zs[:, :, :, 0:BUF],
                     w=QH * NSEQ * BUF, f=lambda x: x.rearrange("p (q b j) -> p q b j", q=QH, b=NSEQ))
                evac("C", C[:].rearrange("p a k h -> p (a k h)"))
                evac("h0", h0[:].rearrange("p a b k -> p (a b k)"), w=2 * P)
                evac("np_s", nprow[:, 0, :], rows=TS)
                evac("np_p", nprow[0:BUF, 1, :], rows=BUF)
                evac("tab", sm[:, 0:3, :].rearrange("p a k -> p (a k)"), w=3 * PAIRS)
                act.wait_ge(s["x_evac"], at["np_p"] + 1)
                act.dma_start(o["pool_s"][0, :, BUF - LSEQ:BUF, :], nprow[:, 0, :]).then_inc(s["np_out"], 16)
                act.dma_start(o["pool_p"][0, 0], nprow[0:BUF, 1, :]).then_inc(s["np_out"], 16)
                ada(0, 8)
                act.wait_ge(s["arg"], 1)
                act.activation(sm[:, 9, :], sm[:, 7, :], ACT.Sin)
                act.activation(sm[:, 10, :], sm[:, 8, :], ACT.Sin).then_inc(s["sins"], 1)
                ada(8, 16)
                pooled_out(0)
                for f in range(8):
                    i, p = divmod(4 * f, PAIRS)
                    evac(f"VB{f}", VB[:, i, p:p + 4, :].rearrange("p k n -> p (k n)"))
                for f in range(8):
                    evac(f"KK{f}", KK[:, 8 * (f // 2) + f % 2:8 * (f // 2) + 8:2, :], rows=GH,
                         f=lambda x: x.rearrange("h (g n) -> h g n", n=P))
                act.wait_ge(s["kk_diag"], 1)
                act.wait_ge(s["t_zero"], 1)
                for i in range(STEP):
                    t = STEP - 1 - i
                    act.dma_start(T[i * GH:(i + 1) * GH, :, t * GH:P], KK[:, :, 0:P - t * GH]).then_inc(s["t_in"], 16)
                pooled_out(1)
                act.wait_ge(s["np_out"], 48)
                for p in range(PAIRS):
                    for i in range(2):
                        evac(f"V{2 * p + i}", H[:, i, p, 1:NCH + 1], w=NCH)
                pooled_out(2)
                pooled_out(3)
                ada(16, 32)
                for g in range(G):
                    if g >= 2:
                        act.wait_ge(y_out[g % 2], 16 * (g // 2))
                    evac(f"Y{g}", yst[:, g % 2, :], w=NCH, func=ACT.Gelu_apprx_tanh)
                    act.wait_ge(s["x_evac"], at[f"Y{g}"] + 1)
                    act.dma_start(g_d[g * GH:(g + 1) * GH, :, :].rearrange("h t c -> t h c"),
                                  yst[:, g % 2, :]).then_inc(y_out[g % 2], 16)
                evac("fin_p", finrow[0:PAIRS, 0:2, :].rearrange("p a n -> p (a n)"), rows=PAIRS, w=2 * P)
                evac("fin_s", finrow[:, 2:4, :].rearrange("p a n -> p (a n)"), w=2 * P)
                act.wait_ge(s["x_evac"], at["fin_s"] + 1)
                for i, n in enumerate(("re", "im")):
                    act.dma_start(o[n + "_p"][0, 0].rearrange("(k g) p -> k (g p)", g=2), finrow[0:PAIRS, i, :]
                                  ).then_inc(s["fin_out"], 16)
                    act.dma_start(o[n + "_s"][0].rearrange("b (k g) p -> (b k) (g p)", g=2), finrow[:, 2 + i, :]
                                  ).then_inc(s["fin_out"], 16)
                act.wait_ge(s["fin_out"], 64)
                for u in range(2):
                    act.wait_ge(y_out[u], 16 * (G // 2))
                    act.wait_ge(p_out[u], 16 * 10)
                    act.wait_ge(mod_out[u], 16 * (1 + ADA_N // 2))

            @block.vector
            def _(dve):
                ch = Chain(dve, s["dve3"])
                tt, ts, stt = dve.tensor_tensor, dve.tensor_scalar, dve.scalar_tensor_tensor

                def exp(out, x, t, ti):
                    ch.link(ts(t[0], x, 1.0 / LN2, ROUND, ALU.mult, ALU.add))
                    ch.link(ts(t[0], t[0], ROUND, None, ALU.subtract))
                    ch.link(stt(out=t[1], in0=t[0], scalar=-LN2_HI, in1=x, op0=ALU.mult, op1=ALU.add))
                    ch.link(stt(out=t[1], in0=t[0], scalar=-LN2_LO, in1=t[1], op0=ALU.mult, op1=ALU.add))
                    ch.link(ts(ti, t[0], 127.0, 1.0, ALU.add, ALU.max))
                    ch.link(ts(ti, ti, 23, None, ALU.logical_shift_left))
                    ch.link(ts(t[2], t[1], EXP_C[0], None, ALU.mult))
                    for c in EXP_C[1:]:
                        ch.link(stt(out=t[2], in0=t[2], scalar=c, in1=t[1], op0=ALU.add, op1=ALU.mult))
                    ch.link(stt(out=out, in0=t[2], scalar=1.0, in1=ti.bitcast(F32), op0=ALU.add, op1=ALU.mult))

                dve.wait_ge(s["tab_in"], 48)
                exp(dtrow[:, 2:4], dtrow[:, 0:2], [sm[0:PAIRS, j, 0:2] for j in (20, 21, 22)],
                    sm[0:PAIRS, 23, 0:2].bitcast(I32))
                dve.tensor_copy(arow[:, 2, :].rearrange("k (g p) -> k g p", g=2),
                                dtrow[:, 2:4].unsqueeze(2).broadcast_to([PAIRS, 2, NS])).then_inc(s["dt_row"], 1)
                dve.wait_ge(s["cnt_i_ok"], 1)
                ch.link(dve.tensor_copy(cnt[:, QH, :], cnt_i[:]))
                for q, w in enumerate(WINDOWS):
                    ins = ts(cnt[:, q, :], cnt[:, QH, :], float(w), None, ALU.min)
                ch.link(ins)
                dve.reciprocal(cnt[:, 0:QH, :], cnt[:, 0:QH, :]).then_inc(s["cnt_ok"], 1)

                dve.wait_ge(s["x_evac"], at["tab"] + 1)
                S = [sm[:, i, :] for i in range(24)]
                tt(S[3], S[0], S[2], ALU.mult)
                ch.link(tt(S[4], S[1], S[2], ALU.mult))
                ch.link(ts(S[11], S[4], 1.0 / TWO_PI, ROUND, ALU.mult, ALU.add))
                ch.link(ts(S[11], S[11], ROUND, None, ALU.subtract))
                ch.link(stt(out=S[7], in0=S[11], scalar=-TWO_PI_HI, in1=S[4], op0=ALU.mult, op1=ALU.add))
                ch.link(stt(out=S[7], in0=S[11], scalar=-TWO_PI_MID, in1=S[7], op0=ALU.mult, op1=ALU.add))
                ch.link(stt(out=S[7], in0=S[11], scalar=-TWO_PI_LO, in1=S[7], op0=ALU.mult, op1=ALU.add))
                ch.link(ts(S[7], S[7], 3.1415925, -3.1415925, ALU.min, ALU.max))
                ch.link(stt(out=S[8], in0=S[7], scalar=-1.0, in1=S[7], op0=ALU.mult, op1=ALU.max))
                ts(S[8], S[8], -1.0, TWO_PI / 4, ALU.mult, ALU.add).then_inc(s["arg"], 1)
                exp(S[5], S[3], [S[20], S[21], S[22]], S[23].bitcast(I32))
                ch.link(tt(S[6], S[5], S[5], ALU.mult))
                ch.link(tt(S[11], S[6], S[6], ALU.mult))
                ch.link(tt(S[6], S[11], S[11], ALU.mult))
                dve.wait_ge(s["sins"], 1)
                R, I = (lambda j: PW[:, 0, j, :]), (lambda j: PW[:, 1, j, :])
                dve.memset(PW[:, 0, 0, :], 1.0)
                dve.memset(PW[:, 1, 0, :], 0.0)
                tt(R(1), S[5], S[10], ALU.mult)
                ch.link(tt(I(1), S[5], S[9], ALU.mult))

                def cmul(outr, outi, ar, ai, br, bi, t, neg_i=False):
                    tt(t[0], ar, br, ALU.mult)
                    tt(t[1], ai, bi, ALU.mult)
                    tt(t[2], ar, bi, ALU.mult)
                    ch.link(tt(t[3], ai, br, ALU.mult))
                    tt(outr, t[0], t[1], ALU.subtract)
                    if neg_i:
                        ch.link(stt(out=outi, in0=t[2], scalar=-1.0, in1=t[3], op0=ALU.mult, op1=ALU.subtract))
                    else:
                        ch.link(tt(outi, t[2], t[3], ALU.add))

                m = 1
                while m < STEP:
                    bc = [PW[:, i, m:m + 1, :].broadcast_to([P, m, PAIRS]) for i in range(2)]
                    t4 = [tmp[:, 0, j * STEP * PAIRS:j * STEP * PAIRS + m * PAIRS].rearrange("p (m k) -> p m k", m=m)
                          for j in range(4)]
                    cmul(PW[:, 0, m + 1:2 * m + 1, :], PW[:, 1, m + 1:2 * m + 1, :], PW[:, 0, 1:m + 1, :],
                         PW[:, 1, 1:m + 1, :], bc[0], bc[1], t4)
                    m *= 2
                ch.link(ts(S[12], R(1), 1.0, None, ALU.subtract))
                tt(S[13], S[0], S[0], ALU.mult)
                ch.link(tt(S[14], S[1], S[1], ALU.mult))
                ch.link(tt(S[13], S[13], S[14], ALU.add))
                ch.link(dve.reciprocal(S[13], S[13]))
                tt(S[14], S[12], S[0], ALU.mult)
                tt(S[15], I(1), S[1], ALU.mult)
                tt(S[16], I(1), S[0], ALU.mult)
                ch.link(tt(S[17], S[12], S[1], ALU.mult))
                tt(S[14], S[14], S[15], ALU.add)
                ch.link(tt(S[16], S[16], S[17], ALU.subtract))
                tt(S[14], S[14], S[13], ALU.mult)
                ch.link(tt(S[15], S[16], S[13], ALU.mult))
                dve.wait_ge(s["b3_in"], 32)
                kb = [S[14 + i].unsqueeze(2).broadcast_to([P, PAIRS, GH]) for i in range(2)]
                NB = PAIRS * GH
                t4 = [tmp[:, 0, j * NB:(j + 1) * NB].rearrange("p (k h) -> p k h", k=PAIRS) for j in range(4)]
                cmul(Bb[:, 0], Bb[:, 1], B[:, 0], B[:, 1], kb[0], kb[1], t4)
                for hp in range(2):
                    ks = slice(8 * hp, 8 * hp + 8)
                    n = 8 * P
                    t4 = [tmp.rearrange("p a n -> p (a n)")[:, j * n:(j + 1) * n].rearrange("p (k t h) -> p k t h", k=8, h=GH)
                          for j in range(4)]
                    pb = [PW[:, i, 0:STEP, ks].rearrange("p t k -> p k t").unsqueeze(3).broadcast_to([P, 8, STEP, GH])
                          for i in range(2)]
                    bb = [Bb[:, i, ks].unsqueeze(2).broadcast_to([P, 8, STEP, GH]) for i in range(2)]
                    wo = [WB[:, i, ks].rearrange("p k (t h) -> p k t h", h=GH) for i in range(2)]
                    cmul(wo[0], wo[1], pb[0], pb[1], bb[0], bb[1], t4)
                dve.sem_inc(s["wb_ready"], 1)
                dve.wait_ge(s["x_evac"], at["C"] + 1)
                for hp in range(4):
                    ks = slice(4 * hp, 4 * hp + 4)
                    n = 4 * (STEP + 1) * GH
                    t4 = [tmp.rearrange("p a n -> p (a n)")[:, j * n:(j + 1) * n].rearrange("p (k t h) -> p k t h", k=4, h=GH)
                          for j in range(4)]
                    pb = [PW[:, i, :, ks].rearrange("p t k -> p k t").unsqueeze(3).broadcast_to([P, 4, STEP + 1, GH])
                          for i in range(2)]
                    cb = [C[:, i, ks].unsqueeze(2).broadcast_to([P, 4, STEP + 1, GH]) for i in range(2)]
                    co = [CL[:, i, ks].rearrange("p k (t h) -> p k t h", h=GH) for i in range(2)]
                    cmul(co[0], co[1], pb[0], pb[1], cb[0], cb[1], t4, neg_i=True)
                dve.sem_inc(s["cl_ready"], 1)
                dve.wait_ge(s["d3_in"], 16)
                ch.link(tt(dd, dskip[:].unsqueeze(2).broadcast_to([GH, G, GH]),
                           k.ident[0:GH, 0:GH].unsqueeze(1).broadcast_to([GH, G, GH]), ALU.mult))
                dve.wait_ge(s["x_evac"], at["KK7"] + 1)
                tt(KK[:, :, 0:GH], KK[:, :, 0:GH], dd, ALU.add).then_inc(s["kk_diag"], 1)

                def unit(r, i, t0, t1):
                    tt(t0, r, r, ALU.mult)
                    ch.link(tt(t1, i, i, ALU.mult))
                    ch.link(tt(t0, t0, t1, ALU.add))
                    ch.link(ts(t0, t0, -0.5, 1.5, ALU.mult, ALU.add))
                    tt(r, r, t0, ALU.mult)
                    ch.link(tt(i, i, t0, ALU.mult))

                t4 = S[16:20]
                cmul(S[20], S[21], S[10], S[9], S[10], S[9], t4)
                unit(S[20], S[21], S[16], S[17])
                for _ in range(2):
                    cmul(S[22], S[23], S[20], S[21], S[20], S[21], t4)
                    unit(S[22], S[23], S[16], S[17])
                    dve.tensor_copy(S[20], S[22])
                    ch.link(dve.tensor_copy(S[21], S[23]))
                dve.wait_ge(s["t_in"], 16 * STEP)
                dve.tensor_copy(E[:, 0, :, 0], S[20])
                ch.link(dve.tensor_copy(E[:, 1, :, 0], S[21]))
                dve.wait_ge(s["x_evac"], at[f"V{2 * PAIRS - 1}"] + 1)
                vb = VB[:].rearrange("p a k n -> p (a k n)")
                m = 1
                while m < PCH:
                    hm = min(m, 64)
                    for c0 in range(0, m, hm):
                        t4 = [vb[:, j * 1024:j * 1024 + PAIRS * hm].rearrange("p (k c) -> p k c", k=PAIRS) for j in range(4)]
                        bc = [S[20 + i].unsqueeze(2).broadcast_to([P, PAIRS, hm]) for i in range(2)]
                        cmul(E[:, 0, :, m + c0:m + c0 + hm], E[:, 1, :, m + c0:m + c0 + hm], E[:, 0, :, c0:c0 + hm],
                             E[:, 1, :, c0:c0 + hm], bc[0], bc[1], t4)
                    cmul(S[22], S[23], S[20], S[21], S[20], S[21], S[16:20])
                    unit(S[22], S[23], S[16], S[17])
                    dve.tensor_copy(S[20], S[22])
                    ch.link(dve.tensor_copy(S[21], S[23]))
                    m *= 2
                p8 = [PW[:, i, STEP:STEP + 1, :].broadcast_to([P, NSEQ, PAIRS]) for i in range(2)]
                t4 = [vb[:, j * P:(j + 1) * P].rearrange("p (b k) -> p b k", b=NSEQ) for j in range(4)]
                fin_t = vb[:, 4 * P:6 * P].rearrange("p (a b k) -> p a b k", a=2, b=NSEQ)
                cmul(fin_t[:, 0], fin_t[:, 1], h0[:, 0], h0[:, 1], p8[0], p8[1], t4)
                for i in range(2):
                    ins = tt(fin_s[:, i], fin_t[:, i], H[:, i, :, 1:NSEQ + 1].rearrange("p k b -> p b k"), ALU.add)
                ch.link(ins)
                for i in range(2):
                    dve.tensor_copy(H[:, i, :, 0:NSEQ].rearrange("p k b -> p b k"), h0[:, i])
                    ins = dve.memset(H[:, i, :, NSEQ:NSEQ + 1], 0.0)
                ch.link(ins)
                n0, PER = ch.n, 8
                with dve.Fori(0, PAIRS - 1, 2) as p0:
                    ch.base, ch.n = p0 * (PER // 2) + n0, 0
                    hr, hi = [H[:, i, bass.ds(p0, 2), NSEQ + 1:NCH + 1] for i in range(2)]
                    er, ei = [E[:, i, bass.ds(p0, 2), :] for i in range(2)]
                    t = [rt[:, j] for j in range(4)]
                    tt(t[0], hr, er, ALU.mult)
                    tt(t[1], hi, ei, ALU.mult)
                    tt(t[2], hi, er, ALU.mult)
                    ch.link(tt(t[3], hr, ei, ALU.mult))
                    tt(hr, t[0], t[1], ALU.add)
                    ch.link(tt(hi, t[2], t[3], ALU.subtract))
                    for j in range(2):
                        rho = sm[:, 6, bass.ds(p0 + j, 1)].broadcast_to([P, PCH])
                        for i in range(2):
                            row = H[:, i, bass.ds(p0 + j, 1), NSEQ + 1:NCH + 1].rearrange("p a c -> p (a c)")
                            ch.link(dve.tensor_tensor_scan(rt[:, 4 + i, j, :], rho, row, 0.0, ALU.mult, ALU.add))
                    gr, gi = rt[:, 4], rt[:, 5]
                    tt(t[0], gr, er, ALU.mult)
                    tt(t[1], gi, ei, ALU.mult)
                    tt(t[2], gr, ei, ALU.mult)
                    ch.link(tt(t[3], gi, er, ALU.mult))
                    tt(hr, t[0], t[1], ALU.subtract)
                    ch.link(tt(hi, t[2], t[3], ALU.add))
                    dve.sem_inc(s["h_ready"], 1)
                assert ch.n == PER


def glu(k, a, g_d, mix_d, wo_hi, wo_lo):
    nc = k.nc
    k.stage = "glu"
    CB = BLK // STEP
    with ExitStack() as st:
        gw = k.sb(st, "gw", [P, QH, HALF])
        gw_hi = k.sb(st, "gw_hi", [P, QH, HALF], F32R)
        gw_lo = k.sb(st, "gw_lo", [P, QH, HALF], F32R)
        gb = k.sb(st, "gb", [P, QH])
        gf = k.sb(st, "gf", [P, 2, QH, BLK])
        g_hi = k.sb(st, "g_hi", [P, 2, QH, BLK], F32R)
        g_lo = k.sb(st, "g_lo", [P, 2, QH, BLK], F32R)
        sg = k.sb(st, "sg", [P, 2, BLK])
        mo = k.sb(st, "mo", [P, 2, BLK])
        wraw = k.sb(st, "wraw", [P, 2, KD, BLK // 2])
        psG = k.ps(st, "psG", [P, 2, BLK])
        gw_in, gb_in, gw_h, gw_l, ghi, glo, g_mm, sg_done, mo_done, wo_h, wo_l = [
            k.sem(n) for n in ("gw_in", "gb_in", "gw_h", "gw_l", "ghi", "glo", "g_mm", "sg_done", "mo_done",
                               "wo_h", "wo_l")]
        g_in = [k.sem(f"g_in{i}") for i in range(2)]
        mo_out = [k.sem(f"mo_out{i}") for i in range(2)]
        wraw_in = [k.sem(f"wraw_in{i}") for i in range(2)]
        WP = D // (BLK // 2)
        with nc.Block() as block:

            def g_load(sp, b, u, w):
                c0 = b * CB + NSEQ if w == BLK else 0
                for q in range(QH):
                    sp.dma_start(gf[:, u, q, 0:w].rearrange("p (s c) -> p s c", s=STEP),
                                 g_d[q * P:(q + 1) * P, :, bass.ds(c0, w // STEP)]).then_inc(g_in[u], 16)

            @block.sync
            def _(sp):
                sp.dma_start(gw[:], a["glu_w"][0].rearrange("(q p) n -> p q n", p=P)).then_inc(gw_in, 16)
                sp.dma_start(gb[:], a["glu_b"][0].rearrange("(q p) -> p q", p=P),
                             allow_slow_non_contiguous=True).then_inc(gb_in, 16)
                for u in range(2):
                    g_load(sp, u, u, BLK)
                for b in range(2, NBLK + 1):
                    sp.wait_ge(mo_done, 4 * (b - 1))
                    g_load(sp, b, b % 2, BLK if b < NBLK else TS)
                for u in range(2):
                    sp.wait_ge(mo_out[u], 16 * 2 * (NBLK + 1))

            @block.gpsimd
            def _(pool):
                w = a["w_out"][0].rearrange("(k p) n -> p k n", p=P)
                for i in range(WP):
                    if i >= 2:
                        pool.wait_ge(wo_l, i - 1)
                    pool.dma_start(wraw[:, i % 2], w[:, :, i * BLK // 2:(i + 1) * BLK // 2]).then_inc(wraw_in[i % 2], 16)

            def store(act, n):
                b, m = divmod(n, 4)
                w = BLK if b < NBLK else TS
                act.wait_ge(mo_done, n + 1)
                act.dma_start(mix_d[HALF + m * P:HALF + (m + 1) * P, b * BLK:b * BLK + w], mo[:, n % 2, 0:w]
                              ).then_inc(mo_out[n % 2], 16)

            @block.scalar
            def _(act):
                act.wait_ge(gw_in, 16)
                act.copy(gw_hi[:], gw[:]).then_inc(gw_h, 1)
                act.wait_ge(gb_in, 16)
                for b in range(NBLK + 1):
                    u, w = b % 2, BLK if b < NBLK else TS
                    act.wait_ge(g_in[u], 16 * QH * (b // 2 + 1))
                    if b >= 2:
                        act.wait_ge(g_mm, 4 * (b - 1))
                    act.copy(g_hi[:, u, :, 0:w], gf[:, u, :, 0:w]).then_inc(ghi, 1)
                    if b < WP:
                        act.wait_ge(wraw_in[b % 2], 16 * (b // 2 + 1))
                        act.copy(wo_hi[:, :, b * BLK // 2:(b + 1) * BLK // 2], wraw[:, b % 2]).then_inc(wo_h, 1)
                    for m in range(QH):
                        n = 4 * b + m
                        act.wait_ge(g_mm, n + 1)
                        if n >= 2:
                            act.wait_ge(mo_done, n - 1)
                        act.activation(sg[:, n % 2, 0:w], psG[:, n % 2, 0:w], ACT.Sigmoid,
                                       bias=gb[:, m:m + 1]).then_inc(sg_done, 1)
                        if n:
                            store(act, n - 1)
                store(act, 4 * NBLK + 3)

            @block.vector
            def _(dve):
                dve.wait_ge(gw_h, 1)
                dve.tensor_tensor(gw_lo[:], gw[:], gw_hi[:].bitcast(F32), ALU.subtract).then_inc(gw_l, 1)
                for b in range(NBLK + 1):
                    u, w = b % 2, BLK if b < NBLK else TS
                    dve.wait_ge(ghi, b + 1)
                    dve.tensor_tensor(g_lo[:, u, :, 0:w], gf[:, u, :, 0:w], g_hi[:, u, :, 0:w].bitcast(F32),
                                      ALU.subtract).then_inc(glo, 1)
                    if b < WP:
                        dve.wait_ge(wo_h, b + 1)
                        c = slice(b * BLK // 2, (b + 1) * BLK // 2)
                        dve.tensor_tensor(wo_lo[:, :, c], wraw[:, b % 2], wo_hi[:, :, c].bitcast(F32), ALU.subtract
                                          ).then_inc(wo_l, 1)
                    for m in range(QH):
                        n = 4 * b + m
                        dve.wait_ge(sg_done, n + 1)
                        if n >= 2:
                            dve.wait_ge(mo_out[n % 2], 16 * (n // 2))
                        dve.tensor_tensor(mo[:, n % 2, 0:w].rearrange("p (c s) -> p s c", s=STEP),
                                          gf[:, u, m, 0:w].rearrange("p (s c) -> p s c", s=STEP),
                                          sg[:, n % 2, 0:w].rearrange("p (s c) -> p s c", s=STEP),
                                          ALU.mult).then_inc(mo_done, 1)

            @block.tensor
            def _(pe):
                pe.wait_ge(gw_l, 1)
                for b in range(NBLK + 1):
                    u, w = b % 2, BLK if b < NBLK else TS
                    pe.wait_ge(glo, b + 1)
                    for m in range(QH):
                        n = 4 * b + m
                        if n >= 2:
                            pe.wait_ge(sg_done, n - 1)
                        for q in range(QH):
                            mm = matmul3(pe, psG[:, n % 2, 0:w], gw_hi[:, q, m * P:(m + 1) * P],
                                         gw_lo[:, q, m * P:(m + 1) * P], g_hi[:, u, q, 0:w], g_lo[:, u, q, 0:w],
                                         q == 0, q == QH - 1)
                        mm.then_inc(g_mm, 1)


def out_projection(k, a, mod_d, mix_d, x2_d, h2_d, wo_hi, wo_lo, lg):
    nc = k.nc
    k.stage = "out_projection"
    NR = 4 + NE
    with ExitStack() as st:
        mixf = k.sb(st, "mixf", [P, 2, KD, P])
        m_hi = k.sb(st, "m_hi", [P, 2, KD, P], F32R)
        m_lo = k.sb(st, "m_lo", [P, 2, KD, P], F32R)
        xt = k.sb(st, "xt", [P, 2, D])
        tmp = k.sb(st, "tmp4", [P, 2, D])
        h2 = k.sb(st, "h2", [P, 2, D])
        junk = k.sb(st, "junk4", [P, D])
        h2T = k.sb(st, "h2T", [P, KD, P])
        g1 = k.sb(st, "g1", [P, 2, D])
        sh2 = k.sb(st, "sh2", [P, 2, D])
        a2 = k.sb(st, "a2", [P, 2, D])
        n2 = k.sb(st, "n2", [P, D])
        rw = k.sb(st, "rw", [P, KD, NR])
        rb = k.sb(st, "rb", [P, NR])
        ss = k.sb(st, "ss4", [P, 2, 4])
        psO = k.ps(st, "psO", [P, 2, D])
        psH = k.ps(st, "psH", [P, D])
        psR = k.ps(st, "psR", [P, NR])
        (rows_in, rw_in, a2_done, mhi, mlo, o_mm, o_tmp, x2_done, sq, ms, rt, rstd, h2_half, h2_done, h_t, h_ev, r_mm,
         lg_done, mz) = [k.sem("o_" + n) for n in (
            "rows_in", "rw_in", "a2_done", "mhi", "mlo", "mm", "tmp", "x2_done", "sq", "ms", "rt", "rstd",
            "h2_half", "h2_done", "h_t", "h_ev", "r_mm", "lg_done", "mz")]
        m_in = [k.sem(f"m_in{i}") for i in range(2)]
        xt_in = [k.sem(f"xt_in{i}") for i in range(2)]
        xt_out = [k.sem(f"xt_out{i}") for i in range(2)]
        h2_out = [k.sem(f"h2_out{i}") for i in range(2)]
        LAST = NT - 1
        mixv = mix_d.rearrange("(k p) n -> p k n", p=P)
        x_s = a["x_sample"].rearrange("b t d -> (b t) d")

        with nc.Block() as block:

            @block.sync
            def _(sp):
                for i, (dst, c0) in enumerate(((g1, 2 * D), (sh2, 3 * D), (a2, 4 * D))):
                    sp.dma_start(dst[:, 0, :], mod_d[0:1, c0:c0 + D].broadcast_to([P, D])).then_inc(rows_in, 16)
                    sp.dma_start(dst[0:TS, 1, :], mod_d[1:ROWS, c0:c0 + D].unsqueeze(1)
                                 .broadcast_to([NSEQ, LSEQ, D])).then_inc(rows_in, 16)
                sp.dma_start(n2[:], a["norm2_g"].broadcast_to([P, D])).then_inc(rows_in, 16)
                sp.dma_start(rw[:, :, 0:4], a["router_w1"][0].rearrange("(k p) n -> p k n", p=P)).then_inc(rw_in, 16)
                for g in range(4):
                    sp.dma_start(rw[:, :, 4 + 4 * g:8 + 4 * g], a["router_w2"][0, g].rearrange("(k p) n -> p k n", p=P)
                                 ).then_inc(rw_in, 16)
                sp.dma_start(rb[:, 0:4], a["router_b1"].broadcast_to([P, 4])).then_inc(rw_in, 16)
                sp.dma_start(rb[:, 4:NR], a["router_b2"].rearrange("a g e -> a (g e)").broadcast_to([P, NE])
                             ).then_inc(rw_in, 16)

                def load(t, u):
                    c0 = t * P if isinstance(t, int) else sp.snap(t * P)
                    sp.dma_start(mixf[:, u], mixv[:, :, bass.ds(c0, P)]).then_inc(m_in[u], 16)
                    sp.dma_start(xt[:, u, :], a["x_prompt"][0, bass.ds(c0, P), :]).then_inc(xt_in[u], 16)

                def store(t, u, rows):
                    c0 = t * P if isinstance(t, int) else sp.snap(t * P)
                    sp.wait_ge(h2_done, t + 1)
                    sp.dma_start(x2_d[bass.ds(c0, rows), :], xt[0:rows, u, :]).then_inc(xt_out[u], 16)
                    sp.dma_start(h2_d[bass.ds(c0, rows), :], h2[0:rows, u, :]).then_inc(h2_out[u], 16)

                for u in range(2):
                    load(u, u)
                with sp.Fori(0, LAST - 3, 2) as t:
                    for u in range(2):
                        store(t + u, u, P)
                        sp.wait_ge(xt_out[u], 8 * t + 16)
                        sp.wait_ge(mlo, t + u + 1)
                        load(t + u + 2, u)
                store(LAST - 2, 0, P)
                sp.wait_ge(xt_out[0], 16 * (LAST // 2))
                sp.wait_ge(mlo, LAST - 1)
                sp.wait_ge(mz, 1)
                sp.dma_start(mixf[:, 0, :, 0:TS], mixv[:, :, TP:TOK]).then_inc(m_in[0], 16)
                sp.dma_start(xt[0:TS, 0, :], x_s).then_inc(xt_in[0], 16)
                store(LAST - 1, 1, P)
                store(LAST, 0, TS)
                for u in range(2):
                    sp.wait_ge(xt_out[u], 16 * ((NT + 1 - u) // 2))
                    sp.wait_ge(h2_out[u], 16 + 16 * ((NT + 1 - u) // 2))

            @block.scalar
            def _(act):
                def split_hi(t, u):
                    act.wait_ge(m_in[u], 8 * t + 16 - 8 * u)
                    if not isinstance(t, int) or t >= 1:
                        act.wait_ge(o_mm, t)
                    act.copy(m_hi[:, u], mixf[:, u]).then_inc(mhi, 1)

                def norm(t, u, rows):
                    act.wait_ge(x2_done, t + 1)
                    act.activation(junk[0:rows, :], xt[0:rows, u, :], ACT.Square,
                                   accum_out=ss[0:rows, u, 0:1]).then_inc(sq, 1)
                    act.wait_ge(ms, t + 1)
                    act.activation(ss[0:rows, u, 2:3], ss[0:rows, u, 1:2], ACT.Sqrt).then_inc(rt, 1)

                def turned(t, u, rows):
                    act.wait_ge(h_t, t + 1)
                    act.wait_ge(r_mm, t + 1)
                    act.copy(h2T[:, :, 0:rows], psH[:].rearrange("p (k n) -> p k n", k=KD)[:, :, 0:rows]
                             ).then_inc(h_ev, 1)

                split_hi(0, 0)
                with act.Fori(0, LAST - 3, 2) as t:
                    for u in range(2):
                        split_hi(t + u + 1, 1 - u)
                        norm(t + u, u, P)
                        turned(t + u, u, P)
                split_hi(LAST - 1, 1)
                norm(LAST - 2, 0, P)
                turned(LAST - 2, 0, P)
                split_hi(LAST, 0)
                norm(LAST - 1, 1, P)
                turned(LAST - 1, 1, P)
                norm(LAST, 0, TS)
                turned(LAST, 0, TS)

            @block.vector
            def _(dve):
                tt = dve.tensor_tensor
                dve.wait_ge(rows_in, 16 * 7)
                for i, r in ((0, P), (1, TS)):
                    dve.scalar_tensor_tensor(out=a2[0:r, i, :], in0=a2[0:r, i, :], scalar=1.0, in1=n2[0:r, :],
                                             op0=ALU.add, op1=ALU.mult).then_inc(a2_done, 1)
                dve.wait_ge(rw_in, 16 * 7)
                dve.memset(lg[:, LAST, :], 0.0).then_inc(a2_done, 1)
                dve.wait_ge(a2_done, 3)

                def split_lo(t, u):
                    dve.wait_ge(mhi, t + 1)
                    tt(m_lo[:, u], mixf[:, u], m_hi[:, u].bitcast(F32), ALU.subtract).then_inc(mlo, 1)

                def tile(t, u, rows, kind):
                    dve.wait_ge(o_mm, t + 1 + 1)
                    dve.wait_ge(xt_in[u], 8 * t + 16 - 8 * u)
                    r = slice(0, rows)
                    tt(tmp[r, u, :], psO[r, u, :], g1[r, kind, :], ALU.mult).then_inc(o_tmp, 1)
                    dve.wait_ge(o_tmp, t + 1)
                    tt(xt[r, u, :], xt[r, u, :], tmp[r, u, :], ALU.add).then_inc(x2_done, 1)
                    dve.wait_ge(sq, t + 1)
                    dve.tensor_scalar(ss[r, u, 1:2], ss[r, u, 0:1], 1.0 / D, EPS, ALU.mult, ALU.add).then_inc(ms, 1)
                    dve.wait_ge(rt, t + 1)
                    dve.reciprocal(ss[r, u, 3:4], ss[r, u, 2:3]).then_inc(rstd, 1)
                    dve.wait_ge(rstd, t + 1)
                    dve.wait_ge(h2_out[u], 8 * t + 16 - 8 * u)
                    dve.scalar_tensor_tensor(out=tmp[r, u, :], in0=xt[r, u, :], scalar=ss[r, u, 3:4],
                                             in1=a2[r, kind, :], op0=ALU.mult, op1=ALU.mult).then_inc(h2_half, 1)
                    dve.wait_ge(h2_half, t + 1)
                    tt(h2[r, u, :], tmp[r, u, :], sh2[r, kind, :], ALU.add).then_inc(h2_done, 1)
                    dve.wait_ge(r_mm, t + 1 + 1)
                    tt(lg[r, bass.ds(t, 1), :].rearrange("p a n -> p (a n)") if not isinstance(t, int) else lg[r, t, :],
                       psR[r, :], rb[r, :], ALU.add).then_inc(lg_done, 1)

                for u in range(2):
                    dve.sem_inc(h2_out[u], 16)
                split_lo(0, 0)
                with dve.Fori(0, LAST - 3, 2) as t:
                    for u in range(2):
                        split_lo(t + u + 1, 1 - u)
                        tile(t + u, u, P, 0)
                split_lo(LAST - 1, 1)
                dve.wait_ge(mlo, LAST - 1)
                dve.memset(mixf[:, 0, :, TS:P], 0.0).then_inc(mz, 1)
                tile(LAST - 2, 0, P, 0)
                split_lo(LAST, 0)
                tile(LAST - 1, 1, P, 0)
                tile(LAST, 0, TS, 1)

            @block.tensor
            def _(pe):
                pe.sem_inc(o_mm, 1)
                pe.sem_inc(r_mm, 1)
                pe.wait_ge(rw_in, 16 * 7)

                def product(t, u):
                    pe.wait_ge(mlo, t + 1)
                    if not isinstance(t, int) or t >= 2:
                        pe.wait_ge(o_tmp, t - 1)
                    for n in range(2):
                        for q in range(KD):
                            c = slice(n * BLK, (n + 1) * BLK)
                            mm = matmul3(pe, psO[:, u, c], m_hi[:, u, q, :], m_lo[:, u, q, :], wo_hi[:, q, c],
                                         wo_lo[:, q, c], q == 0, q == KD - 1)
                    mm.then_inc(o_mm, 1)

                def route(t, u, rows):
                    pe.wait_ge(h2_done, t + 1)
                    for q in range(KD):
                        mm = pe.transpose(psH[:, q * P:q * P + rows], h2[0:rows, u, q * P:(q + 1) * P],
                                          k.ident[0:rows, 0:rows])
                    mm.then_inc(h_t, 1)
                    pe.wait_ge(h_ev, t + 1)
                    if not isinstance(t, int) or t >= 1:
                        pe.wait_ge(lg_done, t)
                    for q in range(KD):
                        mm = pe.matmul(psR[0:rows, :], h2T[:, q, 0:rows], rw[:, q, :], start=q == 0, stop=q == KD - 1)
                    mm.then_inc(r_mm, 1)

                product(0, 0)
                product(1, 1)
                route(0, 0, P)
                with pe.Fori(1, LAST - 2, 2) as t:
                    for u in (1, 0):
                        d = 1 - u
                        product(t + d + 1, 1 - u)
                        route(t + d, u, P)
                product(LAST, 0)
                route(LAST - 1, 1, P)
                route(LAST, 0, TS)


NCOL = 52


def routing(k, lg, R):
    nc = k.nc
    k.stage = "routing"
    with ExitStack() as st:
        sb = lambda n, s, d=F32: k.sb(st, n, s, d)
        W = NT * NE
        io_i = sb("io_i", [P, P], I32)
        tk_i = sb("tk_i", [P, NT], I32)
        io_f = sb("io_f", [P, P])
        tk_f = sb("tk_f", [P, NT])
        ones = sb("ones", [P, P])
        upper = sb("upper", [P, P])
        prio = sb("prio", [P, 4])
        m1 = sb("m1", [P, NT])
        ex = sb("ex", [P, NT, 4])
        sm = sb("sm", [P, NT])
        ptop = sb("ptop", [P, NT])
        key = sb("key", [P, NT, 4])
        km = sb("km", [P, NT])
        ohg = sb("ohg", [P, NT, 4])
        l2s = sb("l2s", [P, NT, 4, 4])
        l2 = sb("l2", [P, NT, 4])
        oh = sb("oh", [P, 2, NT, 4])
        v = sb("v", [P, 2, NT])
        msk = sb("msk", [P, NT, 4])
        gt = sb("gt", [P, NT, 2])
        E = sb("E", [P, 2, NT, 4, 4])
        M = sb("M", [P, NT, NE])
        pre = sb("pre", [P, NT + 1, NE])
        base = sb("base", [P, NT, NE])
        n_i = sb("n_i", [P, NE], I32)
        n_f = sb("n_f", [P, NE])
        pz = sb("pz", [P, 2, 2 * NE])
        st_f = sb("st_f", [P, NE])
        pe_f = sb("pe_f", [P, 2, NT, NE])
        posf = sb("posf", [P, NT, 2])
        col_i = sb("col_i", [P, NT, 2], I32)
        row_i = sb("row_i", [P, NT, 2], I32)
        col_f = sb("col_f", [P, NT, 2])
        row_f = sb("row_f", [P, NT, 2])
        J = sb("J", [P, NT, 2, P])
        A = sb("A", [P, 2, NT, 2, NCOL])
        te = sb("te", [1, NCOL, NE])
        tf = sb("tf", [1, 2, NCOL])
        t_i = sb("t_i", [1, 1], I32)
        tl_f = sb("tl_f", [1, 1])
        psR = k.ps(st, "psRank", [P, W])
        psT = k.ps(st, "psTot", [P, W])
        psS = k.ps(st, "psSlot", [P, 2 * NCOL])
        c, con, ex_done, choices, rank_mm, slots_ready, slot_mm, mx = [k.sem("r_" + n) for n in (
            "chain", "con", "ex_done", "choices", "rank_mm", "slots_ready", "slot_mm", "mx")]

        with nc.Block() as block:

            @block.gpsimd
            def _(pool):
                pool.iota(io_i[:], [[1, P]], base=0, channel_multiplier=0).then_inc(con, 1)
                pool.iota(tk_i[:], [[P, NT]], base=0, channel_multiplier=1).then_inc(con, 1)
                pool.memset(ones[:], 1.0).then_inc(con, 1)
                pool.wait_ge(con, 3)
                pool.affine_select(out=upper[:], in_=ones[:], compare_op=ALU.is_gt, fill=0.0, base=0,
                                   pattern=[[1, P]], channel_multiplier=-1).then_inc(con, 1)

            @block.scalar
            def _(act):
                act.wait_ge(mx, 1)
                act.activation(ex[:], key[:], ACT.Exp).then_inc(ex_done, 1)
                act.wait_ge(mx, 2)
                act.activation(v[:, 1, :], v[:, 1, :], ACT.Exp).then_inc(ex_done, 1)

            @block.vector
            def _(dve):
                ch = Chain(dve, c)
                tt = lambda o, x, y, op: ch.link(dve.tensor_tensor(o, x, y, op))
                ts = lambda o, x, s1, s2, o1, *o2: ch.link(dve.tensor_scalar(o, x, s1, s2, o1, *o2))
                cp = lambda o, x: ch.link(dve.tensor_copy(o, x))
                red = lambda o, x, op: ch.link(dve.tensor_reduce(o, x, AX_X, op))
                b4 = lambda x: x.unsqueeze(2).broadcast_to([P, NT, 4])
                dve.wait_ge(con, 4)
                cp(io_f[:], io_i[:])
                cp(tk_f[:], tk_i[:])
                ch.link(dve.memset(tk_f[TS:P, NT - 1:NT], 0.0))
                ts(prio[:], io_f[:, 0:4], -1.0, 4.0, ALU.mult, ALU.add)
                pr = prio[:].unsqueeze(1).broadcast_to([P, NT, 4])

                def first_max(oh_out, x, m):
                    red(m, x, ALU.max)
                    tt(key[:], x, b4(m), ALU.is_equal)
                    tt(key[:], key[:], pr, ALU.mult)
                    red(km[:], key[:], ALU.max)
                    tt(oh_out, key[:], b4(km[:]), ALU.is_equal)

                g4 = lg[:, :, 0:4]
                first_max(ohg[:], g4, m1[:])
                dve.tensor_tensor(key[:], g4, b4(m1[:]), ALU.subtract).then_inc(mx, 1)
                dve.wait_ge(ex_done, 1)
                red(sm[:], ex[:], ALU.add)
                ch.link(dve.reciprocal(ptop[:], sm[:]))
                tt(l2s[:], lg[:, :, 4:20].rearrange("p t (g e) -> p t g e", g=4),
                   ohg[:].unsqueeze(3).broadcast_to([P, NT, 4, 4]), ALU.mult)
                red(l2[:], l2s[:].rearrange("p t g e -> p t e g"), ALU.add)
                first_max(oh[:, 0], l2[:], v[:, 0, :])
                ts(msk[:], oh[:, 0], -1.0, 1.0, ALU.mult, ALU.add)
                tt(msk[:], msk[:], l2[:], ALU.mult)
                ts(key[:], oh[:, 0], -3.0e38, None, ALU.mult)
                tt(msk[:], msk[:], key[:], ALU.add)
                first_max(oh[:, 1], msk[:], v[:, 1, :])
                dve.tensor_tensor(v[:, 1, :], v[:, 1, :], v[:, 0, :], ALU.subtract).then_inc(mx, 1)
                for i in range(2):
                    tt(E[:, i], ohg[:].unsqueeze(3).broadcast_to([P, NT, 4, 4]),
                       oh[:, i].unsqueeze(2).broadcast_to([P, NT, 4, 4]), ALU.mult)
                    ch.link(dve.memset(E[TS:P, i, NT - 1:NT], 0.0))
                Ef = [E[:, i].rearrange("p t g e -> p t (g e)") for i in range(2)]
                dve.tensor_tensor(M[:], Ef[0], Ef[1], ALU.add).then_inc(choices, 1)
                dve.wait_ge(ex_done, 2)
                ts(sm[:], v[:, 1, :], 1.0, None, ALU.add)
                ch.link(dve.reciprocal(sm[:], sm[:]))
                tt(gt[:, :, 0:1].rearrange("p t a -> p (t a)"), sm[:], ptop[:], ALU.mult)
                tt(gt[:, :, 1:2].rearrange("p t a -> p (t a)"), gt[:, :, 0:1].rearrange("p t a -> p (t a)"),
                   v[:, 1, :], ALU.mult)
                ch.link(dve.memset(gt[TS:P, NT - 1:NT, :], 0.0))
                ch.link(dve.memset(pre[:, 0, :], 0.0))
                dve.wait_ge(rank_mm, 1)
                for t in range(NT):
                    tt(pre[:, t + 1, :], pre[:, t, :], psT[:, t * NE:(t + 1) * NE], ALU.add)
                ts(n_f[:], pre[:, NT, :], float(P - 1), None, ALU.add)
                cp(n_i[:], n_f[:])
                ts(n_i[:], n_i[:], 7, None, ALU.arith_shift_right)
                cp(n_f[:], n_i[:])
                ts(n_f[:], n_f[:], 1.0, None, ALU.max)
                ch.link(dve.memset(pz[:], 0.0))
                cp(pz[:, 0, NE:], n_f[:])
                for i in range(4):
                    tt(pz[:, 1 - i % 2, NE:], pz[:, i % 2, NE:], pz[:, i % 2, NE - 2 ** i:2 * NE - 2 ** i], ALU.add)
                end_f = pz[:, 0, NE:]
                tt(st_f[:], end_f, n_f[:], ALU.subtract)
                ts(n_f[:], st_f[:], float(P), None, ALU.mult)
                tt(base[:], pre[:, 0:NT, :], psR[:].rearrange("p (t e) -> p t e", e=NE), ALU.add)
                tt(base[:], base[:], n_f[:].unsqueeze(1).broadcast_to([P, NT, NE]), ALU.add)
                for i in range(2):
                    tt(pe_f[:, i], Ef[i], base[:], ALU.mult)
                    red(posf[:, :, i:i + 1].rearrange("p t a -> p (t a)"), pe_f[:, i], ALU.add)
                cp(R.pos[:], posf[:])
                ts(col_i[:], R.pos[:], 7, None, ALU.arith_shift_right)
                ts(row_i[:], R.pos[:], P - 1, None, ALU.bitwise_and)
                cp(col_f[:], col_i[:])
                cp(row_f[:], row_i[:])
                b2 = lambda x, n: x.unsqueeze(3).broadcast_to([P, NT, 2, n])
                tt(J[:], b2(row_f[:], P), io_f[:].unsqueeze(1).unsqueeze(1).broadcast_to([P, NT, 2, P]), ALU.is_equal)
                tt(A[:, 1], b2(col_f[:], NCOL), io_f[:, 0:NCOL].unsqueeze(1).unsqueeze(1)
                   .broadcast_to([P, NT, 2, NCOL]), ALU.is_equal)
                tt(A[:, 0], A[:, 1], tk_f[:].unsqueeze(2).unsqueeze(2).broadcast_to([P, NT, 2, NCOL]), ALU.mult)
                dve.tensor_tensor(A[:, 1], A[:, 1], b2(gt[:], NCOL), ALU.mult).then_inc(slots_ready, 1)
                cp(t_i[:], end_f[0:1, NE - 1:NE])
                ts(R.tab[0:1, 0:1], t_i[:], 1, 1, ALU.arith_shift_right, ALU.logical_shift_left)
                cp(tl_f[:], R.tab[0:1, 0:1])
                ts(tl_f[:], tl_f[:], -1.0, float(MAXT + 1), ALU.mult, ALU.add)
                cp(R.tab[0:1, 1 + 2 * NCOL:], tl_f[:])
                io3 = io_f[0:1, 0:NCOL].unsqueeze(2).broadcast_to([1, NCOL, NE])
                tt(te[:], io3, end_f[0:1, :].unsqueeze(1).broadcast_to([1, NCOL, NE]), ALU.is_ge)
                red(tf[:, 0, :], te[:], ALU.add)
                ts(tf[:, 0, :], tf[:, 0, :], float(NE - 1), None, ALU.min)
                tt(te[:], io3, st_f[0:1, :].unsqueeze(1).broadcast_to([1, NCOL, NE]), ALU.is_equal)
                red(tf[:, 1, :], te[:, :, 0:NE - 1], ALU.add)
                cp(R.tab[0:1, 1:1 + 2 * NCOL], tf[:].rearrange("p a n -> p (a n)"))
                dve.wait_ge(slot_mm, 1)
                cp(R.idx[:], psS[:, 0:NCOL])
                cp(R.gate[:], psS[:, NCOL:2 * NCOL])

            @block.tensor
            def _(pe):
                pe.wait_ge(choices, 1)
                Mf = M[:].rearrange("p t e -> p (t e)")
                pe.matmul(psT[:], ones[:], Mf, start=True, stop=True)
                pe.matmul(psR[:], upper[:], Mf, start=True, stop=True).then_inc(rank_mm, 1)
                pe.wait_ge(slots_ready, 1)
                for t in range(NT):
                    for i in range(2):
                        mm = pe.matmul(psS[:], J[:, t, i, :], A[:, :, t, i, :],
                                       start=t == 0 and i == 0, stop=t == NT - 1 and i == 1)
                mm.then_inc(slot_mm, 1)


def experts(k, a, h2_d, o_d, R):
    nc = k.nc
    k.stage = "experts"
    FQ = FH // P
    with ExitStack() as st:
        wraw = k.sb(st, "we_raw", [P, 2, KD, 2 * FH])
        draw = k.sb(st, "wd_raw", [P, 2, FQ, D])
        w_hi = k.sb(st, "we_hi", [P, 2, KD, 2 * FH], F32R)
        w_lo = k.sb(st, "we_lo", [P, 2, KD, 2 * FH], F32R)
        d_hi = k.sb(st, "wd_hi", [P, 2, FQ, D], F32R)
        d_lo = k.sb(st, "wd_lo", [P, 2, FQ, D], F32R)
        xg = k.sb(st, "xg", [P, 2, D])
        x_hi = k.sb(st, "x_hi", [P, 2, KD, P], F32R)
        x_lo = k.sb(st, "x_lo", [P, 2, KD, P], F32R)
        sg = k.sb(st, "sg_e", [P, FH])
        hid = k.sb(st, "hid", [P, 2, FH])
        t_hi = k.sb(st, "hT_hi", [P, FQ, P], F32R)
        t_lo = k.sb(st, "hT_lo", [P, FQ, P], F32R)
        osb = k.sb(st, "o_sb", [P, 2, D])
        ic = k.sb(st, "idx_col", [P, 2, 1], I32)
        psG = k.ps(st, "psGU", [P, 2, 2 * FH])
        psX = k.ps(st, "psX", [P, D])
        psH = k.ps(st, "psHT", [P, FQ * P])
        psD = k.ps(st, "psD", [P, D])
        (raw_ok, whi, wlo, ic_ok, fence, xt_ps, xhi, xlo, gu_mm, sg_ok, hid_ok, ht_ps, hthi, htlo, d_mm, oev_a,
         oev_v, fill, ends) = [k.sem("e_" + n) for n in (
            "raw_ok", "whi", "wlo", "ic_ok", "fence", "xt_ps", "xhi", "xlo", "gu_mm", "sg_ok", "hid_ok", "ht_ps",
            "hthi", "htlo", "d_mm", "oev_a", "oev_v", "fill", "ends")]
        raw_in = [k.sem(f"we_in{i}") for i in range(2)]
        xg_in = [k.sem(f"xg_in{i}") for i in range(2)]
        o_out = [k.sem(f"o_out{i}") for i in range(2)]
        FIRST = 1 + NCOL

        def last_tile(eng):
            return eng.value_load(R.tab[0:1, 0:1], min_val=NE, max_val=MAXT)

        def expert_of(eng, t):
            return eng.value_load(R.tab[0:1, bass.ds(t + 1, 1)], min_val=0, max_val=NE - 1)

        with nc.Block() as block:

            @block.sync
            def _(sp):
                def load(e):
                    u = e % 2
                    sp.dma_start(wraw[:, u, :, 0:FH], a["exp_w_gate"][0, e].rearrange("(k p) f -> p k f", p=P)
                                 ).then_inc(raw_in[u], 16)
                    sp.dma_start(wraw[:, u, :, FH:2 * FH], a["exp_w_up"][0, e].rearrange("(k p) f -> p k f", p=P)
                                 ).then_inc(raw_in[u], 16)
                    sp.dma_start(draw[:, u], a["exp_w_down"][0, e].rearrange("(k p) d -> p k d", p=P)
                                 ).then_inc(raw_in[u], 16)
                load(0)
                load(1)
                for e in range(NE):
                    sp.wait_ge(raw_in[e % 2], 48 * (e // 2 + 1))
                    sp.sem_inc(raw_ok, 1)
                    if e + 2 < NE:
                        sp.wait_ge(wlo, e + 1)
                        load(e + 2)
                n = last_tile(sp) + 1
                with sp.Fori(n, MAXT + 2, 1) as t:
                    sp.dma_start(o_d[bass.ds(sp.snap(t * P), P), :], h2_d[0:P, :]).then_inc(fill, 16)
                left = sp.value_load(R.tab[0:1, 1 + 2 * NCOL:], min_val=1, max_val=MAXT + 2)
                sp.wait_ge(fill, left * 16)
                sp.sem_inc(ends, 1)

            @block.gpsimd
            def _(pool):
                last = last_tile(pool)

                def gather(t, u):
                    if not isinstance(t, int):
                        pool.wait_ge(xt_ps, t - 1)
                    pool.tensor_copy(ic[:, u, :], R.idx[:, bass.ds(t, 1)]).then_inc(ic_ok, 1)
                    pool.wait_ge(ic_ok, t + 1)
                    pool.sem_inc(fence, 1)
                    pool.indirect_dma_start(xg[:, u, :], None, h2_d, bass.IndirectOffsetOnAxis(ic[:, u, :], 0)
                                            ).then_inc(xg_in[u], 16)
                gather(0, 0)
                gather(1, 1)
                with pool.Fori(2, last + 1, 2) as t:
                    for d in range(2):
                        gather(t + d, d)

            @block.scalar
            def _(act):
                last = last_tile(act)
                for u in range(2):
                    act.sem_inc(o_out[u], 16)

                def split(e):
                    if isinstance(e, int):
                        u = slice(e % 2, e % 2 + 1)
                    else:
                        u = bass.ds(act.snap(e & 1), 1)
                    act.wait_ge(raw_ok, e + 1)
                    act.copy(w_hi[:, u], wraw[:, u])
                    act.copy(d_hi[:, u], draw[:, u]).then_inc(whi, 1)

                def x_hi_of(t, u):
                    act.wait_ge(xt_ps, t + 1)
                    act.copy(x_hi[:, u], psX[:].rearrange("p (k n) -> p k n", k=KD)).then_inc(xhi, 1)

                def silu(t, u):
                    act.wait_ge(gu_mm, t + 1)
                    if not isinstance(t, int):
                        act.wait_ge(hid_ok, t)
                    act.activation(sg[:], psG[:, u, 0:FH], ACT.Silu).then_inc(sg_ok, 1)

                def hidden_hi(t):
                    act.wait_ge(ht_ps, t + 1)
                    if not isinstance(t, int):
                        act.wait_ge(d_mm, t)
                    act.copy(t_hi[:], psH[:].rearrange("p (k n) -> p k n", k=FQ)).then_inc(hthi, 1)

                def out(t, u):
                    act.wait_ge(d_mm, t + 1)
                    act.wait_ge(o_out[u], 8 * t + 16 - 8 * u)
                    act.copy(osb[:, u, 0:BLK], psD[:, 0:BLK]).then_inc(oev_a, 1)
                    act.wait_ge(oev_a, t + 1)
                    act.wait_ge(oev_v, t + 1)
                    act.dma_start(o_d[bass.ds(act.snap(t * P), P), :], osb[:, u, :]).then_inc(o_out[u], 16)

                split(0)
                x_hi_of(0, 0)
                silu(0, 0)
                x_hi_of(1, 1)
                split(1)
                with act.Fori(1, last + 1, 2) as t:
                    for d in range(2):
                        u = 1 - d
                        s = t + d
                        silu(s, u)
                        hidden_hi(s - 1)
                        x_hi_of(s + 1, 1 - u)
                        out(s - 1, 1 - u)
                        first = act.value_load(R.tab[0:1, bass.ds(s + FIRST, 1)], min_val=0, max_val=1)
                        with act.If(first > 0):
                            split(expert_of(act, s) + 1)
                hidden_hi(last)
                out(last, 0)
                act.wait_ge(o_out[0], last * 8 + 32)
                act.wait_ge(o_out[1], last * 8 + 16)
                act.sem_inc(ends, 1)

            @block.vector
            def _(dve):
                last = last_tile(dve)

                def split(e):
                    if isinstance(e, int):
                        u = slice(e % 2, e % 2 + 1)
                    else:
                        u = bass.ds(dve.snap(e & 1), 1)
                    dve.wait_ge(whi, e + 1)
                    dve.tensor_tensor(w_lo[:, u], wraw[:, u], w_hi[:, u].bitcast(F32), ALU.subtract)
                    dve.tensor_tensor(d_lo[:, u], draw[:, u], d_hi[:, u].bitcast(F32), ALU.subtract).then_inc(wlo, 1)

                def x_lo_of(t, u):
                    dve.wait_ge(xhi, t + 1)
                    dve.tensor_tensor(x_lo[:, u], psX[:].rearrange("p (k n) -> p k n", k=KD), x_hi[:, u].bitcast(F32),
                                      ALU.subtract).then_inc(xlo, 1)

                def hidden(t, u):
                    dve.wait_ge(sg_ok, t + 1)
                    dve.scalar_tensor_tensor(out=hid[:, u, :], in0=sg[:], scalar=R.gate[:, bass.ds(t, 1)],
                                             in1=psG[:, u, FH:2 * FH], op0=ALU.mult, op1=ALU.mult
                                             ).then_inc(hid_ok, 1)

                def hidden_lo(t):
                    dve.wait_ge(hthi, t + 1)
                    dve.tensor_tensor(t_lo[:], psH[:].rearrange("p (k n) -> p k n", k=FQ), t_hi[:].bitcast(F32),
                                      ALU.subtract).then_inc(htlo, 1)

                def out(t, u):
                    dve.wait_ge(d_mm, t + 1)
                    dve.wait_ge(o_out[u], 8 * t + 16 - 8 * u)
                    dve.tensor_copy(osb[:, u, BLK:D], psD[:, BLK:D]).then_inc(oev_v, 1)

                split(0)
                x_lo_of(0, 0)
                hidden(0, 0)
                x_lo_of(1, 1)
                split(1)
                with dve.Fori(1, last + 1, 2) as t:
                    for d in range(2):
                        u = 1 - d
                        s = t + d
                        hidden(s, u)
                        hidden_lo(s - 1)
                        x_lo_of(s + 1, 1 - u)
                        out(s - 1, 1 - u)
                        first = dve.value_load(R.tab[0:1, bass.ds(s + FIRST, 1)], min_val=0, max_val=1)
                        with dve.If(first > 0):
                            split(expert_of(dve, s) + 1)
                hidden_lo(last)
                out(last, 0)

            @block.tensor
            def _(pe):
                last = last_tile(pe)

                def turn(t, u):
                    pe.wait_ge(xg_in[u], 8 * t + 16 - 8 * u)
                    if not isinstance(t, int) or t >= 1:
                        pe.wait_ge(xlo, t)
                    for q in range(KD):
                        mm = pe.transpose(psX[:, q * P:(q + 1) * P], xg[:, u, q * P:(q + 1) * P], k.ident[:])
                    mm.then_inc(xt_ps, 1)

                def gate_up(t, u, e):
                    w = slice(e, e + 1) if isinstance(e, int) else bass.ds(pe.snap(e & 1), 1)
                    pe.wait_ge(wlo, e + 1)
                    pe.wait_ge(xlo, t + 1)
                    if not isinstance(t, int) :
                        pe.wait_ge(hid_ok, t - 1)
                    for q in range(KD):
                        mm = matmul3(pe, psG[:, u, :], x_hi[:, u, q, :], x_lo[:, u, q, :],
                                     w_hi[:, w, q, :].rearrange("p a n -> p (a n)"),
                                     w_lo[:, w, q, :].rearrange("p a n -> p (a n)"), q == 0, q == KD - 1)
                    mm.then_inc(gu_mm, 1)

                def turn_hidden(t, u):
                    pe.wait_ge(hid_ok, t + 1)
                    if not isinstance(t, int):
                        pe.wait_ge(htlo, t)
                    for q in range(FQ):
                        mm = pe.transpose(psH[:, q * P:(q + 1) * P], hid[:, u, q * P:(q + 1) * P], k.ident[:])
                    mm.then_inc(ht_ps, 1)

                def down(t, e):
                    w = slice(e, e + 1) if isinstance(e, int) else bass.ds(pe.snap(e & 1), 1)
                    pe.wait_ge(htlo, t + 1)
                    if not isinstance(t, int):
                        pe.wait_ge(oev_a, t)
                        pe.wait_ge(oev_v, t)
                    for c in range(2):
                        for q in range(FQ):
                            cs = slice(c * BLK, (c + 1) * BLK)
                            mm = matmul3(pe, psD[:, cs], t_hi[:, q, :], t_lo[:, q, :],
                                         d_hi[:, w, q, cs].rearrange("p a n -> p (a n)"),
                                         d_lo[:, w, q, cs].rearrange("p a n -> p (a n)"), q == 0, q == FQ - 1)
                    mm.then_inc(d_mm, 1)

                turn(0, 0)
                gate_up(0, 0, 0)
                turn(1, 1)
                with pe.Fori(1, last + 1, 2) as t:
                    for d in range(2):
                        u = 1 - d
                        s = t + d
                        gate_up(s, u, expert_of(pe, s))
                        turn_hidden(s - 1, 1 - u)
                        turn(s + 1, 1 - u)
                        down(s - 1, expert_of(pe, s - 1))
                turn_hidden(last, 0)
                down(last, expert_of(pe, last))


def combine(k, a, o, x2_d, o_d, mod_d, pos):
    nc = k.nc
    k.stage = "combine"
    LAST = NT - 1
    NB = 4
    with ExitStack() as st:
        x2 = k.sb(st, "x2", [P, NB, D])
        r1 = k.sb(st, "r1", [P, NB, D])
        r2 = k.sb(st, "r2", [P, NB, D])
        y = k.sb(st, "y", [P, NB, D])
        g2 = k.sb(st, "g2", [P, 2, D])
        gn = k.sb(st, "gn", [P, D])
        junk = k.sb(st, "junk6", [P, D])
        ss = k.sb(st, "ss6", [P, NT, 4])
        rows_in, sum1, gated, x3, sq, ms, rt, y_done, rstd = [k.sem("c_" + n) for n in (
            "rows_in", "sum1", "gated", "x3", "sq", "ms", "rt", "y_done", "rstd")]
        x_in = [k.sem(f"cx_in{i}") for i in range(NB)]
        r_in = [k.sem(f"cr_in{i}") for i in range(NB)]
        y_out = [k.sem(f"fin_out{i}") for i in range(NB)]

        with nc.Block() as block:

            @block.sync
            def _(sp):
                sp.dma_start(g2[:, 0, :], mod_d[0:1, 5 * D:6 * D].broadcast_to([P, D])).then_inc(rows_in, 16)
                sp.dma_start(g2[0:TS, 1, :], mod_d[1:ROWS, 5 * D:6 * D].unsqueeze(1).broadcast_to([NSEQ, LSEQ, D])
                             ).then_inc(rows_in, 16)
                sp.dma_start(gn[:], a["final_norm_g"].unsqueeze(0).broadcast_to([P, D])).then_inc(rows_in, 16)
                y_s = o["y_sample"].rearrange("b t d -> (b t) d")
                for t in range(NT + NB):
                    if t < NT:
                        u, rows = t % NB, P if t < LAST else TS
                        if t >= NB:
                            sp.wait_ge(x3, t - NB + 1)
                        sp.dma_start(x2[0:rows, u, :], x2_d[t * P:t * P + rows, :]).then_inc(x_in[u], 16)
                    s = t - NB
                    if s >= 0:
                        sp.wait_ge(y_done, s + 1)
                        u, rows = s % NB, P if s < LAST else TS
                        dst = o["y_prompt"][0, s * P:(s + 1) * P, :] if s < LAST else y_s
                        sp.dma_start(dst, y[0:rows, u, :]).then_inc(y_out[u], 16)
                for u in range(NB):
                    sp.wait_ge(y_out[u], 16 * ((NT - 1 - u) // NB + 1))

            @block.gpsimd
            def _(pool):
                for t in range(NT):
                    u, rows = t % NB, P if t < LAST else TS
                    if t >= NB:
                        pool.wait_ge(sum1, t - NB + 1)
                    for i, r in enumerate((r1, r2)):
                        pool.indirect_dma_start(r[0:rows, u, :], None, o_d,
                                                bass.IndirectOffsetOnAxis(pos[0:rows, t, i:i + 1], 0)
                                                ).then_inc(r_in[u], 16)

            @block.scalar
            def _(act):
                for t in range(NT):
                    u, rows = t % NB, P if t < LAST else TS
                    act.wait_ge(x3, t + 1)
                    act.activation(junk[0:rows, :], y[0:rows, u, :], ACT.Square, accum_out=ss[0:rows, t, 0:1]
                                   ).then_inc(sq, 1)
                    act.wait_ge(ms, t + 1)
                    act.activation(ss[0:rows, t, 2:3], ss[0:rows, t, 1:2], ACT.Sqrt).then_inc(rt, 1)

            @block.vector
            def _(dve):
                dve.wait_ge(rows_in, 48)
                tt = dve.tensor_tensor

                def add(t):
                    u, kind, r = t % NB, int(t == LAST), slice(0, P if t < LAST else TS)
                    n = t // NB + 1
                    dve.wait_ge(r_in[u], 32 * n)
                    if t >= NB:
                        dve.wait_ge(y_out[u], 16 * (n - 1))
                    tt(y[r, u, :], r1[r, u, :], r2[r, u, :], ALU.add).then_inc(sum1, 1)
                    dve.wait_ge(sum1, t + 1)
                    tt(y[r, u, :], y[r, u, :], g2[r, kind, :], ALU.mult).then_inc(gated, 1)
                    dve.wait_ge(gated, t + 1)
                    dve.wait_ge(x_in[u], 16 * n)
                    tt(y[r, u, :], y[r, u, :], x2[r, u, :], ALU.add).then_inc(x3, 1)

                def scale(t):
                    u, r = t % NB, slice(0, P if t < LAST else TS)
                    dve.wait_ge(sq, t + 1)
                    dve.tensor_scalar(ss[r, t, 1:2], ss[r, t, 0:1], 1.0 / D, EPS, ALU.mult, ALU.add).then_inc(ms, 1)
                    dve.wait_ge(rt, t + 1)
                    dve.reciprocal(ss[r, t, 3:4], ss[r, t, 2:3]).then_inc(rstd, 1)
                    dve.wait_ge(rstd, t + 1)
                    dve.scalar_tensor_tensor(out=y[r, u, :], in0=y[r, u, :], scalar=ss[r, t, 3:4], in1=gn[r, :],
                                             op0=ALU.mult, op1=ALU.mult).then_inc(y_done, 1)

                for t in range(NT + 1):
                    if t < NT:
                        add(t)
                    if t:
                        scale(t - 1)


class Routed:

    def __init__(self, k, st):
        self.pos = k.sb(st, "pos", [P, NT, 2], I32)
        self.tab = k.sb(st, "tab", [1, 2 + 2 * NCOL], I32)
        self.idx = k.sb(st, "idx", [P, NCOL], I32)
        self.gate = k.sb(st, "gate", [P, NCOL])


def hybrid_step(nc, a, o):
    with ExitStack() as s0:
        k = Core(nc, s0)
        k.ident = k.sb(s0, "ident", [P, P])
        k.cT = k.sb(s0, "cT", [P, KD, ROWS])
        u_pool = k.dram("u_pool", [HALF, TOK])
        u_ssm = k.dram("u_ssm", [HALF, STEP, NCH])
        mod_d = k.dram("mod_d", [ROWS, 6 * D])
        mix_d = k.dram("mix_d", [D, TOK])
        g_d = k.dram("g_d", [HALF, STEP, NCH])
        x2_d = k.dram("x2_d", [TOK, D])
        h2_d = k.dram("h2_d", [TOK, D])
        o_d = k.dram("o_d", [(MAXT + 2) * P, D])
        s1 = {n: k.sem(n) for n in ("x_in", "ct_sb", "hs", "store_go")}
        with ExitStack() as st:
            w_hi = k.sb(st, "w_hi", [P, KD, D], F32R)
            w_lo = k.sb(st, "w_lo", [P, KD, D], F32R)
            xraw = k.sb(st, "xraw", [P, TPB, D])
            A1 = k.sb(st, "A1", [P, KD, ROWS])
            B1 = k.sb(st, "B1", [P, KD, ROWS])
            adaln_first(k, a, s1, w_hi, w_lo, xraw, A1, B1)
            in_projection(k, a, s1, w_hi, w_lo, xraw, A1, B1, u_pool, u_ssm)
        mixers(k, a, o, mod_d, u_pool, u_ssm, mix_d, g_d)
        k.clear_semaphores()
        k.stage = "all"
        R = Routed(k, s0)
        lg = k.sb(s0, "lg", [P, NT, 4 + NE])
        with ExitStack() as st:
            wo_hi = k.sb(st, "wo_hi", [P, KD, D], F32R)
            wo_lo = k.sb(st, "wo_lo", [P, KD, D], F32R)
            glu(k, a, g_d, mix_d, wo_hi, wo_lo)
            out_projection(k, a, mod_d, mix_d, x2_d, h2_d, wo_hi, wo_lo, lg)
        routing(k, lg, R)
        experts(k, a, h2_d, o_d, R)
        combine(k, a, o, x2_d, o_d, mod_d, R.pos)


_OUTS = [("y_prompt", (1, TP, D)), ("y_sample", (NSEQ, LSEQ, D)), ("pool_p", (1, 1, BUF, HALF)),
         ("pool_s", (1, NSEQ, BUF, HALF)), ("re_p", (1, 1, G, NS)), ("im_p", (1, 1, G, NS)),
         ("re_s", (1, NSEQ, G, NS)), ("im_s", (1, NSEQ, G, NS))]


def kernel(**inputs):
    import numpy as _np
    import concourse.bacc as _bacc
    from concourse.bass_utils import run_bass_kernel_spmd as _run

    nc = _bacc.Bacc("TRN2", target_bir_lowering=False, num_devices=1)
    arrays = {"in_" + n: _np.ascontiguousarray(x) for n, x in inputs.items()}
    a = {n[3:]: nc.dram_tensor(n, x.shape, F32, kind="ExternalInput").ap() for n, x in arrays.items()}
    o = {n: nc.dram_tensor("out_" + n, shape, F32, kind="ExternalOutput").ap() for n, shape in _OUTS}
    hybrid_step(nc, a, o)
    r = _run(nc, [arrays], core_ids=[0])
    return tuple(r.results[0]["out_" + n] for n, _ in _OUTS)
```

```python
from contextlib import ExitStack

import numpy as np

import concourse.bass as bass
from concourse import mybir

F32 = mybir.dt.float32
F32R = mybir.dt.float32r
I32 = mybir.dt.int32
ALU = mybir.AluOpType
ACT = mybir.ActivationFunctionType
AX_X = mybir.AxisListType.X

P = 128
D = 1024
KD = D // P
HALF = D // 2
QH = HALF // P
TP = 2048
NSEQ = 8
LSEQ = 8
TS = NSEQ * LSEQ
TOK = TP + TS
ROWS = NSEQ + 1
BLK = 512
NBLK = TP // BLK
TPB = BLK // P
STEP = 8
NCH = TOK // STEP
PCH = TP // STEP
LOG_CH = PCH.bit_length() - 1
G = 32
GH = 16
NS = 64
PAIRS = G // 2
BUF = 15
WINDOWS = (2, 4, 8, 16)
NE = 16
EPG = 4
FH = 256
NT = (TOK + P - 1) // P
EPS = 1e-6
MAXT = (2 * TOK + NE * (P - 1)) // P // 2 * 2


class Chain:

    def __init__(self, eng, sem):
        self.eng, self.sem, self.base, self.n = eng, sem, 0, 0

    def link(self, ins):
        self.n += 1
        ins.then_inc(self.sem, 1)
        self.eng.wait_ge(self.sem, self.base + self.n)


class Core:

    def __init__(self, nc, stack):
        self.nc, self.stack, self.stage = nc, stack, "all"
        self.own = []

    def sb(self, stack, name, shape, dt=F32):
        return stack.enter_context(self.nc.sbuf_tensor(f"{self.stage}_{name}", shape, dt))

    def ps(self, stack, name, shape):
        return stack.enter_context(self.nc.psum_tensor(f"{self.stage}_{name}", shape, F32))

    def sem(self, name):
        self.own.append(self.nc.alloc_semaphore(name=name))
        return self.own[-1]

    def clear_semaphores(self):
        self.nc.clear_and_free_semaphores(self.own)
        self.nc.all_engine_barrier()
        self.own = []

    def dram(self, name, shape, dt=F32):
        return self.nc.dram_tensor(name, shape, dt).ap()


def matmul3(pe, out, l_hi, l_lo, r_hi, r_lo, start, stop):
    pe.matmul(out, l_hi, r_hi, start=start, stop=False)
    pe.matmul(out, l_lo, r_hi, start=False, stop=False)
    return pe.matmul(out, l_hi, r_lo, start=False, stop=stop)


def normalise(dve, s1, b, rows, tiles, xraw, xn, ss):
    dve.wait_ge(s1["sq_done"], b + 1)
    dve.tensor_scalar(ss[0:rows, TPB:TPB + tiles], ss[0:rows, 0:tiles], 1.0 / D, EPS,
                      ALU.mult, ALU.add).then_inc(s1["ms_done"], 1)
    dve.wait_ge(s1["rt_done"], b + 1)
    dve.reciprocal(ss[0:rows, 3 * TPB:3 * TPB + tiles],
                   ss[0:rows, 2 * TPB:2 * TPB + tiles]).then_inc(s1["rstd_done"], 1)
    dve.wait_ge(s1["rstd_done"], b + 1)
    if not isinstance(b, int) or b:
        dve.wait_ge(s1["t_done"], 8 * b)
    for j in range(tiles):
        ins = dve.tensor_scalar(xn[0:rows, j, :], xraw[0:rows, j, :], ss[0:rows, 3 * TPB + j:3 * TPB + j + 1], None,
                                ALU.mult)
    ins.then_inc(s1["xn_done"], 1)


def adaln_first(k, a, s1, w_hi, w_lo, xraw, xn, ss, A1, B1):
    nc = k.nc
    k.stage = "adaln_first"
    with ExitStack() as st:
        c_sb = k.sb(st, "c_sb", [ROWS, D])
        cs = k.sb(st, "cs", [ROWS, D])
        brow = k.sb(st, "brow1", [ROWS, 2 * D])
        modA = k.sb(st, "modA", [ROWS, 2 * D])
        n1col = k.sb(st, "n1col", [P, KD])
        raw = k.sb(st, "raw1", [P, 2, KD, BLK])
        psT = k.ps(st, "psT1", [P, KD * ROWS])
        psB = k.ps(st, "psB1", [P, 2, BLK])
        psC = k.ps(st, "psC1", [P, 2 * KD * ROWS])
        c_in, small_in, silu_done, ct_ps, ada_mm, ada_row, modt_ps, modt_sb, w1_hi, w1_lo, ident_ok = [
            k.sem(n) for n in ("c_in", "small_in1", "silu_done", "ct_ps", "ada_mm", "ada_row", "modt_ps",
                               "modt_sb", "w1_hi", "w1_lo", "ident_ok")]
        raw_in = [k.sem(f"raw1_in{i}") for i in range(2)]
        NA = 2 * D // BLK
        with nc.Block() as block:

            @block.sync
            def _(sp):
                sp.dma_start(c_sb[0:1, :], a["c_prompt"]).then_inc(c_in, 16)
                sp.dma_start(c_sb[1:ROWS, :], a["c_sample"]).then_inc(c_in, 16)
                sp.dma_start(brow[:], a["b_ada"][:, 0:2 * D].broadcast_to([ROWS, 2 * D])).then_inc(small_in, 16)
                sp.dma_start(n1col[:], a["norm1_g"][0].rearrange("(k p) -> p k", p=P),
                             allow_slow_non_contiguous=True).then_inc(small_in, 16)
                ada = a["w_ada"][0].rearrange("(k p) n -> p k n", p=P)
                w_in = a["w_in"][0].rearrange("(k p) n -> p k n", p=P)
                for j in range(NA + 2):
                    if j == 2:
                        sp.dma_start(xraw[:], a["x_prompt"][0, 0:BLK, :].rearrange("(j p) d -> p j d", p=P)
                                     ).then_inc(s1["x_in"], 16)
                    if 2 <= j < NA + 2:
                        sp.wait_ge(ada_mm, j - 1)
                    src = ada[:, :, j * BLK:(j + 1) * BLK] if j < NA else w_in[:, :, (j - NA) * BLK:(j - NA + 1) * BLK]
                    sp.dma_start(raw[:, j % 2], src).then_inc(raw_in[j % 2], 16)

            @block.gpsimd
            def _(pool):
                pool.memset(k.ident[:], 0.0).then_inc(ident_ok, 1)
                pool.wait_ge(ident_ok, 1)
                pool.affine_select(out=k.ident[:], in_=k.ident[:], compare_op=ALU.not_equal, fill=1.0, base=0,
                                   pattern=[[-1, P]], channel_multiplier=1).then_inc(ident_ok, 1)

            @block.scalar
            def _(act):
                act.wait_ge(c_in, 32)
                act.activation(cs[:], c_sb[:], ACT.Silu).then_inc(silu_done, 1)
                act.wait_ge(s1["x_in"], 16)
                for j in range(TPB):
                    ins = act.activation(xn[:, j, :], xraw[:, j, :], ACT.Square, accum_out=ss[:, j:j + 1])
                ins.then_inc(s1["sq_done"], 1)
                act.wait_ge(s1["ms_done"], 1)
                act.activation(ss[:, 2 * TPB:3 * TPB], ss[:, TPB:2 * TPB], ACT.Sqrt).then_inc(s1["rt_done"], 1)
                for h in range(2):
                    act.wait_ge(raw_in[(NA + h) % 2], 16 * ((NA + h) // 2 + 1))
                    act.copy(w_hi[:, :, h * BLK:(h + 1) * BLK], raw[:, (NA + h) % 2]).then_inc(w1_hi, 1)

            @block.tensor
            def _(pe):
                pe.wait_ge(ident_ok, 2)
                pe.wait_ge(silu_done, 1)
                for t in range(KD):
                    mm = pe.transpose(psT[:, t * ROWS:(t + 1) * ROWS], cs[:, t * P:(t + 1) * P],
                                      k.ident[0:ROWS, 0:ROWS])
                mm.then_inc(ct_ps, 1)
                pe.wait_ge(s1["ct_sb"], 1)
                for j in range(NA):
                    pe.wait_ge(raw_in[j % 2], 16 * (j // 2 + 1))
                    if j >= 2:
                        pe.wait_ge(ada_row, j - 1)
                    for t in range(KD):
                        mm = pe.matmul(psB[0:ROWS, j % 2, :], k.cT[:, t, :], raw[:, j % 2, t, :],
                                       start=t == 0, stop=t == KD - 1)
                    mm.then_inc(ada_mm, 1)
                pe.wait_ge(ada_row, NA)
                for t in range(2 * KD):
                    mm = pe.transpose(psC[:, t * ROWS:(t + 1) * ROWS], modA[:, t * P:(t + 1) * P],
                                      k.ident[0:ROWS, 0:ROWS])
                mm.then_inc(modt_ps, 1)

            @block.vector
            def _(dve):
                dve.wait_ge(ct_ps, 1)
                dve.tensor_copy(k.cT[:].rearrange("p k r -> p (k r)"), psT[:]).then_inc(s1["ct_sb"], 1)
                dve.wait_ge(small_in, 32)
                for j in range(NA):
                    if j == 2:
                        normalise(dve, s1, 0, P, TPB, xraw, xn, ss)
                    dve.wait_ge(ada_mm, j + 1)
                    dve.tensor_tensor(modA[:, j * BLK:(j + 1) * BLK], psB[0:ROWS, j % 2, :],
                                      brow[:, j * BLK:(j + 1) * BLK], ALU.add).then_inc(ada_row, 1)
                dve.wait_ge(modt_ps, 1)
                dve.tensor_copy(B1[:].rearrange("p k r -> p (k r)"), psC[:, 0:KD * ROWS]).then_inc(modt_sb, 1)
                dve.scalar_tensor_tensor(out=A1[:], in0=psC[:, KD * ROWS:].rearrange("p (k r) -> p k r", r=ROWS),
                                         scalar=1.0, in1=n1col[:].unsqueeze(2).broadcast_to([P, KD, ROWS]),
                                         op0=ALU.add, op1=ALU.mult).then_inc(modt_sb, 1)
                for h in range(2):
                    dve.wait_ge(w1_hi, h + 1)
                    dve.tensor_tensor(w_lo[:, :, h * BLK:(h + 1) * BLK], raw[:, (NA + h) % 2],
                                      w_hi[:, :, h * BLK:(h + 1) * BLK].bitcast(F32), ALU.subtract).then_inc(w1_lo, 1)


def in_projection(k, a, s1, w_hi, w_lo, xraw, xn, ss, A1, B1, u_pool, u_ssm):
    nc = k.nc
    k.stage = "in_projection"
    with ExitStack() as st:
        junk = k.sb(st, "junk2", [P, TPB, D])
        hf = k.sb(st, "hf", [P, 2, BLK])
        hT_hi = k.sb(st, "hT_hi", [P, 2, KD, BLK], F32R)
        hT_lo = k.sb(st, "hT_lo", [P, 2, KD, BLK], F32R)
        u_s = k.sb(st, "u_s", [TS, 2, HALF])
        ust = k.sb(st, "ust", [P, 2, BLK])
        psT = k.ps(st, "psT2", [P, 2, BLK])
        psM = k.ps(st, "psM2", [P, 2, BLK])
        hf_done, hi_done, lo_done, mm_done, u_evac, us_done = [
            k.sem(n) for n in ("hf_done", "hi_done", "lo_done", "mm_done", "u_evac", "us_done")]
        sq_done, ms_done, rt_done, xn_done, t_done = [s1[n] for n in ("sq_done", "ms_done", "rt_done", "xn_done", "t_done")]
        ust_out = [k.sem(f"ust_out{i}") for i in range(2)]
        x_in = s1["x_in"]
        MM0, UE0 = 1, 2
        x_s = a["x_sample"].rearrange("b t d -> (b t) d")

        def t_steps(m):
            return (2 * (m - 3), 2 * (m - 3) + 1) if 3 <= m <= 6 else ()

        with nc.Block() as block:

            @block.sync
            def _(sp):
                for u in range(2):
                    sp.sem_inc(ust_out[u], 16)

                def stores(b, w):
                    for m in range(KD):
                        sp.wait_ge(u_evac, UE0 + 8 * b + m + 1)
                        sp.sem_inc(s1["store_go"], 1)
                        if m < QH:
                            dst = u_pool[m * P:(m + 1) * P, bass.ds(b * BLK, w)]
                            sp.dma_start(dst, ust[:, m % 2, 0:w]).then_inc(ust_out[m % 2], 16)
                        else:
                            c0 = NSEQ + b * (BLK // STEP) if w == BLK else 0
                            dst = u_ssm[(m - QH) * P:(m - QH + 1) * P, :, bass.ds(c0, w // STEP)]
                            sp.dma_start(dst, ust[:, m % 2, 0:w].rearrange("p (s c) -> p s c", s=STEP)
                                         ).then_inc(ust_out[m % 2], 16)

                with sp.Fori(0, NBLK - 1) as b:
                    row = sp.snap(b * BLK + BLK)
                    sp.wait_ge(xn_done, b + 1)
                    sp.dma_start(xraw[:], a["x_prompt"][0, bass.ds(row, BLK), :]
                                 .rearrange("(j p) d -> p j d", p=P)).then_inc(x_in, 16)
                    stores(b, BLK)
                sp.wait_ge(xn_done, NBLK)
                sp.dma_start(xraw[0:TS, 0, :], x_s).then_inc(x_in, 16)
                stores(NBLK - 1, BLK)
                sp.wait_ge(u_evac, UE0 + 8 * NBLK + 1)
                sp.dma_start(u_pool[:, TP:TOK].rearrange("(m p) n -> p m n", p=P),
                             ust[:, 0, 0:QH * TS].rearrange("p (m n) -> p m n", m=QH)).then_inc(ust_out[0], 16)
                sp.wait_ge(u_evac, UE0 + 8 * NBLK + 2)
                for m in range(QH):
                    sp.dma_start(u_ssm[m * P:(m + 1) * P, :, 0:NSEQ], ust[:, 1, m * TS:(m + 1) * TS]
                                 .rearrange("p (s c) -> p s c", s=STEP)).then_inc(ust_out[1], 16)
                sp.wait_ge(ust_out[0], 16 * (1 + 4 * NBLK + 1))
                sp.wait_ge(ust_out[1], 16 * (1 + 4 * NBLK + QH))

            @block.scalar
            def _(act):
                act.sem_inc(u_evac, UE0)

                def norm(b, rows, tiles):
                    act.wait_ge(x_in, 16 * b + 16)
                    for j in range(tiles):
                        ins = act.activation(junk[0:rows, j, :], xraw[0:rows, j, :], ACT.Square,
                                             accum_out=ss[0:rows, j:j + 1])
                    ins.then_inc(sq_done, 1)
                    act.wait_ge(ms_done, b + 1)
                    act.activation(ss[0:rows, 2 * TPB:2 * TPB + tiles], ss[0:rows, TPB:TPB + tiles],
                                   ACT.Sqrt).then_inc(rt_done, 1)

                def modulate(b, t, first=False):
                    act.wait_ge(t_done, 8 * b + t + 1)
                    if not (first and t < 2):
                        act.wait_ge(lo_done, 8 * b + t - 1)
                    act.activation(hf[:, t % 2, :], psT[:, t % 2, :], ACT.Identity, bias=B1[:, t, 0:1],
                                   scale=A1[:, t, 0:1]).then_inc(hf_done, 1)

                def evac(b, m, w):
                    act.wait_ge(mm_done, MM0 + 8 * b + m + 1)
                    act.wait_ge(ust_out[m % 2], 16 * (4 * b + m // 2) + 16)
                    if m < QH:
                        act.copy(ust[:, m % 2, 0:w], psM[:, m % 2, 0:w]).then_inc(u_evac, 1)
                    else:
                        act.copy(ust[:, m % 2, 0:w].rearrange("p (s c) -> p c s", s=STEP),
                                 psM[:, m % 2, 0:w].rearrange("p (c s) -> p c s", s=STEP)).then_inc(u_evac, 1)

                for t in range(KD):
                    modulate(0, t, first=True)
                with act.Fori(0, NBLK - 1) as b:
                    for m in range(KD):
                        evac(b, m, BLK)
                        if m == 1:
                            norm(b + 1, P, TPB)
                        for t in t_steps(m):
                            modulate(b + 1, t)
                for m in range(KD):
                    evac(NBLK - 1, m, BLK)
                    if m == 1:
                        norm(NBLK, TS, 1)
                act.wait_ge(mm_done, MM0 + 8 * NBLK + 1)
                act.copy(u_s[:, 0, :], psM[0:TS, 0, :]).then_inc(us_done, 1)
                act.wait_ge(mm_done, MM0 + 8 * NBLK + 2)
                act.wait_ge(ust_out[0], 16 * (1 + 4 * NBLK))
                act.copy(ust[:, 0, 0:QH * TS], psT[:, 0, 0:QH * TS]).then_inc(u_evac, 1)
                act.wait_ge(ust_out[1], 16 * (1 + 4 * NBLK))
                act.copy(ust[:, 1, 0:QH * TS].rearrange("p (m s c) -> p m s c", m=QH, s=STEP),
                         psT[:, 0, QH * TS:2 * QH * TS].rearrange("p (m c s) -> p m s c", m=QH, s=STEP)
                         ).then_inc(u_evac, 1)

            @block.vector
            def _(dve):
                def split(b, t, w, par):
                    dve.wait_ge(hf_done, 8 * b + t + 1)
                    hi = hT_hi[:, par, t, 0:w] if isinstance(par, int) else \
                        hT_hi[:, bass.ds(par, 1), t, 0:w].rearrange("p a n -> p (a n)")
                    lo = hT_lo[:, par, t, 0:w] if isinstance(par, int) else \
                        hT_lo[:, bass.ds(par, 1), t, 0:w].rearrange("p a n -> p (a n)")
                    dve.tensor_copy(hi, hf[:, t % 2, 0:w]).then_inc(hi_done, 1)
                    dve.wait_ge(hi_done, 8 * b + t + 1)
                    dve.tensor_tensor(lo, hf[:, t % 2, 0:w], hi.bitcast(F32), ALU.subtract).then_inc(lo_done, 1)

                for t in range(KD):
                    split(0, t, BLK, 0)
                with dve.Fori(0, NBLK - 1) as b:
                    normalise(dve, s1, b + 1, P, TPB, xraw, xn, ss)
                    dve.wait_ge(mm_done, MM0 + 8 * b)
                    for t in range(KD):
                        split(b + 1, t, BLK, (b + 1) & 1)
                normalise(dve, s1, NBLK, TS, 1, xraw, xn, ss)
                dve.wait_ge(mm_done, MM0 + 8 * (NBLK - 1))
                for t in range(KD):
                    dve.wait_ge(t_done, 8 * NBLK + t + 1)
                    ps = psT[:, t % 2, 0:TS].rearrange("p (q s) -> p q s", s=LSEQ)
                    h = hf[:, t % 2, 0:TS].rearrange("p (q s) -> p q s", s=LSEQ)
                    dve.tensor_tensor(h, ps, A1[:, t, 1:ROWS].unsqueeze(2).broadcast_to([P, NSEQ, LSEQ]),
                                      ALU.mult).then_inc(s1["hs"], 1)
                    dve.wait_ge(s1["hs"], t + 1)
                    dve.tensor_tensor(h, h, B1[:, t, 1:ROWS].unsqueeze(2).broadcast_to([P, NSEQ, LSEQ]),
                                      ALU.add).then_inc(hf_done, 1)
                    split(NBLK, t, TS, NBLK % 2)
                dve.wait_ge(mm_done, MM0 + 8 * NBLK + 1)
                dve.tensor_copy(u_s[:, 1, :], psM[0:TS, 1, :]).then_inc(us_done, 1)

            @block.tensor
            def _(pe):
                pe.sem_inc(mm_done, MM0)

                def turn(b, t, rows, tiles, first=False):
                    if t == 0:
                        pe.wait_ge(xn_done, b + 1)
                    if not (first and t < 2):
                        pe.wait_ge(hf_done, 8 * b + t - 1)
                    for j in range(tiles):
                        mm = pe.transpose(psT[:, t % 2, j * P:j * P + rows], xn[0:rows, j, t * P:(t + 1) * P],
                                          k.ident[0:rows, 0:rows])
                    mm.then_inc(t_done, 1)

                def product(b, m, w, par):
                    if m == 0:
                        pe.wait_ge(lo_done, 8 * b + 8)
                    pe.wait_ge(u_evac, UE0 + 8 * b + m - 1)
                    for t in range(KD):
                        r = [x[:, par, t, 0:w] if isinstance(par, int) else
                             x[:, bass.ds(par, 1), t, 0:w].rearrange("p a n -> p (a n)") for x in (hT_hi, hT_lo)]
                        mm = matmul3(pe, psM[:, m % 2, 0:w], w_hi[:, t, m * P:(m + 1) * P],
                                     w_lo[:, t, m * P:(m + 1) * P], r[0], r[1], t == 0, t == KD - 1)
                    mm.then_inc(mm_done, 1)

                for t in range(KD):
                    turn(0, t, P, TPB, first=True)
                with pe.Fori(0, NBLK - 1) as b:
                    for m in range(KD):
                        product(b, m, BLK, b & 1)
                        for t in t_steps(m):
                            turn(b + 1, t, P, TPB)
                for m in range(KD):
                    product(NBLK - 1, m, BLK, (NBLK - 1) % 2)
                    for t in t_steps(m):
                        turn(NBLK, t, TS, 1)
                pe.wait_ge(lo_done, 8 * (NBLK + 1))
                pe.wait_ge(u_evac, UE0 + 8 * NBLK)
                for n in range(2):
                    c = slice(n * BLK, (n + 1) * BLK)
                    for t in range(KD):
                        mm = matmul3(pe, psM[0:TS, n, :], hT_hi[:, NBLK % 2, t, 0:TS], hT_lo[:, NBLK % 2, t, 0:TS],
                                     w_hi[:, t, c], w_lo[:, t, c], t == 0, t == KD - 1)
                mm.then_inc(mm_done, 1)
                pe.wait_ge(us_done, 2)
                for m in range(KD):
                    mm = pe.transpose(psT[:, 0, m * TS:(m + 1) * TS], u_s[:, m // QH, m % QH * P:(m % QH + 1) * P],
                                      k.ident[0:TS, 0:TS])
                mm.then_inc(mm_done, 1)


TWO_PI = 6.283185307179586
TWO_PI_HI = 6.28125
TWO_PI_MID = float(np.float32(TWO_PI - TWO_PI_HI))
TWO_PI_LO = TWO_PI - TWO_PI_HI - TWO_PI_MID
LN2 = 0.6931471805599453
LN2_HI = 0.693359375
LN2_LO = LN2 - LN2_HI
EXP_C = [1 / 5040, 1 / 720, 1 / 120, 1 / 24, 1 / 6, 1 / 2, 1.0]
ROUND = 12582912.0
LATE_POOL = 4
ADA_W = 128
ADA_FIRST = 2 * D
ADA_N = (6 * D - ADA_FIRST) // ADA_W
ZP = BUF + TP
ZS = BUF + LSEQ


def mixers(k, a, o, mod_d, u_pool, u_ssm, mix_d, g_d):
    nc = k.nc
    k.stage = "mixers"
    with ExitStack() as st:
        U = k.sb(st, "U", [P, G, NCH])
        H = k.sb(st, "H", [P, 2, PAIRS, NCH + 1])
        scratch = k.sb(st, "scratch", [P, 2, 2, PAIRS * P])
        T = k.sb(st, "T", [P, G, P])
        VB = k.sb(st, "VB", [P, 2, PAIRS, P])
        CL = k.sb(st, "CL", [P, 2, PAIRS, (STEP + 1) * GH])
        raw = k.sb(st, "raw3", [P, 2, KD, ADA_W])
        brow = k.sb(st, "brow3", [1, 2, ADA_W])
        ones = k.sb(st, "ones3", [1, ROWS])
        modrow = k.sb(st, "modrow", [ROWS, 2, ADA_W])
        z = k.sb(st, "z", [P, 3, ZP])
        zs = k.sb(st, "zs", [P, QH, NSEQ, ZS])
        ws = k.sb(st, "ws", [P, 2, NSEQ, ZS])
        pooled_s = k.sb(st, "pooled_s", [P, TS])
        yst = k.sb(st, "yst", [P, 2, NCH])
        pst = k.sb(st, "pst", [P, 2, BLK])
        pw = k.sb(st, "pw", [P, QH, P])
        pscale = k.sb(st, "pscale", [P, QH])
        cnt_i = k.sb(st, "cnt_i", [P, 16], I32)
        cnt = k.sb(st, "cnt", [P, QH + 1, 16])
        B = k.sb(st, "B", [P, 2, PAIRS, GH])
        Bb = k.sb(st, "Bb", [P, 2, PAIRS, GH])
        C = k.sb(st, "C", [P, 2, PAIRS, GH])
        h0 = k.sb(st, "h0", [P, 2, NSEQ, PAIRS])
        fin_s = k.sb(st, "fin_s", [P, 2, NSEQ, PAIRS])
        PW = k.sb(st, "PW", [P, 2, STEP + 1, PAIRS])
        sm = k.sb(st, "sm", [P, 24, PAIRS])
        ph = B[:].rearrange("p a k h -> p (a k h)")[:, 0:(LOG_CH + 2) * 2 * PAIRS].rearrange(
            "p (j a k) -> p j a k", j=LOG_CH + 2, a=2)
        dskip = k.sb(st, "dskip", [GH, G])
        dd = yst[:].rearrange("p a c -> p (a c)")[0:GH, 0:G * GH].rearrange("h (g e) -> h g e", g=G)
        Hf = H[:].rearrange("p a b c -> p (a b c)")
        crow = Hf[0:GH, 0:2 * G * NS].rearrange("h (a n) -> h a n", a=2)
        o1 = 2 * G * NS
        arow = Hf[0:PAIRS, o1:o1 + 3 * P].rearrange("k (a n) -> k a n", a=3)
        dtrow = Hf[0:PAIRS, o1 + 3 * P:o1 + 3 * P + 4]
        o2 = o1 + 3 * P + 4
        h0row = Hf[:, o2:o2 + 2 * P].rearrange("p (a n) -> p a n", a=2)
        o3 = o2 + 2 * P
        sprow = Hf[0:NSEQ * BUF, o3:o3 + HALF]
        o4 = o3 + HALF
        nprow = Hf[0:TS, o4:o4 + 2 * HALF].rearrange("p (a n) -> p a n", a=2)
        o5 = o4 + 2 * HALF
        ztail = Hf[:, o5:o5 + QH * BUF].rearrange("p (q j) -> p q j", q=QH)
        o6 = o5 + QH * BUF
        zsrow = Hf[:, o6:o6 + QH * TS].rearrange("p (q j) -> p q j", q=QH)
        WB = scratch[:, 0].rearrange("p a (k n) -> p a k n", k=PAIRS)
        tmp = scratch[:, 1]
        KK = scratch[0:GH, 1].rearrange("h a n -> h (a n)").rearrange("h (g n) -> h g n", g=G)
        E = scratch[:].rearrange("p a b n -> p (a b n)").rearrange("p (a k c) -> p a k c", a=2, k=PAIRS)
        rt = VB[:].rearrange("p a k n -> p (a k n)").rearrange("p (t k c) -> p t k c", t=8, k=2)
        finrow = rt[:, 6].rearrange("p k (a n) -> p (k a) n", n=P)

        psA = k.ps(st, "psA3", [P, 2, BLK])
        psX = k.ps(st, "psX3", [P, 4, BLK])
        psP = k.ps(st, "psP3", [P, 2, BLK])
        names = ("tab_in", "c3_in", "h0_in", "sp_in", "pw_in", "u3_in", "zs_in", "z_in", "dt_row",
                 "x_fill", "x_evac", "ada2_mm", "a_evac", "arg", "sins", "wb_ready", "cl_ready",
                 "kk_diag", "t_zero", "t_in", "dve3", "pool3", "cnt_i_ok", "cnt_ok", "pooled", "p_mm", "p_evac",
                 "h_ready", "h_fix", "np_out", "fin_out", "b3_in", "d3_in", "ones_ok", "z_head", "zt_in")
        s = {n: k.sem(n) for n in names}
        raw_in = [k.sem(f"raw3_in{i}") for i in range(2)]
        mod_out = [k.sem(f"mod_out{i}") for i in range(2)]
        y_out = [k.sem(f"y_out{i}") for i in range(2)]
        p_out = [k.sem(f"p_out{i}") for i in range(2)]
        order = ["hist", "C", "h0", "np_s", "np_p", "tab"] + [f"VB{i}" for i in range(8)] + \
            [f"KK{i}" for i in range(8)] + [f"V{i}" for i in range(2 * PAIRS)] + [f"Y{i}" for i in range(G)] + \
            ["fin_p", "fin_s"]
        at = {n: i for i, n in enumerate(order)}
        PB = [(j * BLK, BLK) for j in range(NBLK)] + [(TP, TS)]

        with nc.Block() as block:

            @block.sync
            def _(sp):
                for i, n in enumerate(("ssm_a_re", "ssm_a_im")):
                    sp.dma_start(arow[:, i, :], a[n][0].rearrange("(k g) p -> k (g p)", g=2)).then_inc(s["tab_in"], 16)
                sp.dma_start(dtrow[:, 0:2], a["ssm_log_dt"][0].rearrange("(k g) -> k g", g=2)).then_inc(s["tab_in"], 16)
                for i, n in enumerate(("ssm_c_re", "ssm_c_im")):
                    sp.dma_start(crow[:, i, :].rearrange("h (g p) -> h g p", g=G),
                                 a[n][0].rearrange("g h p -> h g p")).then_inc(s["c3_in"], 16)
                for i, n in enumerate(("ssm_b_re", "ssm_b_im")):
                    sp.dma_start(B[:, i], a[n][0].rearrange("(k g) p h -> (g p) k h", g=2)).then_inc(s["b3_in"], 16)
                sp.dma_start(sprow, a["state_pool"][0].rearrange("b j c -> (b j) c")).then_inc(s["sp_in"], 16)
                for i, n in enumerate(("state_ssm_re", "state_ssm_im")):
                    sp.dma_start(h0row[:, i, :], a[n][0].rearrange("b (k g) p -> (b k) (g p)", g=2)
                                 ).then_inc(s["h0_in"], 16)
                for q in range(QH):
                    sp.dma_start(zs[:, q, :, BUF:ZS], u_pool[q * P:(q + 1) * P, TP:TOK]
                                 .rearrange("p (b j) -> p b j", b=NSEQ)).then_inc(s["zs_in"], 16)
                sp.dma_start(zsrow, u_pool[:, TP:TOK].rearrange("(q p) j -> p q j", p=P)).then_inc(s["zt_in"], 16)
                sp.dma_start(ztail, u_pool[:, TP - BUF:TP].rearrange("(q p) j -> p q j", p=P)).then_inc(s["zt_in"], 16)
                sp.dma_start(dskip[:], a["ssm_d"][0].rearrange("g h -> h g"),
                             allow_slow_non_contiguous=True).then_inc(s["d3_in"], 16)
                sp.dma_start(pw[:], a["pool_w"][0].rearrange("q c d -> c q d")).then_inc(s["pw_in"], 16)
                sp.dma_start(pscale[:], a["pool_scale"][0].rearrange("(q p) -> p q", p=P),
                             allow_slow_non_contiguous=True).then_inc(s["pw_in"], 16)
                sp.dma_start(o["pool_s"][0, :, 0:BUF - LSEQ, :], a["state_pool"][0, :, LSEQ:BUF, :]).then_inc(s["np_out"], 16)
                ada = a["w_ada"][0].rearrange("(k p) n -> p k n", p=P)

                def ada_load(j, u):
                    c0 = sp.snap((j + u) * ADA_W + ADA_FIRST) if not isinstance(j, int) else (j + u) * ADA_W + ADA_FIRST
                    sp.wait_ge(s["ada2_mm"], j + u + 1)
                    sp.dma_start(raw[:, u], ada[:, :, bass.ds(c0, ADA_W)]).then_inc(raw_in[u], 16)
                    sp.dma_start(brow[:, u, :], a["b_ada"][:, bass.ds(c0, ADA_W)]).then_inc(raw_in[u], 16)

                for u in range(2):
                    ada_load(0, u)
                for i in range(STEP):
                    sp.dma_start(U[i * GH:(i + 1) * GH, :, :],
                                 u_ssm[:, STEP - 1 - i, :].rearrange("(g h) c -> h g c", h=GH)).then_inc(s["u3_in"], 16)
                with sp.Fori(2, ADA_N - 1, 2) as j:
                    for u in range(2):
                        ada_load(j, u)

            @block.gpsimd
            def _(pool):
                ch = Chain(pool, s["pool3"])
                pool.memset(ones[:], 1.0).then_inc(s["ones_ok"], 1)
                pool.memset(T[:], 0.0).then_inc(s["t_zero"], 1)
                pool.iota(cnt_i[:], [[1, 16]], base=1, channel_multiplier=0).then_inc(s["cnt_i_ok"], 1)
                pool.memset(z[:, 0, 0:BUF], 0.0).then_inc(s["z_head"], 1)
                pool.wait_ge(s["zs_in"], 16 * QH)
                pool.wait_ge(s["x_evac"], at["hist"] + 1)
                for q, w in enumerate(WINDOWS):
                    if q:
                        pool.wait_ge(s["p_mm"], 5 * q)
                    pool.dma_start(z[:, 0, BUF:ZP], u_pool[q * P:(q + 1) * P, 0:TP]).then_inc(s["z_in"], 16)
                    pool.wait_ge(s["z_in"], 16 * (q + 1))
                    pool.wait_ge(s["z_head"], 1)
                    zc, sc = z[:, 0], zs[:, q]
                    lag, slot = 1, 0
                    while lag < w:
                        zn, sn = z[:, 1 + slot % 2], ws[:, slot % 2]
                        b0 = 2 * lag - 1
                        pool.tensor_tensor(zn[:, b0:ZP], zc[:, b0:ZP], zc[:, b0 - lag:ZP - lag], ALU.add
                                           ).then_inc(s["pool3"], 1)
                        pool.tensor_tensor(sn[:, :, b0:ZS], sc[:, :, b0:ZS], sc[:, :, b0 - lag:ZS - lag], ALU.add
                                           ).then_inc(s["pool3"], 1)
                        ch.n += 2
                        pool.wait_ge(s["pool3"], ch.n)
                        zc, sc, lag, slot = zn, sn, 2 * lag, slot + 1
                    pool.wait_ge(s["cnt_ok"], 1)
                    pool.tensor_tensor(zc[:, BUF:BUF + 16], zc[:, BUF:BUF + 16], cnt[:, q, :], ALU.mult).then_inc(s["pool3"], 1)
                    pool.tensor_scalar(zc[:, BUF + 16:ZP], zc[:, BUF + 16:ZP], 1.0 / w, None, ALU.mult).then_inc(s["pool3"], 1)
                    pool.tensor_scalar(sc[:, :, BUF:ZS], sc[:, :, BUF:ZS], 1.0 / w, None, ALU.mult).then_inc(s["pool3"], 1)
                    ch.n += 3
                    pool.wait_ge(s["pool3"], ch.n)
                    pool.tensor_tensor(zc[:, BUF:ZP], zc[:, BUF:ZP], z[:, 0, BUF:ZP], ALU.subtract).then_inc(s["pooled"], 1)
                    pool.tensor_tensor(pooled_s[:].rearrange("p (b j) -> p b j", b=NSEQ), sc[:, :, BUF:ZS],
                                       zs[:, q, :, BUF:ZS], ALU.subtract).then_inc(s["pooled"], 1)

            @block.tensor
            def _(pe):
                pe.sem_inc(s["ada2_mm"], 2)
                pe.wait_ge(s["ones_ok"], 1)
                idt = k.ident

                def slot(n):
                    i = at[n]
                    if i >= 4:
                        pe.wait_ge(s["x_evac"], i - 3)
                    return psX[:, i % 4, :]

                def ada(j0, j1):
                    with pe.Fori(j0, j1 - 1, 2) as j:
                        for u in range(2):
                            pe.wait_ge(raw_in[u], 16 * j + 32)
                            pe.wait_ge(s["a_evac"], j + u + 1)
                            out = psA[0:ROWS, u, 0:ADA_W]
                            for t in range(KD):
                                pe.matmul(out, k.cT[:, t, :], raw[:, u, t, :], start=t == 0, stop=False)
                            pe.matmul(out, ones[0:1, :], brow[0:1, u, :], start=False, stop=True
                                      ).then_inc(s["ada2_mm"], 1)

                def pooled_product(q):
                    pe.wait_ge(s["pw_in"], 32)
                    pe.wait_ge(s["pooled"], 2 * q + 2)
                    src = z[:, 1 + q % 2]
                    for j, (c0, w) in enumerate(PB):
                        n = 5 * q + j
                        if n >= 2:
                            pe.wait_ge(s["p_evac"], n - 1)
                        rhs = src[:, BUF + c0:BUF + c0 + w] if w == BLK else pooled_s[:]
                        pe.matmul(psP[:, n % 2, 0:w], pw[:, q, :], rhs, start=True, stop=True).then_inc(s["p_mm"], 1)

                pe.wait_ge(s["sp_in"], 16)
                x = slot("hist")
                nh = NSEQ * BUF
                for q in range(QH):
                    mm = pe.transpose(x[:, q * nh:(q + 1) * nh], sprow[:, q * P:(q + 1) * P], idt[0:nh, 0:nh])
                mm.then_inc(s["x_fill"], 1)
                pe.wait_ge(s["c3_in"], 32)
                x = slot("C")
                for i in range(2):
                    for p in range(PAIRS):
                        c0 = (i * PAIRS + p) * GH
                        mm = pe.transpose(x[:, c0:c0 + GH], crow[:, i, p * P:(p + 1) * P], idt[0:GH, 0:GH])
                mm.then_inc(s["x_fill"], 1)
                pe.wait_ge(s["h0_in"], 32)
                x = slot("h0")
                for i in range(2):
                    mm = pe.transpose(x[:, i * P:(i + 1) * P], h0row[:, i, :], idt[:])
                mm.then_inc(s["x_fill"], 1)
                pe.wait_ge(s["zt_in"], 32)
                x = slot("np_s")
                for q in range(QH):
                    mm = pe.transpose(x[0:TS, q * P:(q + 1) * P], zsrow[:, q, :], idt[:])
                mm.then_inc(s["x_fill"], 1)
                x = slot("np_p")
                for q in range(QH):
                    mm = pe.transpose(x[0:BUF, q * P:(q + 1) * P], ztail[:, q, :], idt[:])
                mm.then_inc(s["x_fill"], 1)
                pe.wait_ge(s["dt_row"], 1)
                x = slot("tab")
                for i in range(3):
                    mm = pe.transpose(x[:, i * PAIRS:(i + 1) * PAIRS], arow[:, i, :], idt[0:PAIRS, 0:PAIRS])
                mm.then_inc(s["x_fill"], 1)
                ada(0, 8)
                pooled_product(0)
                pe.wait_ge(s["wb_ready"], 1)
                for f in range(8):
                    x = slot(f"VB{f}")
                    for j in range(4):
                        i, p = divmod(4 * f + j, PAIRS)
                        mm = pe.transpose(x[:, j * P:(j + 1) * P], WB[:, i, p, :], idt[:])
                    mm.then_inc(s["x_fill"], 1)
                pe.wait_ge(s["cl_ready"], 1)
                for f in range(8):
                    x = slot(f"KK{f}")
                    for j in range(4):
                        p, g2 = 4 * (f // 2) + j, f % 2
                        r = slice(NS * g2, NS * g2 + NS)
                        for i in range(2):
                            mm = pe.matmul(x[0:GH, j * P:(j + 1) * P], Bb[r, i, p, :], CL[r, i, p, 0:P],
                                           start=i == 0, stop=i == 1)
                    mm.then_inc(s["x_fill"], 1)
                pooled_product(1)
                pe.wait_ge(s["u3_in"], 16 * STEP)
                for p in range(PAIRS):
                    for i in range(2):
                        x = slot(f"V{2 * p + i}")
                        for g2 in range(2):
                            mm = pe.matmul(x[NS * g2:NS * g2 + NS, 0:NCH], VB[:, i, p, NS * g2:NS * g2 + NS],
                                           U[:, 2 * p + g2, :], start=True, stop=True)
                        mm.then_inc(s["x_fill"], 1)
                ada(8, 16)
                pooled_product(2)
                ada(16, 32)
                pe.wait_ge(s["t_in"], 16 * STEP)
                for g in range(G):
                    if g == LATE_POOL:
                        pooled_product(3)
                    p, g2 = divmod(g, 2)
                    pe.wait_ge(s["h_ready"], g // 4 + 1)
                    x = slot(f"Y{g}")[:, 0:NCH]
                    r = slice(NS * g2, NS * g2 + NS)
                    pe.matmul(x, T[:, g, :], U[:, g, :], start=True, stop=False)
                    for i in range(2):
                        mm = pe.matmul(x, CL[r, i, p, GH:], H[r, i, p, 0:NCH], start=False, stop=i == 1)
                    mm.then_inc(s["x_fill"], 1)
                x = slot("fin_p")
                for i in range(2):
                    mm = pe.transpose(x[0:PAIRS, i * P:(i + 1) * P], H[:, i, :, NCH], idt[:])
                mm.then_inc(s["x_fill"], 1)
                x = slot("fin_s")
                for i in range(2):
                    mm = pe.transpose(x[:, i * P:(i + 1) * P], fin_s[:, i].rearrange("p b k -> p (b k)"), idt[:])
                mm.then_inc(s["x_fill"], 1)

            @block.scalar
            def _(act):
                act.sem_inc(s["a_evac"], 2)
                for u in range(2):
                    act.sem_inc(mod_out[u], 16)
                def evac(n, out, rows=P, w=BLK, func=None, f=None):
                    i = at[n]
                    act.wait_ge(s["x_fill"], i + 1)
                    x = psX[0:rows, i % 4, 0:w]
                    if f:
                        x = f(x)
                    (act.activation(out, x, func) if func else act.copy(out, x)).then_inc(s["x_evac"], 1)

                def ada(j0, j1):
                    with act.Fori(j0, j1 - 1, 2) as j:
                        for u in range(2):
                            c0 = act.snap((j + u) * ADA_W + ADA_FIRST)
                            act.wait_ge(mod_out[u], 8 * j + 16)
                            act.wait_ge(s["ada2_mm"], j + u + 3)
                            act.copy(modrow[:, u, :], psA[0:ROWS, u, 0:ADA_W]).then_inc(s["a_evac"], 1)
                            act.wait_ge(s["a_evac"], j + u + 3)
                            act.dma_start(mod_d[:, bass.ds(c0, ADA_W)], modrow[:, u, :]).then_inc(mod_out[u], 16)

                def pooled_out(q):
                    for j, (c0, w) in enumerate(PB):
                        n = 5 * q + j
                        act.wait_ge(s["p_mm"], n + 1)
                        if n >= 2:
                            act.wait_ge(p_out[n % 2], 16 * (n // 2))
                        act.activation(pst[:, n % 2, 0:w], psP[:, n % 2, 0:w], ACT.Copy,
                                       scale=pscale[:, q:q + 1]).then_inc(s["p_evac"], 1)
                        act.wait_ge(s["p_evac"], n + 1)
                        act.dma_start(mix_d[q * P:(q + 1) * P, c0:c0 + w], pst[:, n % 2, 0:w]).then_inc(p_out[n % 2], 16)

                evac("hist", zs[:, :, :, 0:BUF],
                     w=QH * NSEQ * BUF, f=lambda x: x.rearrange("p (q b j) -> p q b j", q=QH, b=NSEQ))
                evac("C", C[:].rearrange("p a k h -> p (a k h)"))
                evac("h0", h0[:].rearrange("p a b k -> p (a b k)"), w=2 * P)
                evac("np_s", nprow[:, 0, :], rows=TS)
                evac("np_p", nprow[0:BUF, 1, :], rows=BUF)
                evac("tab", sm[:, 0:3, :].rearrange("p a k -> p (a k)"), w=3 * PAIRS)
                act.wait_ge(s["x_evac"], at["np_p"] + 1)
                act.dma_start(o["pool_s"][0, :, BUF - LSEQ:BUF, :], nprow[:, 0, :]).then_inc(s["np_out"], 16)
                act.dma_start(o["pool_p"][0, 0], nprow[0:BUF, 1, :]).then_inc(s["np_out"], 16)
                act.wait_ge(s["arg"], 1)
                act.activation(sm[:, 9, :], sm[:, 7, :], ACT.Sin)
                act.activation(sm[:, 10, :], sm[:, 8, :], ACT.Sin).then_inc(s["sins"], 1)
                ada(0, 8)
                pooled_out(0)
                for f in range(8):
                    i, p = divmod(4 * f, PAIRS)
                    evac(f"VB{f}", VB[:, i, p:p + 4, :].rearrange("p k n -> p (k n)"))
                for f in range(8):
                    evac(f"KK{f}", KK[:, 8 * (f // 2) + f % 2:8 * (f // 2) + 8:2, :], rows=GH,
                         f=lambda x: x.rearrange("h (g n) -> h g n", n=P))
                act.wait_ge(s["kk_diag"], 1)
                act.wait_ge(s["t_zero"], 1)
                for i in range(STEP):
                    t = STEP - 1 - i
                    act.dma_start(T[i * GH:(i + 1) * GH, :, t * GH:P], KK[:, :, 0:P - t * GH]).then_inc(s["t_in"], 16)
                pooled_out(1)
                act.wait_ge(s["np_out"], 48)
                for p in range(PAIRS):
                    for i in range(2):
                        evac(f"V{2 * p + i}", H[:, i, p, 1:NCH + 1], w=NCH)
                ada(8, 16)
                pooled_out(2)
                ada(16, 32)
                for g in range(G):
                    if g == LATE_POOL:
                        pooled_out(3)
                    if g >= 2:
                        act.wait_ge(y_out[g % 2], 16 * (g // 2))
                    evac(f"Y{g}", yst[:, g % 2, :], w=NCH, func=ACT.Gelu_apprx_tanh)
                    act.wait_ge(s["x_evac"], at[f"Y{g}"] + 1)
                    act.dma_start(g_d[g * GH:(g + 1) * GH, :, :].rearrange("h t c -> t h c"),
                                  yst[:, g % 2, :]).then_inc(y_out[g % 2], 16)
                evac("fin_p", finrow[0:PAIRS, 0:2, :].rearrange("p a n -> p (a n)"), rows=PAIRS, w=2 * P)
                evac("fin_s", finrow[:, 2:4, :].rearrange("p a n -> p (a n)"), w=2 * P)
                act.wait_ge(s["x_evac"], at["fin_s"] + 1)
                for i, n in enumerate(("re", "im")):
                    act.dma_start(o[n + "_p"][0, 0].rearrange("(k g) p -> k (g p)", g=2), finrow[0:PAIRS, i, :]
                                  ).then_inc(s["fin_out"], 16)
                    act.dma_start(o[n + "_s"][0].rearrange("b (k g) p -> (b k) (g p)", g=2), finrow[:, 2 + i, :]
                                  ).then_inc(s["fin_out"], 16)
                act.wait_ge(s["fin_out"], 64)
                for u in range(2):
                    act.wait_ge(y_out[u], 16 * (G // 2))
                    act.wait_ge(p_out[u], 16 * 10)
                    act.wait_ge(mod_out[u], 16 * (1 + ADA_N // 2))

            @block.vector
            def _(dve):
                ch = Chain(dve, s["dve3"])
                tt, ts, stt = dve.tensor_tensor, dve.tensor_scalar, dve.scalar_tensor_tensor

                def exp(out, x, t, ti):
                    ch.link(ts(t[0], x, 1.0 / LN2, ROUND, ALU.mult, ALU.add))
                    ch.link(ts(t[0], t[0], ROUND, None, ALU.subtract))
                    ch.link(stt(out=t[1], in0=t[0], scalar=-LN2_HI, in1=x, op0=ALU.mult, op1=ALU.add))
                    ch.link(stt(out=t[1], in0=t[0], scalar=-LN2_LO, in1=t[1], op0=ALU.mult, op1=ALU.add))
                    ch.link(ts(ti, t[0], 127.0, 1.0, ALU.add, ALU.max))
                    ch.link(ts(ti, ti, 23, None, ALU.logical_shift_left))
                    ch.link(ts(t[2], t[1], EXP_C[0], None, ALU.mult))
                    for c in EXP_C[1:]:
                        ch.link(stt(out=t[2], in0=t[2], scalar=c, in1=t[1], op0=ALU.add, op1=ALU.mult))
                    ch.link(stt(out=out, in0=t[2], scalar=1.0, in1=ti.bitcast(F32), op0=ALU.add, op1=ALU.mult))

                dve.wait_ge(s["tab_in"], 48)
                exp(dtrow[:, 2:4], dtrow[:, 0:2], [sm[0:PAIRS, j, 0:2] for j in (20, 21, 22)],
                    sm[0:PAIRS, 23, 0:2].bitcast(I32))
                dve.tensor_copy(arow[:, 2, :].rearrange("k (g p) -> k g p", g=2),
                                dtrow[:, 2:4].unsqueeze(2).broadcast_to([PAIRS, 2, NS])).then_inc(s["dt_row"], 1)
                dve.wait_ge(s["cnt_i_ok"], 1)
                ch.link(dve.tensor_copy(cnt[:, QH, :], cnt_i[:]))
                for q, w in enumerate(WINDOWS):
                    ins = ts(cnt[:, q, :], cnt[:, QH, :], float(w), None, ALU.min)
                ch.link(ins)
                dve.reciprocal(cnt[:, 0:QH, :], cnt[:, 0:QH, :]).then_inc(s["cnt_ok"], 1)

                dve.wait_ge(s["x_evac"], at["tab"] + 1)
                S = [sm[:, i, :] for i in range(24)]
                tt(S[3], S[0], S[2], ALU.mult)
                ch.link(tt(S[4], S[1], S[2], ALU.mult))
                ch.link(ts(S[11], S[4], 1.0 / TWO_PI, ROUND, ALU.mult, ALU.add))
                ch.link(ts(S[11], S[11], ROUND, None, ALU.subtract))
                ch.link(stt(out=S[7], in0=S[11], scalar=-TWO_PI_HI, in1=S[4], op0=ALU.mult, op1=ALU.add))
                ch.link(stt(out=S[7], in0=S[11], scalar=-TWO_PI_MID, in1=S[7], op0=ALU.mult, op1=ALU.add))
                ch.link(stt(out=S[7], in0=S[11], scalar=-TWO_PI_LO, in1=S[7], op0=ALU.mult, op1=ALU.add))
                ch.link(ts(S[7], S[7], 3.1415925, -3.1415925, ALU.min, ALU.max))
                ch.link(stt(out=S[8], in0=S[7], scalar=-1.0, in1=S[7], op0=ALU.mult, op1=ALU.max))
                ts(S[8], S[8], -1.0, TWO_PI / 4, ALU.mult, ALU.add).then_inc(s["arg"], 1)
                exp(S[5], S[3], [S[20], S[21], S[22]], S[23].bitcast(I32))
                ch.link(tt(S[6], S[5], S[5], ALU.mult))
                ch.link(tt(S[11], S[6], S[6], ALU.mult))
                ch.link(tt(S[6], S[11], S[11], ALU.mult))
                dve.wait_ge(s["sins"], 1)
                R, I = (lambda j: PW[:, 0, j, :]), (lambda j: PW[:, 1, j, :])
                dve.memset(PW[:, 0, 0, :], 1.0)
                dve.memset(PW[:, 1, 0, :], 0.0)
                tt(R(1), S[5], S[10], ALU.mult)
                ch.link(tt(I(1), S[5], S[9], ALU.mult))

                def cmul(outr, outi, ar, ai, br, bi, t, neg_i=False):
                    tt(t[0], ar, br, ALU.mult)
                    tt(t[1], ai, bi, ALU.mult)
                    tt(t[2], ar, bi, ALU.mult)
                    ch.link(tt(t[3], ai, br, ALU.mult))
                    tt(outr, t[0], t[1], ALU.subtract)
                    if neg_i:
                        ch.link(stt(out=outi, in0=t[2], scalar=-1.0, in1=t[3], op0=ALU.mult, op1=ALU.subtract))
                    else:
                        ch.link(tt(outi, t[2], t[3], ALU.add))

                m = 1
                while m < STEP:
                    bc = [PW[:, i, m:m + 1, :].broadcast_to([P, m, PAIRS]) for i in range(2)]
                    t4 = [tmp[:, 0, j * STEP * PAIRS:j * STEP * PAIRS + m * PAIRS].rearrange("p (m k) -> p m k", m=m)
                          for j in range(4)]
                    cmul(PW[:, 0, m + 1:2 * m + 1, :], PW[:, 1, m + 1:2 * m + 1, :], PW[:, 0, 1:m + 1, :],
                         PW[:, 1, 1:m + 1, :], bc[0], bc[1], t4)
                    m *= 2
                ch.link(ts(S[12], R(1), 1.0, None, ALU.subtract))
                tt(S[13], S[0], S[0], ALU.mult)
                ch.link(tt(S[14], S[1], S[1], ALU.mult))
                ch.link(tt(S[13], S[13], S[14], ALU.add))
                ch.link(dve.reciprocal(S[13], S[13]))
                tt(S[14], S[12], S[0], ALU.mult)
                tt(S[15], I(1), S[1], ALU.mult)
                tt(S[16], I(1), S[0], ALU.mult)
                ch.link(tt(S[17], S[12], S[1], ALU.mult))
                tt(S[14], S[14], S[15], ALU.add)
                ch.link(tt(S[16], S[16], S[17], ALU.subtract))
                tt(S[14], S[14], S[13], ALU.mult)
                ch.link(tt(S[15], S[16], S[13], ALU.mult))
                dve.wait_ge(s["b3_in"], 32)
                kb = [S[14 + i].unsqueeze(2).broadcast_to([P, PAIRS, GH]) for i in range(2)]
                NB = PAIRS * GH
                t4 = [tmp[:, 0, j * NB:(j + 1) * NB].rearrange("p (k h) -> p k h", k=PAIRS) for j in range(4)]
                cmul(Bb[:, 0], Bb[:, 1], B[:, 0], B[:, 1], kb[0], kb[1], t4)
                for hp in range(2):
                    ks = slice(8 * hp, 8 * hp + 8)
                    n = 8 * P
                    t4 = [tmp.rearrange("p a n -> p (a n)")[:, j * n:(j + 1) * n].rearrange("p (k t h) -> p k t h", k=8, h=GH)
                          for j in range(4)]
                    pb = [PW[:, i, 0:STEP, ks].rearrange("p t k -> p k t").unsqueeze(3).broadcast_to([P, 8, STEP, GH])
                          for i in range(2)]
                    bb = [Bb[:, i, ks].unsqueeze(2).broadcast_to([P, 8, STEP, GH]) for i in range(2)]
                    wo = [WB[:, i, ks].rearrange("p k (t h) -> p k t h", h=GH) for i in range(2)]
                    cmul(wo[0], wo[1], pb[0], pb[1], bb[0], bb[1], t4)
                dve.sem_inc(s["wb_ready"], 1)
                dve.wait_ge(s["x_evac"], at["C"] + 1)
                for hp in range(4):
                    ks = slice(4 * hp, 4 * hp + 4)
                    n = 4 * (STEP + 1) * GH
                    t4 = [tmp.rearrange("p a n -> p (a n)")[:, j * n:(j + 1) * n].rearrange("p (k t h) -> p k t h", k=4, h=GH)
                          for j in range(4)]
                    pb = [PW[:, i, :, ks].rearrange("p t k -> p k t").unsqueeze(3).broadcast_to([P, 4, STEP + 1, GH])
                          for i in range(2)]
                    cb = [C[:, i, ks].unsqueeze(2).broadcast_to([P, 4, STEP + 1, GH]) for i in range(2)]
                    co = [CL[:, i, ks].rearrange("p k (t h) -> p k t h", h=GH) for i in range(2)]
                    cmul(co[0], co[1], pb[0], pb[1], cb[0], cb[1], t4, neg_i=True)
                dve.sem_inc(s["cl_ready"], 1)
                dve.wait_ge(s["d3_in"], 16)
                ch.link(tt(dd, dskip[:].unsqueeze(2).broadcast_to([GH, G, GH]),
                           k.ident[0:GH, 0:GH].unsqueeze(1).broadcast_to([GH, G, GH]), ALU.mult))

                def unit(r, i, t0, t1):
                    tt(t0, r, r, ALU.mult)
                    ch.link(tt(t1, i, i, ALU.mult))
                    ch.link(tt(t0, t0, t1, ALU.add))
                    ch.link(ts(t0, t0, -0.5, 1.5, ALU.mult, ALU.add))
                    tt(r, r, t0, ALU.mult)
                    ch.link(tt(i, i, t0, ALU.mult))

                t4 = S[16:20]
                src = (S[10], S[9])
                for j in range(LOG_CH + 2):
                    dst = (ph[:, j, 0, :], ph[:, j, 1, :])
                    cmul(dst[0], dst[1], src[0], src[1], src[0], src[1], t4)
                    unit(dst[0], dst[1], S[16], S[17])
                    src = dst
                dve.wait_ge(s["x_evac"], at["KK7"] + 1)
                tt(KK[:, :, 0:GH], KK[:, :, 0:GH], dd, ALU.add).then_inc(s["kk_diag"], 1)

                dve.wait_ge(s["t_in"], 16 * STEP)
                dve.tensor_copy(E[:, 0, :, 0], ph[:, 2, 0, :])
                ch.link(dve.tensor_copy(E[:, 1, :, 0], ph[:, 2, 1, :]))
                dve.wait_ge(s["x_evac"], at[f"V{2 * PAIRS - 1}"] + 1)
                vb = VB[:].rearrange("p a k n -> p (a k n)")
                for j in range(LOG_CH):
                    m = 2 ** j
                    hm = min(m, 64)
                    for c0 in range(0, m, hm):
                        t4 = [vb[:, i * 1024:i * 1024 + PAIRS * hm].rearrange("p (k c) -> p k c", k=PAIRS) for i in range(4)]
                        bc = [ph[:, 2 + j, i, :].unsqueeze(2).broadcast_to([P, PAIRS, hm]) for i in range(2)]
                        cmul(E[:, 0, :, m + c0:m + c0 + hm], E[:, 1, :, m + c0:m + c0 + hm], E[:, 0, :, c0:c0 + hm],
                             E[:, 1, :, c0:c0 + hm], bc[0], bc[1], t4)
                p8 = [PW[:, i, STEP:STEP + 1, :].broadcast_to([P, NSEQ, PAIRS]) for i in range(2)]
                t4 = [vb[:, j * P:(j + 1) * P].rearrange("p (b k) -> p b k", b=NSEQ) for j in range(4)]
                fin_t = vb[:, 4 * P:6 * P].rearrange("p (a b k) -> p a b k", a=2, b=NSEQ)
                cmul(fin_t[:, 0], fin_t[:, 1], h0[:, 0], h0[:, 1], p8[0], p8[1], t4)
                for i in range(2):
                    ins = tt(fin_s[:, i], fin_t[:, i], H[:, i, :, 1:NSEQ + 1].rearrange("p k b -> p b k"), ALU.add)
                ch.link(ins)
                for i in range(2):
                    dve.tensor_copy(H[:, i, :, 0:NSEQ].rearrange("p k b -> p b k"), h0[:, i])
                    ins = dve.memset(H[:, i, :, NSEQ:NSEQ + 1], 0.0)
                ch.link(ins)
                n0, PER = ch.n, 8
                with dve.Fori(0, PAIRS - 1, 2) as p0:
                    ch.base, ch.n = p0 * (PER // 2) + n0, 0
                    hr, hi = [H[:, i, bass.ds(p0, 2), NSEQ + 1:NCH + 1] for i in range(2)]
                    er, ei = [E[:, i, bass.ds(p0, 2), :] for i in range(2)]
                    t = [rt[:, j] for j in range(4)]
                    tt(t[0], hr, er, ALU.mult)
                    tt(t[1], hi, ei, ALU.mult)
                    tt(t[2], hi, er, ALU.mult)
                    ch.link(tt(t[3], hr, ei, ALU.mult))
                    tt(hr, t[0], t[1], ALU.add)
                    ch.link(tt(hi, t[2], t[3], ALU.subtract))
                    for j in range(2):
                        rho = sm[:, 6, bass.ds(p0 + j, 1)].broadcast_to([P, PCH])
                        for i in range(2):
                            row = H[:, i, bass.ds(p0 + j, 1), NSEQ + 1:NCH + 1].rearrange("p a c -> p (a c)")
                            ch.link(dve.tensor_tensor_scan(rt[:, 4 + i, j, :], rho, row, 0.0, ALU.mult, ALU.add))
                    gr, gi = rt[:, 4], rt[:, 5]
                    tt(t[0], gr, er, ALU.mult)
                    tt(t[1], gi, ei, ALU.mult)
                    tt(t[2], gr, ei, ALU.mult)
                    ch.link(tt(t[3], gi, er, ALU.mult))
                    tt(hr, t[0], t[1], ALU.subtract)
                    ch.link(tt(hi, t[2], t[3], ALU.add))
                    dve.sem_inc(s["h_ready"], 1)
                assert ch.n == PER


def glu(k, a, g_d, mix_d, wo_hi, wo_lo):
    nc = k.nc
    k.stage = "glu"
    CB = BLK // STEP
    with ExitStack() as st:
        gw = k.sb(st, "gw", [P, QH, HALF])
        gw_hi = k.sb(st, "gw_hi", [P, QH, HALF], F32R)
        gw_lo = k.sb(st, "gw_lo", [P, QH, HALF], F32R)
        gb = k.sb(st, "gb", [P, QH])
        gf = k.sb(st, "gf", [P, 3, QH, BLK])
        g_hi = k.sb(st, "g_hi", [P, 2, QH, BLK], F32R)
        g_lo = k.sb(st, "g_lo", [P, 2, QH, BLK], F32R)
        sg = k.sb(st, "sg", [P, 2, BLK])
        mo = k.sb(st, "mo", [P, 2, BLK])
        wraw = k.sb(st, "wraw", [P, 2, KD, BLK // 2])
        psG = k.ps(st, "psG", [P, 2, BLK])
        gw_in, gb_in, gw_h, gw_l, ghi, glo, g_mm, sg_done, mo_done, wo_h, wo_l = [
            k.sem(n) for n in ("gw_in", "gb_in", "gw_h", "gw_l", "ghi", "glo", "g_mm", "sg_done", "mo_done",
                               "wo_h", "wo_l")]
        g_in = [k.sem(f"g_in{i}") for i in range(3)]
        mo_out = [k.sem(f"mo_out{i}") for i in range(2)]
        wraw_in = [k.sem(f"wraw_in{i}") for i in range(2)]
        WP = D // (BLK // 2)
        with nc.Block() as block:

            def g_load(sp, b, u, w):
                c0 = b * CB + NSEQ if w == BLK else 0
                for q in range(QH):
                    sp.dma_start(gf[:, u, q, 0:w].rearrange("p (s c) -> p s c", s=STEP),
                                 g_d[q * P:(q + 1) * P, :, bass.ds(c0, w // STEP)]).then_inc(g_in[u], 16)

            @block.sync
            def _(sp):
                sp.dma_start(gw[:], a["glu_w"][0].rearrange("(q p) n -> p q n", p=P)).then_inc(gw_in, 16)
                for u in range(3):
                    g_load(sp, u, u, BLK)
                sp.dma_start(gb[:], a["glu_b"][0].rearrange("(q p) -> p q", p=P),
                             allow_slow_non_contiguous=True).then_inc(gb_in, 16)
                for b in range(3, NBLK + 1):
                    sp.wait_ge(mo_done, 4 * (b - 2))
                    g_load(sp, b, b % 3, BLK if b < NBLK else TS)
                for u in range(2):
                    sp.wait_ge(mo_out[u], 16 * 2 * (NBLK + 1))

            @block.gpsimd
            def _(pool):
                w = a["w_out"][0].rearrange("(k p) n -> p k n", p=P)
                pool.wait_ge(g_in[0], 16 * QH)
                for i in range(WP):
                    if i >= 2:
                        pool.wait_ge(wo_l, i - 1)
                    pool.dma_start(wraw[:, i % 2], w[:, :, i * BLK // 2:(i + 1) * BLK // 2]).then_inc(wraw_in[i % 2], 16)

            def store(act, n):
                b, m = divmod(n, 4)
                w = BLK if b < NBLK else TS
                act.wait_ge(mo_done, n + 1)
                act.dma_start(mix_d[HALF + m * P:HALF + (m + 1) * P, b * BLK:b * BLK + w], mo[:, n % 2, 0:w]
                              ).then_inc(mo_out[n % 2], 16)

            @block.scalar
            def _(act):
                act.wait_ge(gw_in, 16)
                act.copy(gw_hi[:], gw[:]).then_inc(gw_h, 1)

                def split_hi(b):
                    u, w = b % 2, BLK if b < NBLK else TS
                    act.wait_ge(g_in[b % 3], 16 * QH * (b // 3 + 1))
                    if b >= 2:
                        act.wait_ge(g_mm, 4 * (b - 1))
                    act.copy(g_hi[:, u, :, 0:w], gf[:, b % 3, :, 0:w]).then_inc(ghi, 1)

                split_hi(0)
                act.wait_ge(gb_in, 16)
                for b in range(NBLK + 1):
                    u, w = b % 2, BLK if b < NBLK else TS
                    for m in range(QH):
                        if m == 1 and b < NBLK:
                            split_hi(b + 1)
                        if m == 3 and b < WP:
                            act.wait_ge(wraw_in[b % 2], 16 * (b // 2 + 1))
                            act.copy(wo_hi[:, :, b * BLK // 2:(b + 1) * BLK // 2], wraw[:, b % 2]).then_inc(wo_h, 1)
                        n = 4 * b + m
                        act.wait_ge(g_mm, n + 1)
                        if n >= 2:
                            act.wait_ge(mo_done, n - 1)
                        act.activation(sg[:, n % 2, 0:w], psG[:, n % 2, 0:w], ACT.Sigmoid,
                                       bias=gb[:, m:m + 1]).then_inc(sg_done, 1)
                        if n:
                            store(act, n - 1)
                store(act, 4 * NBLK + 3)

            @block.vector
            def _(dve):
                dve.wait_ge(gw_h, 1)
                dve.tensor_tensor(gw_lo[:], gw[:], gw_hi[:].bitcast(F32), ALU.subtract).then_inc(gw_l, 1)

                def split_lo(b):
                    u, w = b % 2, BLK if b < NBLK else TS
                    dve.wait_ge(ghi, b + 1)
                    dve.tensor_tensor(g_lo[:, u, :, 0:w], gf[:, b % 3, :, 0:w], g_hi[:, u, :, 0:w].bitcast(F32),
                                      ALU.subtract).then_inc(glo, 1)

                split_lo(0)
                for b in range(NBLK + 1):
                    u, w = b % 2, BLK if b < NBLK else TS
                    for m in range(QH):
                        if m == 1 and b < NBLK:
                            split_lo(b + 1)
                        if m == 3 and b < WP:
                            dve.wait_ge(wo_h, b + 1)
                            c = slice(b * BLK // 2, (b + 1) * BLK // 2)
                            dve.tensor_tensor(wo_lo[:, :, c], wraw[:, b % 2], wo_hi[:, :, c].bitcast(F32), ALU.subtract
                                              ).then_inc(wo_l, 1)
                        n = 4 * b + m
                        dve.wait_ge(sg_done, n + 1)
                        if n >= 2:
                            dve.wait_ge(mo_out[n % 2], 16 * (n // 2))
                        dve.tensor_tensor(mo[:, n % 2, 0:w].rearrange("p (c s) -> p s c", s=STEP),
                                          gf[:, b % 3, m, 0:w].rearrange("p (s c) -> p s c", s=STEP),
                                          sg[:, n % 2, 0:w].rearrange("p (s c) -> p s c", s=STEP),
                                          ALU.mult).then_inc(mo_done, 1)

            @block.tensor
            def _(pe):
                pe.wait_ge(gw_l, 1)
                for b in range(NBLK + 1):
                    u, w = b % 2, BLK if b < NBLK else TS
                    pe.wait_ge(glo, b + 1)
                    for m in range(QH):
                        n = 4 * b + m
                        if n >= 2:
                            pe.wait_ge(sg_done, n - 1)
                        for q in range(QH):
                            mm = matmul3(pe, psG[:, n % 2, 0:w], gw_hi[:, q, m * P:(m + 1) * P],
                                         gw_lo[:, q, m * P:(m + 1) * P], g_hi[:, u, q, 0:w], g_lo[:, u, q, 0:w],
                                         q == 0, q == QH - 1)
                        mm.then_inc(g_mm, 1)


def out_projection(k, a, mod_d, mix_d, x2_d, h2_d, wo_hi, wo_lo, lg):
    nc = k.nc
    k.stage = "out_projection"
    NR = 4 + NE
    with ExitStack() as st:
        mixf = k.sb(st, "mixf", [P, 2, KD, P])
        m_hi = k.sb(st, "m_hi", [P, 2, KD, P], F32R)
        m_lo = k.sb(st, "m_lo", [P, 2, KD, P], F32R)
        xt = k.sb(st, "xt", [P, 2, D])
        tmp = k.sb(st, "tmp4", [P, 2, D])
        h2 = k.sb(st, "h2", [P, 2, D])
        junk = k.sb(st, "junk4", [P, D])
        h2T = k.sb(st, "h2T", [P, KD, P])
        g1 = k.sb(st, "g1", [P, 2, D])
        sh2 = k.sb(st, "sh2", [P, 2, D])
        a2 = k.sb(st, "a2", [P, 2, D])
        n2 = k.sb(st, "n2", [P, D])
        rw = k.sb(st, "rw", [P, KD, NR])
        rb = k.sb(st, "rb", [P, NR])
        ss = k.sb(st, "ss4", [P, 2, 4])
        psO = k.ps(st, "psO", [P, 2, D])
        psH = k.ps(st, "psH", [P, D])
        psR = k.ps(st, "psR", [P, NR])
        (rows_in, rw_in, a2_done, mhi, mlo, o_mm, o_tmp, x2_done, sq, ms, rt, rstd, h2_half, h2_done, h_t, h_ev, r_mm,
         lg_done, mz) = [k.sem("o_" + n) for n in (
            "rows_in", "rw_in", "a2_done", "mhi", "mlo", "mm", "tmp", "x2_done", "sq", "ms", "rt", "rstd",
            "h2_half", "h2_done", "h_t", "h_ev", "r_mm", "lg_done", "mz")]
        m_in = [k.sem(f"m_in{i}") for i in range(2)]
        xt_in = [k.sem(f"xt_in{i}") for i in range(2)]
        xt_out = [k.sem(f"xt_out{i}") for i in range(2)]
        h2_out = [k.sem(f"h2_out{i}") for i in range(2)]
        LAST = NT - 1
        mixv = mix_d.rearrange("(k p) n -> p k n", p=P)
        x_s = a["x_sample"].rearrange("b t d -> (b t) d")

        with nc.Block() as block:

            @block.sync
            def _(sp):
                def load_mix(t, u):
                    c0 = t * P if isinstance(t, int) else sp.snap(t * P)
                    sp.dma_start(mixf[:, u], mixv[:, :, bass.ds(c0, P)]).then_inc(m_in[u], 16)

                def load_x(t, u):
                    c0 = t * P if isinstance(t, int) else sp.snap(t * P)
                    sp.dma_start(xt[:, u, :], a["x_prompt"][0, bass.ds(c0, P), :]).then_inc(xt_in[u], 16)

                def store(t, u, rows):
                    c0 = t * P if isinstance(t, int) else sp.snap(t * P)
                    sp.wait_ge(h2_done, t + 1)
                    sp.dma_start(x2_d[bass.ds(c0, rows), :], xt[0:rows, u, :]).then_inc(xt_out[u], 16)
                    sp.dma_start(h2_d[bass.ds(c0, rows), :], h2[0:rows, u, :]).then_inc(h2_out[u], 16)

                for u in range(2):
                    load_mix(u, u)
                for i, (dst, c0) in enumerate(((g1, 2 * D), (sh2, 3 * D), (a2, 4 * D))):
                    sp.dma_start(dst[:, 0, :], mod_d[0:1, c0:c0 + D].broadcast_to([P, D])).then_inc(rows_in, 16)
                    sp.dma_start(dst[0:TS, 1, :], mod_d[1:ROWS, c0:c0 + D].unsqueeze(1)
                                 .broadcast_to([NSEQ, LSEQ, D])).then_inc(rows_in, 16)
                sp.dma_start(n2[:], a["norm2_g"].broadcast_to([P, D])).then_inc(rows_in, 16)
                sp.dma_start(rw[:, :, 0:4], a["router_w1"][0].rearrange("(k p) n -> p k n", p=P)).then_inc(rw_in, 16)
                for g in range(4):
                    sp.dma_start(rw[:, :, 4 + 4 * g:8 + 4 * g], a["router_w2"][0, g].rearrange("(k p) n -> p k n", p=P)
                                 ).then_inc(rw_in, 16)
                sp.dma_start(rb[:, 0:4], a["router_b1"].broadcast_to([P, 4])).then_inc(rw_in, 16)
                sp.dma_start(rb[:, 4:NR], a["router_b2"].rearrange("a g e -> a (g e)").broadcast_to([P, NE])
                             ).then_inc(rw_in, 16)

                for u in range(2):
                    load_x(u, u)
                with sp.Fori(0, LAST - 3, 2) as t:
                    for u in range(2):
                        sp.wait_ge(mlo, t + u + 1)
                        load_mix(t + u + 2, u)
                        store(t + u, u, P)
                        sp.wait_ge(xt_out[u], 8 * t + 16)
                        load_x(t + u + 2, u)
                sp.wait_ge(mz, 1)
                sp.dma_start(mixf[:, 0, :, 0:TS], mixv[:, :, TP:TOK]).then_inc(m_in[0], 16)
                store(LAST - 2, 0, P)
                sp.wait_ge(xt_out[0], 16 * (LAST // 2))
                sp.dma_start(xt[0:TS, 0, :], x_s).then_inc(xt_in[0], 16)
                store(LAST - 1, 1, P)
                store(LAST, 0, TS)
                for u in range(2):
                    sp.wait_ge(xt_out[u], 16 * ((NT + 1 - u) // 2))
                    sp.wait_ge(h2_out[u], 16 + 16 * ((NT + 1 - u) // 2))

            @block.scalar
            def _(act):
                def split_hi(t, u):
                    act.wait_ge(m_in[u], 8 * t + 16 - 8 * u)
                    if not isinstance(t, int) or t >= 1:
                        act.wait_ge(o_mm, t)
                    act.copy(m_hi[:, u], mixf[:, u]).then_inc(mhi, 1)

                def norm(t, u, rows):
                    act.wait_ge(x2_done, t + 1)
                    act.activation(junk[0:rows, :], xt[0:rows, u, :], ACT.Square,
                                   accum_out=ss[0:rows, u, 0:1]).then_inc(sq, 1)
                    act.wait_ge(ms, t + 1)
                    act.activation(ss[0:rows, u, 2:3], ss[0:rows, u, 1:2], ACT.Sqrt).then_inc(rt, 1)

                def turned(t, u, rows):
                    act.wait_ge(h_t, t + 1)
                    act.wait_ge(r_mm, t + 1)
                    act.copy(h2T[:, :, 0:rows], psH[:].rearrange("p (k n) -> p k n", k=KD)[:, :, 0:rows]
                             ).then_inc(h_ev, 1)

                split_hi(0, 0)
                split_hi(1, 1)
                with act.Fori(0, LAST - 3, 2) as t:
                    for u in range(2):
                        norm(t + u, u, P)
                        split_hi(t + u + 2, u)
                        turned(t + u, u, P)
                norm(LAST - 2, 0, P)
                split_hi(LAST, 0)
                turned(LAST - 2, 0, P)
                norm(LAST - 1, 1, P)
                turned(LAST - 1, 1, P)
                norm(LAST, 0, TS)
                turned(LAST, 0, TS)

            @block.vector
            def _(dve):
                tt = dve.tensor_tensor

                def split_lo(t, u):
                    dve.wait_ge(mhi, t + 1)
                    tt(m_lo[:, u], mixf[:, u], m_hi[:, u].bitcast(F32), ALU.subtract).then_inc(mlo, 1)

                split_lo(0, 0)
                split_lo(1, 1)
                dve.wait_ge(rows_in, 16 * 7)
                for i, r in ((0, P), (1, TS)):
                    dve.scalar_tensor_tensor(out=a2[0:r, i, :], in0=a2[0:r, i, :], scalar=1.0, in1=n2[0:r, :],
                                             op0=ALU.add, op1=ALU.mult).then_inc(a2_done, 1)
                dve.wait_ge(rw_in, 16 * 7)
                dve.memset(lg[:, LAST, :], 0.0).then_inc(a2_done, 1)
                dve.wait_ge(a2_done, 3)

                def tile(t, u, rows, kind):
                    dve.wait_ge(o_mm, t + 1 + 1)
                    dve.wait_ge(xt_in[u], 8 * t + 16 - 8 * u)
                    r = slice(0, rows)
                    tt(tmp[r, u, :], psO[r, u, :], g1[r, kind, :], ALU.mult).then_inc(o_tmp, 1)
                    dve.wait_ge(o_tmp, t + 1)
                    tt(xt[r, u, :], xt[r, u, :], tmp[r, u, :], ALU.add).then_inc(x2_done, 1)
                    dve.wait_ge(sq, t + 1)
                    dve.tensor_scalar(ss[r, u, 1:2], ss[r, u, 0:1], 1.0 / D, EPS, ALU.mult, ALU.add).then_inc(ms, 1)
                    dve.wait_ge(rt, t + 1)
                    dve.reciprocal(ss[r, u, 3:4], ss[r, u, 2:3]).then_inc(rstd, 1)
                    dve.wait_ge(rstd, t + 1)
                    dve.wait_ge(h2_out[u], 8 * t + 16 - 8 * u)
                    dve.scalar_tensor_tensor(out=tmp[r, u, :], in0=xt[r, u, :], scalar=ss[r, u, 3:4],
                                             in1=a2[r, kind, :], op0=ALU.mult, op1=ALU.mult).then_inc(h2_half, 1)
                    dve.wait_ge(h2_half, t + 1)
                    tt(h2[r, u, :], tmp[r, u, :], sh2[r, kind, :], ALU.add).then_inc(h2_done, 1)

                def logits(t, rows):
                    r = slice(0, rows)
                    dve.wait_ge(r_mm, t + 1 + 1)
                    tt(lg[r, bass.ds(t, 1), :].rearrange("p a n -> p (a n)") if not isinstance(t, int) else lg[r, t, :],
                       psR[r, :], rb[r, :], ALU.add).then_inc(lg_done, 1)

                for u in range(2):
                    dve.sem_inc(h2_out[u], 16)
                dve.sem_inc(lg_done, 1)
                tile(0, 0, P, 0)
                split_lo(2, 0)
                with dve.Fori(1, LAST - 4, 2) as t:
                    for u in (1, 0):
                        d = 1 - u
                        tile(t + d, u, P, 0)
                        split_lo(t + d + 2, u)
                        logits(t + d - 1, P)
                dve.wait_ge(mlo, LAST - 1)
                dve.memset(mixf[:, 0, :, TS:P], 0.0).then_inc(mz, 1)
                for t in (LAST - 3, LAST - 2):
                    tile(t, t % 2, P, 0)
                    split_lo(t + 2, t % 2)
                    logits(t - 1, P)
                tile(LAST - 1, 1, P, 0)
                logits(LAST - 2, P)
                tile(LAST, 0, TS, 1)
                logits(LAST - 1, P)
                logits(LAST, TS)

            @block.tensor
            def _(pe):
                pe.sem_inc(o_mm, 1)
                pe.sem_inc(r_mm, 1)

                def product(t, u, halves=(0, 1)):
                    if 0 in halves:
                        pe.wait_ge(mlo, t + 1)
                        if not isinstance(t, int) or t >= 2:
                            pe.wait_ge(o_tmp, t - 1)
                    for n in halves:
                        for q in range(KD):
                            c = slice(n * BLK, (n + 1) * BLK)
                            mm = matmul3(pe, psO[:, u, c], m_hi[:, u, q, :], m_lo[:, u, q, :], wo_hi[:, q, c],
                                         wo_lo[:, q, c], q == 0, q == KD - 1)
                    if 1 in halves:
                        mm.then_inc(o_mm, 1)

                def turn(t, u, rows):
                    pe.wait_ge(h2_done, t + 1)
                    for q in range(KD):
                        mm = pe.transpose(psH[:, q * P:q * P + rows], h2[0:rows, u, q * P:(q + 1) * P],
                                          k.ident[0:rows, 0:rows])
                    mm.then_inc(h_t, 1)

                def route(t, rows):
                    pe.wait_ge(h_ev, t + 1)
                    pe.wait_ge(lg_done, t + 1)
                    for q in range(KD):
                        mm = pe.matmul(psR[0:rows, :], h2T[:, q, 0:rows], rw[:, q, :], start=q == 0, stop=q == KD - 1)
                    mm.then_inc(r_mm, 1)

                product(0, 0)
                product(1, 1)
                pe.wait_ge(rw_in, 16 * 7)
                with pe.Fori(0, LAST - 3, 2) as t:
                    for u in range(2):
                        turn(t + u, u, P)
                        product(t + u + 2, u, (0,))
                        route(t + u, P)
                        product(t + u + 2, u, (1,))
                turn(LAST - 2, 0, P)
                product(LAST, 0, (0,))
                route(LAST - 2, P)
                product(LAST, 0, (1,))
                turn(LAST - 1, 1, P)
                route(LAST - 1, P)
                turn(LAST, 0, TS)
                route(LAST, TS)


FQ = FH // P


class ExpertWeights:

    def __init__(self, k, st):
        self.wraw = k.sb(st, "we_raw", [P, 2, KD, 2 * FH])
        self.draw = k.sb(st, "wd_raw", [P, 2, FQ, D])
        self.w_hi = k.sb(st, "we_hi", [P, 2, KD, 2 * FH], F32R)
        self.w_lo = k.sb(st, "we_lo", [P, 2, KD, 2 * FH], F32R)
        self.d_hi = k.sb(st, "wd_hi", [P, 2, FQ, D], F32R)
        self.d_lo = k.sb(st, "wd_lo", [P, 2, FQ, D], F32R)
        self.whi, self.wlo, self.dhi, self.dlo = [k.sem("e_" + n) for n in ("whi", "wlo", "dhi", "dlo")]
        self.raw_in = [k.sem(f"we_in{i}") for i in range(2)]
        self.draw_in = [k.sem(f"wd_in{i}") for i in range(2)]
        self.xg = k.sb(st, "xg", [P, 2, D])
        self.ic = k.sb(st, "idx_col", [P, 2, 1], I32)
        self.ic_ok, self.fence = k.sem("e_ic_ok"), k.sem("e_fence")
        self.xg_in = [k.sem(f"xg_in{i}") for i in range(2)]

    def gather(self, pool, R, h2_d, t, u):
        pool.tensor_copy(self.ic[:, u, :], R.idx[:, bass.ds(t, 1)]).then_inc(self.ic_ok, 1)
        pool.wait_ge(self.ic_ok, t + 1)
        pool.sem_inc(self.fence, 1)
        pool.indirect_dma_start(self.xg[:, u, :], None, h2_d, bass.IndirectOffsetOnAxis(self.ic[:, u, :], 0)
                                ).then_inc(self.xg_in[u], 16)

    def load(self, sp, a, e):
        u = e % 2
        if e >= 2:
            sp.wait_ge(self.wlo, 4 * (e - 1))
        for i, n in enumerate(("exp_w_gate", "exp_w_up")):
            sp.dma_start(self.wraw[:, u, :, i * FH:(i + 1) * FH], a[n][0, e].rearrange("(k p) f -> p k f", p=P)
                         ).then_inc(self.raw_in[u], 16)
        if e >= 2:
            sp.wait_ge(self.dlo, e - 1)
        sp.dma_start(self.draw[:, u], a["exp_w_down"][0, e].rearrange("(k p) d -> p k d", p=P)
                     ).then_inc(self.draw_in[u], 16)


NCOL = 52


def routing(k, a, h2_d, lg, R, W):
    nc = k.nc
    k.stage = "routing"
    with ExitStack() as st:
        sb = lambda n, s, d=F32: k.sb(st, n, s, d)
        io_i = sb("io_i", [P, P], I32)
        tk_i = sb("tk_i", [P, NT], I32)
        io_f = sb("io_f", [P, P])
        tk_f = sb("tk_f", [P, NT])
        ones = sb("ones", [P, P])
        upper = sb("upper", [P, P])
        prio = sb("prio", [P, 4])
        m1 = sb("m1", [P, NT])
        ex = sb("ex", [P, NT, 4])
        sm = sb("sm", [P, NT])
        ptop = sb("ptop", [P, NT])
        key = sb("key", [P, NT, 4])
        km = sb("km", [P, NT])
        ohg = sb("ohg", [P, NT, 4])
        l2s = sb("l2s", [P, NT, 4, 4])
        l2 = sb("l2", [P, NT, 4])
        oh = sb("oh", [P, 2, NT, 4])
        v = sb("v", [P, 2, NT])
        msk = sb("msk", [P, NT, 4])
        gt = sb("gt", [P, NT, 2])
        E = sb("E", [P, 2, NT, 4, 4])
        M = sb("M", [P, NT, NE])
        pre = sb("pre", [P, NT + 1, NE])
        base = sb("base", [P, NT, NE])
        n_i = sb("n_i", [P, NE], I32)
        n_f = sb("n_f", [P, NE])
        pz = sb("pz", [P, 2, 2 * NE])
        st_f = sb("st_f", [P, NE])
        pe_f = sb("pe_f", [P, 2, NT, NE])
        posf = sb("posf", [P, NT, 2])
        col_i = sb("col_i", [P, NT, 2], I32)
        row_i = sb("row_i", [P, NT, 2], I32)
        col_f = sb("col_f", [P, NT, 2])
        row_f = sb("row_f", [P, NT, 2])
        J = sb("J", [P, NT, 2, P])
        A = sb("A", [P, 2, NT, 2, NCOL])
        te = sb("te", [1, NCOL, NE])
        tf = sb("tf", [1, 2, NCOL])
        t_i = sb("t_i", [1, 1], I32)
        tl_f = sb("tl_f", [1, 1])
        psR = k.ps(st, "psRank", [P, NT * NE])
        psT = k.ps(st, "psTot", [P, NT * NE])
        psS = k.ps(st, "psSlot", [P, 2 * NCOL])
        c, con, ex_done, choices, rank_mm, slots_ready, slot_mm, mx, idx_ok = [k.sem("r_" + n) for n in (
            "chain", "con", "ex_done", "choices", "rank_mm", "slots_ready", "slot_mm", "mx", "idx_ok")]

        with nc.Block() as block:

            @block.gpsimd
            def _(pool):
                pool.iota(io_i[:], [[1, P]], base=0, channel_multiplier=0).then_inc(con, 1)
                pool.iota(tk_i[:], [[P, NT]], base=0, channel_multiplier=1).then_inc(con, 1)
                pool.memset(ones[:], 1.0).then_inc(con, 1)
                pool.wait_ge(con, 3)
                pool.affine_select(out=upper[:], in_=ones[:], compare_op=ALU.is_gt, fill=0.0, base=0,
                                   pattern=[[1, P]], channel_multiplier=-1).then_inc(con, 1)
                pool.wait_ge(idx_ok, 1)
                for t in range(2):
                    W.gather(pool, R, h2_d, t, t)

            @block.sync
            def _(sp):
                for e in range(2):
                    W.load(sp, a, e)

            @block.scalar
            def _(act):
                act.wait_ge(mx, 1)
                act.activation(ex[:], key[:], ACT.Exp).then_inc(ex_done, 1)
                act.wait_ge(mx, 2)
                act.activation(v[:, 1, :], v[:, 1, :], ACT.Exp).then_inc(ex_done, 1)
                act.wait_ge(W.raw_in[0], 32)
                for h in range(4):
                    act.copy(W.w_hi[:, 0, 2 * h:2 * h + 2, :], W.wraw[:, 0, 2 * h:2 * h + 2, :]).then_inc(W.whi, 1)
                act.wait_ge(W.draw_in[0], 16)
                act.copy(W.d_hi[:, 0], W.draw[:, 0]).then_inc(W.dhi, 1)

            @block.vector
            def _(dve):
                ch = Chain(dve, c)
                tt = lambda o, x, y, op: ch.link(dve.tensor_tensor(o, x, y, op))
                ts = lambda o, x, s1, s2, o1, *o2: ch.link(dve.tensor_scalar(o, x, s1, s2, o1, *o2))
                cp = lambda o, x: ch.link(dve.tensor_copy(o, x))
                red = lambda o, x, op: ch.link(dve.tensor_reduce(o, x, AX_X, op))
                b4 = lambda x: x.unsqueeze(2).broadcast_to([P, NT, 4])
                dve.wait_ge(con, 4)
                cp(io_f[:], io_i[:])
                cp(tk_f[:], tk_i[:])
                ch.link(dve.memset(tk_f[TS:P, NT - 1:NT], 0.0))
                ts(prio[:], io_f[:, 0:4], -1.0, 4.0, ALU.mult, ALU.add)
                pr = prio[:].unsqueeze(1).broadcast_to([P, NT, 4])

                def first_max(oh_out, x, m):
                    red(m, x, ALU.max)
                    tt(key[:], x, b4(m), ALU.is_equal)
                    tt(key[:], key[:], pr, ALU.mult)
                    red(km[:], key[:], ALU.max)
                    tt(oh_out, key[:], b4(km[:]), ALU.is_equal)

                g4 = lg[:, :, 0:4]
                first_max(ohg[:], g4, m1[:])
                dve.tensor_tensor(key[:], g4, b4(m1[:]), ALU.subtract).then_inc(mx, 1)
                dve.wait_ge(ex_done, 1)
                red(sm[:], ex[:], ALU.add)
                ch.link(dve.reciprocal(ptop[:], sm[:]))
                tt(l2s[:], lg[:, :, 4:20].rearrange("p t (g e) -> p t g e", g=4),
                   ohg[:].unsqueeze(3).broadcast_to([P, NT, 4, 4]), ALU.mult)
                red(l2[:], l2s[:].rearrange("p t g e -> p t e g"), ALU.add)
                first_max(oh[:, 0], l2[:], v[:, 0, :])
                ts(msk[:], oh[:, 0], -1.0, 1.0, ALU.mult, ALU.add)
                tt(msk[:], msk[:], l2[:], ALU.mult)
                ts(key[:], oh[:, 0], -3.0e38, None, ALU.mult)
                tt(msk[:], msk[:], key[:], ALU.add)
                first_max(oh[:, 1], msk[:], v[:, 1, :])
                dve.tensor_tensor(v[:, 1, :], v[:, 1, :], v[:, 0, :], ALU.subtract).then_inc(mx, 1)
                for i in range(2):
                    tt(E[:, i], ohg[:].unsqueeze(3).broadcast_to([P, NT, 4, 4]),
                       oh[:, i].unsqueeze(2).broadcast_to([P, NT, 4, 4]), ALU.mult)
                    ch.link(dve.memset(E[TS:P, i, NT - 1:NT], 0.0))
                Ef = [E[:, i].rearrange("p t g e -> p t (g e)") for i in range(2)]
                dve.tensor_tensor(M[:], Ef[0], Ef[1], ALU.add).then_inc(choices, 1)
                dve.wait_ge(ex_done, 2)
                ts(sm[:], v[:, 1, :], 1.0, None, ALU.add)
                ch.link(dve.reciprocal(sm[:], sm[:]))
                tt(gt[:, :, 0:1].rearrange("p t a -> p (t a)"), sm[:], ptop[:], ALU.mult)
                tt(gt[:, :, 1:2].rearrange("p t a -> p (t a)"), gt[:, :, 0:1].rearrange("p t a -> p (t a)"),
                   v[:, 1, :], ALU.mult)
                ch.link(dve.memset(gt[TS:P, NT - 1:NT, :], 0.0))
                ch.link(dve.memset(pre[:, 0, :], 0.0))
                dve.wait_ge(rank_mm, 1)
                for t in range(NT):
                    tt(pre[:, t + 1, :], pre[:, t, :], psT[:, t * NE:(t + 1) * NE], ALU.add)
                ts(n_f[:], pre[:, NT, :], float(P - 1), None, ALU.add)
                cp(n_i[:], n_f[:])
                ts(n_i[:], n_i[:], 7, None, ALU.arith_shift_right)
                cp(n_f[:], n_i[:])
                ts(n_f[:], n_f[:], 1.0, None, ALU.max)
                ch.link(dve.memset(pz[:], 0.0))
                cp(pz[:, 0, NE:], n_f[:])
                for i in range(4):
                    tt(pz[:, 1 - i % 2, NE:], pz[:, i % 2, NE:], pz[:, i % 2, NE - 2 ** i:2 * NE - 2 ** i], ALU.add)
                end_f = pz[:, 0, NE:]
                tt(st_f[:], end_f, n_f[:], ALU.subtract)
                ts(n_f[:], st_f[:], float(P), None, ALU.mult)
                tt(base[:], pre[:, 0:NT, :], psR[:].rearrange("p (t e) -> p t e", e=NE), ALU.add)
                tt(base[:], base[:], n_f[:].unsqueeze(1).broadcast_to([P, NT, NE]), ALU.add)
                for i in range(2):
                    tt(pe_f[:, i], Ef[i], base[:], ALU.mult)
                    red(posf[:, :, i:i + 1].rearrange("p t a -> p (t a)"), pe_f[:, i], ALU.add)
                cp(R.pos[:], posf[:])
                ts(col_i[:], R.pos[:], 7, None, ALU.arith_shift_right)
                ts(row_i[:], R.pos[:], P - 1, None, ALU.bitwise_and)
                cp(col_f[:], col_i[:])
                cp(row_f[:], row_i[:])
                b2 = lambda x, n: x.unsqueeze(3).broadcast_to([P, NT, 2, n])
                tt(J[:], b2(row_f[:], P), io_f[:].unsqueeze(1).unsqueeze(1).broadcast_to([P, NT, 2, P]), ALU.is_equal)
                tt(A[:, 1], b2(col_f[:], NCOL), io_f[:, 0:NCOL].unsqueeze(1).unsqueeze(1)
                   .broadcast_to([P, NT, 2, NCOL]), ALU.is_equal)
                tt(A[:, 0], A[:, 1], tk_f[:].unsqueeze(2).unsqueeze(2).broadcast_to([P, NT, 2, NCOL]), ALU.mult)
                dve.tensor_tensor(A[:, 1], A[:, 1], b2(gt[:], NCOL), ALU.mult).then_inc(slots_ready, 1)
                cp(t_i[:], end_f[0:1, NE - 1:NE])
                ts(R.tab[0:1, 0:1], t_i[:], 1, 1, ALU.arith_shift_right, ALU.logical_shift_left)
                cp(tl_f[:], R.tab[0:1, 0:1])
                ts(tl_f[:], tl_f[:], -1.0, float(MAXT + 1), ALU.mult, ALU.add)
                cp(R.tab[0:1, 1 + 2 * NCOL:], tl_f[:])
                io3 = io_f[0:1, 0:NCOL].unsqueeze(2).broadcast_to([1, NCOL, NE])
                tt(te[:], io3, end_f[0:1, :].unsqueeze(1).broadcast_to([1, NCOL, NE]), ALU.is_ge)
                red(tf[:, 0, :], te[:], ALU.add)
                ts(tf[:, 0, :], tf[:, 0, :], float(NE - 1), None, ALU.min)
                tt(te[:], io3, st_f[0:1, :].unsqueeze(1).broadcast_to([1, NCOL, NE]), ALU.is_equal)
                red(tf[:, 1, :], te[:, :, 0:NE - 1], ALU.add)
                tt(te[:, :, 0:1].rearrange("p n a -> p (n a)")[:, 0:NCOL - 1], tf[:, 1, 1:NCOL], tf[:, 1, 1:NCOL], ALU.add)
                tt(tf[:, 1, 0:NCOL - 1], tf[:, 1, 0:NCOL - 1],
                   te[:, :, 0:1].rearrange("p n a -> p (n a)")[:, 0:NCOL - 1], ALU.add)
                ts(te[:, :, 0:1].rearrange("p n a -> p (n a)"), tf[:, 0, :], 4.0, None, ALU.mult)
                tt(tf[:, 1, :], tf[:, 1, :], te[:, :, 0:1].rearrange("p n a -> p (n a)"), ALU.add)
                cp(R.tab[0:1, 1:1 + 2 * NCOL], tf[:].rearrange("p a n -> p (a n)"))
                dve.wait_ge(slot_mm, 1)
                dve.tensor_copy(R.idx[:], psS[:, 0:NCOL]).then_inc(idx_ok, 1)
                dve.tensor_copy(R.gate[:], psS[:, NCOL:2 * NCOL])
                dve.wait_ge(W.whi, 4)
                for h in range(4):
                    q = slice(2 * h, 2 * h + 2)
                    dve.tensor_tensor(W.w_lo[:, 0, q, :], W.wraw[:, 0, q, :], W.w_hi[:, 0, q, :].bitcast(F32),
                                      ALU.subtract).then_inc(W.wlo, 1)
                dve.wait_ge(W.dhi, 1)
                dve.tensor_tensor(W.d_lo[:, 0], W.draw[:, 0], W.d_hi[:, 0].bitcast(F32), ALU.subtract
                                  ).then_inc(W.dlo, 1)

            @block.tensor
            def _(pe):
                pe.wait_ge(choices, 1)
                Mf = M[:].rearrange("p t e -> p (t e)")
                pe.matmul(psT[:], ones[:], Mf, start=True, stop=True)
                pe.matmul(psR[:], upper[:], Mf, start=True, stop=True).then_inc(rank_mm, 1)
                pe.wait_ge(slots_ready, 1)
                for t in range(NT):
                    for i in range(2):
                        mm = pe.matmul(psS[:], J[:, t, i, :], A[:, :, t, i, :],
                                       start=t == 0 and i == 0, stop=t == NT - 1 and i == 1)
                mm.then_inc(slot_mm, 1)


def experts(k, a, h2_d, o_d, R, W):
    nc = k.nc
    k.stage = "experts"
    with ExitStack() as st:
        wraw, draw, w_hi, w_lo, d_hi, d_lo = W.wraw, W.draw, W.w_hi, W.w_lo, W.d_hi, W.d_lo
        raw_in, draw_in, whi, wlo, dhi, dlo = W.raw_in, W.draw_in, W.whi, W.wlo, W.dhi, W.dlo
        xg, xg_in = W.xg, W.xg_in
        x_hi = k.sb(st, "x_hi", [P, 2, KD, P], F32R)
        x_lo = k.sb(st, "x_lo", [P, 2, KD, P], F32R)
        sg = k.sb(st, "sg_e", [P, FH])
        hid = k.sb(st, "hid", [P, 2, FH])
        t_hi = k.sb(st, "hT_hi", [P, FQ, P], F32R)
        t_lo = k.sb(st, "hT_lo", [P, FQ, P], F32R)
        osb = k.sb(st, "o_sb", [P, 2, D])
        psG = k.ps(st, "psGU", [P, 2, 2 * FH])
        psX = k.ps(st, "psX", [P, D])
        psH = k.ps(st, "psHT", [P, FQ * P])
        psD = k.ps(st, "psD", [P, D])
        (raw_ok, draw_ok, xt_ps, xhi, xlo, gu_mm, sg_ok, hid_ok, ht_ps, hthi, htlo, d_mm, oev_a,
         oev_v, fill, ends) = [k.sem("e_" + n) for n in (
            "raw_ok", "draw_ok", "xt_ps", "xhi", "xlo", "gu_mm", "sg_ok", "hid_ok", "ht_ps",
            "hthi", "htlo", "d_mm", "oev_a", "oev_v", "fill", "ends")]
        o_out = [k.sem(f"o_out{i}") for i in range(2)]
        PART1, PART2 = range(3), range(3, 4)
        CODES = 1 + NCOL

        def last_tile(eng):
            return eng.value_load(R.tab[0:1, 0:1], min_val=NE, max_val=MAXT)

        def expert_of(eng, t):
            return eng.value_load(R.tab[0:1, bass.ds(t + 1, 1)], min_val=0, max_val=NE - 1)

        def code_of(eng, t):
            return eng.value_load(R.tab[0:1, bass.ds(t + CODES, 1)], min_val=0, max_val=4 * NE - 1)

        with nc.Block() as block:

            @block.sync
            def _(sp):
                for e in range(NE):
                    sp.wait_ge(raw_in[e % 2], 32 * (e // 2 + 1))
                    sp.sem_inc(raw_ok, 1)
                    sp.wait_ge(draw_in[e % 2], 16 * (e // 2 + 1))
                    sp.sem_inc(draw_ok, 1)
                    if e + 2 < NE:
                        W.load(sp, a, e + 2)
                n = last_tile(sp) + 1
                with sp.Fori(n, MAXT + 2, 1) as t:
                    sp.dma_start(o_d[bass.ds(sp.snap(t * P), P), :], h2_d[0:P, :]).then_inc(fill, 16)
                left = sp.value_load(R.tab[0:1, 1 + 2 * NCOL:], min_val=1, max_val=MAXT + 2)
                sp.wait_ge(fill, left * 16)
                sp.sem_inc(ends, 1)

            @block.gpsimd
            def _(pool):
                last = last_tile(pool)

                with pool.Fori(2, last + 1, 2) as t:
                    for d in range(2):
                        pool.wait_ge(xt_ps, t + d - 1)
                        W.gather(pool, R, h2_d, t + d, d)

            @block.scalar
            def _(act):
                last = last_tile(act)
                for u in range(2):
                    act.sem_inc(o_out[u], 16)

                def split_gu(e, parts):
                    u = slice(e % 2, e % 2 + 1) if isinstance(e, int) else bass.ds(act.snap(e & 1), 1)
                    act.wait_ge(raw_ok, e + 1)
                    for h in parts:
                        q = slice(h * 2, h * 2 + 2)
                        act.copy(w_hi[:, u, q, :], wraw[:, u, q, :]).then_inc(whi, 1)

                def split_d(e):
                    u = slice(e % 2, e % 2 + 1) if isinstance(e, int) else bass.ds(act.snap(e & 1), 1)
                    act.wait_ge(draw_ok, e + 1)
                    act.copy(d_hi[:, u], draw[:, u]).then_inc(dhi, 1)

                def x_hi_of(t, u):
                    act.wait_ge(xt_ps, t + 1)
                    act.copy(x_hi[:, u], psX[:].rearrange("p (k n) -> p k n", k=KD)).then_inc(xhi, 1)

                def silu(t, u):
                    act.wait_ge(gu_mm, t + 1)
                    if not isinstance(t, int):
                        act.wait_ge(hid_ok, t)
                    act.activation(sg[:], psG[:, u, 0:FH], ACT.Silu).then_inc(sg_ok, 1)

                def hidden_hi(t):
                    act.wait_ge(ht_ps, t + 1)
                    if not isinstance(t, int):
                        act.wait_ge(d_mm, t)
                    act.copy(t_hi[:], psH[:].rearrange("p (k n) -> p k n", k=FQ)).then_inc(hthi, 1)

                def out(t, u):
                    act.wait_ge(d_mm, t + 1)
                    act.wait_ge(o_out[u], 8 * t + 16 - 8 * u)
                    act.copy(osb[:, u, 0:BLK], psD[:, 0:BLK]).then_inc(oev_a, 1)

                def store(t, u):
                    act.wait_ge(oev_a, t + 1)
                    act.wait_ge(oev_v, t + 1)
                    act.dma_start(o_d[bass.ds(act.snap(t * P), P), :], osb[:, u, :]).then_inc(o_out[u], 16)

                x_hi_of(0, 0)
                split_gu(1, PART1)
                silu(0, 0)
                x_hi_of(1, 1)
                split_gu(1, PART2)
                split_d(1)
                with act.If((code_of(act, 0) & 2) > 0):
                    split_gu(2, PART1)
                with act.Fori(1, last + 1, 2) as t:
                    for d in range(2):
                        u = 1 - d
                        s = t + d
                        code = code_of(act, s)
                        hidden_hi(s - 1)
                        silu(s, u)
                        x_hi_of(s + 1, 1 - u)
                        out(s - 1, 1 - u)
                        with act.If((code & 1) > 0):
                            after = act.snap((code >> 2) + 1)
                            split_gu(after, PART2)
                            split_d(after)
                        with act.If((code & 2) > 0):
                            split_gu(act.snap((code >> 2) + 2), PART1)
                        store(s - 1, 1 - u)
                hidden_hi(last)
                out(last, 0)
                store(last, 0)
                act.wait_ge(o_out[0], last * 8 + 32)
                act.wait_ge(o_out[1], last * 8 + 16)
                act.sem_inc(ends, 1)

            @block.vector
            def _(dve):
                last = last_tile(dve)

                def split_gu(e, parts):
                    u = slice(e % 2, e % 2 + 1) if isinstance(e, int) else bass.ds(dve.snap(e & 1), 1)
                    for h in parts:
                        q = slice(h * 2, h * 2 + 2)
                        dve.wait_ge(whi, 4 * e + (h + 1))
                        dve.tensor_tensor(w_lo[:, u, q, :], wraw[:, u, q, :], w_hi[:, u, q, :].bitcast(F32),
                                          ALU.subtract).then_inc(wlo, 1)

                def split_d(e):
                    u = slice(e % 2, e % 2 + 1) if isinstance(e, int) else bass.ds(dve.snap(e & 1), 1)
                    dve.wait_ge(dhi, e + 1)
                    dve.tensor_tensor(d_lo[:, u], draw[:, u], d_hi[:, u].bitcast(F32), ALU.subtract).then_inc(dlo, 1)

                def x_lo_of(t, u):
                    dve.wait_ge(xhi, t + 1)
                    dve.tensor_tensor(x_lo[:, u], psX[:].rearrange("p (k n) -> p k n", k=KD), x_hi[:, u].bitcast(F32),
                                      ALU.subtract).then_inc(xlo, 1)

                def hidden(t, u):
                    dve.wait_ge(sg_ok, t + 1)
                    dve.scalar_tensor_tensor(out=hid[:, u, :], in0=sg[:], scalar=R.gate[:, bass.ds(t, 1)],
                                             in1=psG[:, u, FH:2 * FH], op0=ALU.mult, op1=ALU.mult
                                             ).then_inc(hid_ok, 1)

                def hidden_lo(t):
                    dve.wait_ge(hthi, t + 1)
                    dve.tensor_tensor(t_lo[:], psH[:].rearrange("p (k n) -> p k n", k=FQ), t_hi[:].bitcast(F32),
                                      ALU.subtract).then_inc(htlo, 1)

                def out(t, u):
                    dve.wait_ge(d_mm, t + 1)
                    dve.wait_ge(o_out[u], 8 * t + 16 - 8 * u)
                    dve.tensor_copy(osb[:, u, BLK:D], psD[:, BLK:D]).then_inc(oev_v, 1)

                x_lo_of(0, 0)
                split_gu(1, PART1)
                hidden(0, 0)
                x_lo_of(1, 1)
                split_gu(1, PART2)
                split_d(1)
                with dve.If((code_of(dve, 0) & 2) > 0):
                    split_gu(2, PART1)
                with dve.Fori(1, last + 1, 2) as t:
                    for d in range(2):
                        u = 1 - d
                        s = t + d
                        code = code_of(dve, s)
                        hidden_lo(s - 1)
                        hidden(s, u)
                        x_lo_of(s + 1, 1 - u)
                        out(s - 1, 1 - u)
                        with dve.If((code & 1) > 0):
                            after = dve.snap((code >> 2) + 1)
                            split_gu(after, PART2)
                            split_d(after)
                        with dve.If((code & 2) > 0):
                            split_gu(dve.snap((code >> 2) + 2), PART1)
                hidden_lo(last)
                out(last, 0)

            @block.tensor
            def _(pe):
                last = last_tile(pe)

                def turn(t, u):
                    pe.wait_ge(xg_in[u], 8 * t + 16 - 8 * u)
                    if not isinstance(t, int) or t >= 1:
                        pe.wait_ge(xlo, t)
                    for q in range(KD):
                        mm = pe.transpose(psX[:, q * P:(q + 1) * P], xg[:, u, q * P:(q + 1) * P], k.ident[:])
                    mm.then_inc(xt_ps, 1)

                def gate_up(t, u, e):
                    w = slice(e, e + 1) if isinstance(e, int) else bass.ds(pe.snap(e & 1), 1)
                    pe.wait_ge(wlo, 4 * e + 4)
                    pe.wait_ge(xlo, t + 1)
                    if not isinstance(t, int) :
                        pe.wait_ge(hid_ok, t - 1)
                    for q in range(KD):
                        if q == KD // 2 and not isinstance(t, int):
                            turn_hidden(t - 1, 1 - u)
                        mm = matmul3(pe, psG[:, u, :], x_hi[:, u, q, :], x_lo[:, u, q, :],
                                     w_hi[:, w, q, :].rearrange("p a n -> p (a n)"),
                                     w_lo[:, w, q, :].rearrange("p a n -> p (a n)"), q == 0, q == KD - 1)
                    mm.then_inc(gu_mm, 1)

                def turn_hidden(t, u):
                    pe.wait_ge(hid_ok, t + 1)
                    if not isinstance(t, int):
                        pe.wait_ge(htlo, t)
                    for q in range(FQ):
                        mm = pe.transpose(psH[:, q * P:(q + 1) * P], hid[:, u, q * P:(q + 1) * P], k.ident[:])
                    mm.then_inc(ht_ps, 1)

                def down(t, e):
                    w = slice(e, e + 1) if isinstance(e, int) else bass.ds(pe.snap(e & 1), 1)
                    pe.wait_ge(dlo, e + 1)
                    pe.wait_ge(htlo, t + 1)
                    if not isinstance(t, int):
                        pe.wait_ge(oev_a, t)
                        pe.wait_ge(oev_v, t)
                    for c in range(2):
                        for q in range(FQ):
                            cs = slice(c * BLK, (c + 1) * BLK)
                            mm = matmul3(pe, psD[:, cs], t_hi[:, q, :], t_lo[:, q, :],
                                         d_hi[:, w, q, cs].rearrange("p a n -> p (a n)"),
                                         d_lo[:, w, q, cs].rearrange("p a n -> p (a n)"), q == 0, q == FQ - 1)
                    mm.then_inc(d_mm, 1)

                turn(0, 0)
                gate_up(0, 0, 0)
                turn(1, 1)
                with pe.Fori(1, last + 1, 2) as t:
                    before, now, after = [expert_of(pe, t + i) for i in (-1, 0, 1)]
                    for d in range(2):
                        u = 1 - d
                        s = t + d
                        gate_up(s, u, now)
                        turn(s + 1, 1 - u)
                        down(s - 1, before)
                        before, now = now, after
                turn_hidden(last, 0)
                down(last, expert_of(pe, last))


def combine(k, a, o, x2_d, o_d, mod_d, pos):
    nc = k.nc
    k.stage = "combine"
    LAST = NT - 1
    NB = 4
    with ExitStack() as st:
        x2 = k.sb(st, "x2", [P, NB, D])
        r1 = k.sb(st, "r1", [P, NB, D])
        r2 = k.sb(st, "r2", [P, NB, D])
        y = k.sb(st, "y", [P, NB, D])
        g2 = k.sb(st, "g2", [P, 2, D])
        gn = k.sb(st, "gn", [P, D])
        junk = k.sb(st, "junk6", [P, D])
        ss = k.sb(st, "ss6", [P, NT, 4])
        rows_in, sum1, gated, x3, sq, ms, rt, y_done, rstd = [k.sem("c_" + n) for n in (
            "rows_in", "sum1", "gated", "x3", "sq", "ms", "rt", "y_done", "rstd")]
        x_in = [k.sem(f"cx_in{i}") for i in range(NB)]
        r_in = [k.sem(f"cr_in{i}") for i in range(NB)]
        y_out = [k.sem(f"fin_out{i}") for i in range(NB)]

        with nc.Block() as block:

            @block.sync
            def _(sp):
                sp.dma_start(g2[:, 0, :], mod_d[0:1, 5 * D:6 * D].broadcast_to([P, D])).then_inc(rows_in, 16)
                sp.dma_start(g2[0:TS, 1, :], mod_d[1:ROWS, 5 * D:6 * D].unsqueeze(1).broadcast_to([NSEQ, LSEQ, D])
                             ).then_inc(rows_in, 16)
                sp.dma_start(gn[:], a["final_norm_g"].unsqueeze(0).broadcast_to([P, D])).then_inc(rows_in, 16)
                y_s = o["y_sample"].rearrange("b t d -> (b t) d")
                for t in range(NT + NB):
                    if t < NT:
                        u, rows = t % NB, P if t < LAST else TS
                        if t >= NB:
                            sp.wait_ge(x3, t - NB + 1)
                        sp.dma_start(x2[0:rows, u, :], x2_d[t * P:t * P + rows, :]).then_inc(x_in[u], 16)
                    s = t - NB
                    if s >= 0:
                        sp.wait_ge(y_done, s + 1)
                        u, rows = s % NB, P if s < LAST else TS
                        dst = o["y_prompt"][0, s * P:(s + 1) * P, :] if s < LAST else y_s
                        sp.dma_start(dst, y[0:rows, u, :]).then_inc(y_out[u], 16)
                for u in range(NB):
                    sp.wait_ge(y_out[u], 16 * ((NT - 1 - u) // NB + 1))

            @block.gpsimd
            def _(pool):
                for t in range(NT):
                    u, rows = t % NB, P if t < LAST else TS
                    if t >= NB:
                        pool.wait_ge(sum1, t - NB + 1)
                    for i, r in enumerate((r1, r2)):
                        pool.indirect_dma_start(r[0:rows, u, :], None, o_d,
                                                bass.IndirectOffsetOnAxis(pos[0:rows, t, i:i + 1], 0)
                                                ).then_inc(r_in[u], 16)

            @block.scalar
            def _(act):
                for t in range(NT):
                    u, rows = t % NB, P if t < LAST else TS
                    act.wait_ge(x3, t + 1)
                    act.activation(junk[0:rows, :], y[0:rows, u, :], ACT.Square, accum_out=ss[0:rows, t, 0:1]
                                   ).then_inc(sq, 1)
                    act.wait_ge(ms, t + 1)
                    act.activation(ss[0:rows, t, 2:3], ss[0:rows, t, 1:2], ACT.Sqrt).then_inc(rt, 1)

            @block.vector
            def _(dve):
                dve.wait_ge(rows_in, 48)
                tt = dve.tensor_tensor

                def add(t):
                    u, kind, r = t % NB, int(t == LAST), slice(0, P if t < LAST else TS)
                    n = t // NB + 1
                    dve.wait_ge(r_in[u], 32 * n)
                    if t >= NB:
                        dve.wait_ge(y_out[u], 16 * (n - 1))
                    tt(y[r, u, :], r1[r, u, :], r2[r, u, :], ALU.add).then_inc(sum1, 1)
                    dve.wait_ge(sum1, t + 1)
                    tt(y[r, u, :], y[r, u, :], g2[r, kind, :], ALU.mult).then_inc(gated, 1)
                    dve.wait_ge(gated, t + 1)
                    dve.wait_ge(x_in[u], 16 * n)
                    tt(y[r, u, :], y[r, u, :], x2[r, u, :], ALU.add).then_inc(x3, 1)

                def scale(t):
                    u, r = t % NB, slice(0, P if t < LAST else TS)
                    dve.wait_ge(sq, t + 1)
                    dve.tensor_scalar(ss[r, t, 1:2], ss[r, t, 0:1], 1.0 / D, EPS, ALU.mult, ALU.add).then_inc(ms, 1)
                    dve.wait_ge(rt, t + 1)
                    dve.reciprocal(ss[r, t, 3:4], ss[r, t, 2:3]).then_inc(rstd, 1)
                    dve.wait_ge(rstd, t + 1)
                    dve.scalar_tensor_tensor(out=y[r, u, :], in0=y[r, u, :], scalar=ss[r, t, 3:4], in1=gn[r, :],
                                             op0=ALU.mult, op1=ALU.mult).then_inc(y_done, 1)

                for t in range(NT + 1):
                    if t < NT:
                        add(t)
                    if t:
                        scale(t - 1)


class Routed:

    def __init__(self, k, st):
        self.pos = k.sb(st, "pos", [P, NT, 2], I32)
        self.tab = k.sb(st, "tab", [1, 2 + 2 * NCOL], I32)
        self.idx = k.sb(st, "idx", [P, NCOL], I32)
        self.gate = k.sb(st, "gate", [P, NCOL])


def hybrid_step(nc, a, o):
    with ExitStack() as s0:
        k = Core(nc, s0)
        k.ident = k.sb(s0, "ident", [P, P])
        k.cT = k.sb(s0, "cT", [P, KD, ROWS])
        u_pool = k.dram("u_pool", [HALF, TOK])
        u_ssm = k.dram("u_ssm", [HALF, STEP, NCH])
        mod_d = k.dram("mod_d", [ROWS, 6 * D])
        mix_d = k.dram("mix_d", [D, TOK])
        g_d = k.dram("g_d", [HALF, STEP, NCH])
        x2_d = k.dram("x2_d", [TOK, D])
        h2_d = k.dram("h2_d", [TOK, D])
        o_d = k.dram("o_d", [(MAXT + 2) * P, D])
        s1 = {n: k.sem(n) for n in ("x_in", "ct_sb", "hs", "store_go", "sq_done", "ms_done", "rt_done", "rstd_done",
                                     "xn_done", "t_done")}
        with ExitStack() as st:
            w_hi = k.sb(st, "w_hi", [P, KD, D], F32R)
            w_lo = k.sb(st, "w_lo", [P, KD, D], F32R)
            xraw = k.sb(st, "xraw", [P, TPB, D])
            xn = k.sb(st, "xn", [P, TPB, D])
            ss = k.sb(st, "ss", [P, 4 * TPB])
            A1 = k.sb(st, "A1", [P, KD, ROWS])
            B1 = k.sb(st, "B1", [P, KD, ROWS])
            adaln_first(k, a, s1, w_hi, w_lo, xraw, xn, ss, A1, B1)
            in_projection(k, a, s1, w_hi, w_lo, xraw, xn, ss, A1, B1, u_pool, u_ssm)
        mixers(k, a, o, mod_d, u_pool, u_ssm, mix_d, g_d)
        k.clear_semaphores()
        k.stage = "all"
        R = Routed(k, s0)
        lg = k.sb(s0, "lg", [P, NT, 4 + NE])
        with ExitStack() as st:
            wo_hi = k.sb(st, "wo_hi", [P, KD, D], F32R)
            wo_lo = k.sb(st, "wo_lo", [P, KD, D], F32R)
            glu(k, a, g_d, mix_d, wo_hi, wo_lo)
            out_projection(k, a, mod_d, mix_d, x2_d, h2_d, wo_hi, wo_lo, lg)
        with ExitStack() as st:
            k.stage = "weights"
            W = ExpertWeights(k, st)
            routing(k, a, h2_d, lg, R, W)
            experts(k, a, h2_d, o_d, R, W)
        combine(k, a, o, x2_d, o_d, mod_d, R.pos)


_OUTS = [("y_prompt", (1, TP, D)), ("y_sample", (NSEQ, LSEQ, D)), ("pool_p", (1, 1, BUF, HALF)),
         ("pool_s", (1, NSEQ, BUF, HALF)), ("re_p", (1, 1, G, NS)), ("im_p", (1, 1, G, NS)),
         ("re_s", (1, NSEQ, G, NS)), ("im_s", (1, NSEQ, G, NS))]


def kernel(**inputs):
    import numpy as _np
    import concourse.bacc as _bacc
    from concourse.bass_utils import run_bass_kernel_spmd as _run

    nc = _bacc.Bacc("TRN2", target_bir_lowering=False, num_devices=1)
    arrays = {"in_" + n: _np.ascontiguousarray(x) for n, x in inputs.items()}
    a = {n[3:]: nc.dram_tensor(n, x.shape, F32, kind="ExternalInput").ap() for n, x in arrays.items()}
    o = {n: nc.dram_tensor("out_" + n, shape, F32, kind="ExternalOutput").ap() for n, shape in _OUTS}
    hybrid_step(nc, a, o)
    r = _run(nc, [arrays], core_ids=[0])
    return tuple(r.results[0]["out_" + n] for n, _ in _OUTS)
```
